# Optimizing a Trainium2 kernel written in Bass

```python
import math
import jax
import jax.numpy as jnp
from jax import lax
import numpy as np

D_MODEL = 1024
BATCH = 1
SEQ = 256
DEPTH = 2
DEC_BATCH = 8
DEC_SEQ = 4
PAST_LEN = 2048
PAGE_SIZE = 128

N_MIXERS = 2
N_MLSTM_LAYERS = (DEPTH + 1) // 2
N_CMLP_LAYERS = DEPTH // 2

MLSTM_PROJ = 2
MLSTM_INNER = MLSTM_PROJ * D_MODEL
MLSTM_HEADS = 4
MLSTM_HEAD_DIM = MLSTM_INNER // MLSTM_HEADS
QKV_BLOCK = 4
N_QKV_BLOCKS = MLSTM_INNER // QKV_BLOCK
CONV_WIDTH = 4
MLSTM_CHUNK = 64
STAB_INIT = -1e30

CMLP_CHUNK = 128
CMLP_HIDDEN = 4 * D_MODEL
CMLP_HALF = CMLP_HIDDEN // 2
CMLP_GROUPS = 8
CMLP_GROUP_DIM = CMLP_HALF // CMLP_GROUPS

MOE_GROUPS = 4
MOE_EXPERTS_PER_GROUP = 8
MOE_TOP_GROUPS = 1
MOE_TOP_K = 2
MOE_HIDDEN = 512

kernel_name = 'mlstm_gmlp_hier_moe_decoder_step'

def rms_norm(x, g, eps=1e-6):
    xf = x.astype(jnp.float32)
    y = xf * lax.rsqrt(jnp.mean(xf * xf, axis=-1, keepdims=True) + eps)
    return (y * g.astype(jnp.float32)).astype(x.dtype)

def layer_norm(x, w, b, eps=1e-5):
    xf = x.astype(jnp.float32)
    mu = jnp.mean(xf, axis=-1, keepdims=True)
    var = jnp.mean(jnp.square(xf - mu), axis=-1, keepdims=True)
    y = (xf - mu) * lax.rsqrt(var + eps) * w.astype(jnp.float32) + b.astype(jnp.float32)
    return y.astype(x.dtype)

def head_layer_norm(h, w, eps=1e-5):
    mu = jnp.mean(h, axis=-1, keepdims=True)
    var = jnp.mean(jnp.square(h - mu), axis=-1, keepdims=True)
    return (h - mu) * lax.rsqrt(var + eps) * w.astype(jnp.float32)

def causal_depthwise_conv(x_ext, w, b, out_len):
    y = x_ext[:, 0:out_len] * w[0]
    for j in range(1, CONV_WIDTH):
        y = y + x_ext[:, j:j + out_len] * w[j]
    return y + b

def headwise_proj(t, w):
    bsz, s, _ = t.shape
    y = jnp.einsum('bsnc,ncd->bsnd', t.reshape(bsz, s, N_QKV_BLOCKS, QKV_BLOCK), w)
    return y.reshape(bsz, s, MLSTM_INNER)

def mlstm_chunk_step(carry, inp):
    c_prev, n_prev, m_prev = carry
    q, k, v, ig, lf = inp
    length = q.shape[2]
    bcum = jnp.cumsum(lf, axis=-1)
    causal = jnp.tril(jnp.ones((length, length), dtype=bool))
    log_d = jnp.where(causal, bcum[..., :, None] - bcum[..., None, :] + ig[..., None, :], -jnp.inf)
    m_inter = bcum + m_prev[..., None]
    m_t = jnp.maximum(m_inter, jnp.max(log_d, axis=-1))
    s = jnp.einsum('bhld,bhsd->bhls', q, k) * jnp.exp(log_d - m_t[..., None])
    inter = jnp.exp(m_inter - m_t)
    num = jnp.einsum('bhls,bhsv->bhlv', s, v) + inter[..., None] * jnp.einsum('bhld,bhdv->bhlv', q, c_prev)
    den = jnp.sum(s, axis=-1) + inter * jnp.einsum('bhld,bhd->bhl', q, n_prev)
    h = num / jnp.maximum(jnp.abs(den), jnp.exp(-m_t))[..., None]
    m_new = m_t[..., -1]
    w = jnp.exp(bcum[..., -1:] - bcum + ig - m_new[..., None])
    decay = jnp.exp(bcum[..., -1] + m_prev - m_new)
    wk = w[..., None] * k
    c_new = decay[..., None, None] * c_prev + jnp.einsum('bhld,bhlv->bhdv', wk, v)
    n_new = decay[..., None] * n_prev + jnp.sum(wk, axis=2)
    return (c_new, n_new, m_new), h

def mlstm_cell(q, k, v, ig, lf, c0, n0, m0):
    bsz, s = q.shape[0], q.shape[1]
    length = math.gcd(s, MLSTM_CHUNK)
    nc = s // length

    def to_chunks(t):
        t = t.reshape((bsz, nc, length) + t.shape[2:])
        return jnp.swapaxes(jnp.moveaxis(t, 1, 0), 2, 3)

    carry0 = (c0.astype(jnp.float32), n0.astype(jnp.float32), m0.astype(jnp.float32))
    xs = (to_chunks(q), to_chunks(k), to_chunks(v), to_chunks(ig), to_chunks(lf))
    (c1, n1, m1), hs = lax.scan(mlstm_chunk_step, carry0, xs)
    h = jnp.transpose(hs, (1, 0, 3, 2, 4)).reshape(bsz, s, MLSTM_HEADS, MLSTM_HEAD_DIM)
    return h, c1, n1, m1

def mlstm_mixer(x, conv_buf, c0, n0, m0, p, j):
    bsz, s, _ = x.shape
    xm, z = jnp.split(x @ p['mlstm_w_up'][j], 2, axis=-1)
    x_ext = jnp.concatenate([conv_buf.astype(xm.dtype), xm], axis=1)
    xc = jax.nn.silu(causal_depthwise_conv(x_ext, p['mlstm_conv_w'][j], p['mlstm_conv_b'][j], s))
    q = headwise_proj(xc, p['mlstm_w_q'][j])
    k = headwise_proj(xc, p['mlstm_w_k'][j])
    v = headwise_proj(xm, p['mlstm_w_v'][j])
    qkv = jnp.concatenate([q, k, v], axis=-1)
    ig = (qkv @ p['mlstm_w_ig'][j] + p['mlstm_b_ig'][j]).astype(jnp.float32)
    lf = jax.nn.log_sigmoid((qkv @ p['mlstm_w_fg'][j] + p['mlstm_b_fg'][j]).astype(jnp.float32))

    def heads(t):
        return t.astype(jnp.float32).reshape(bsz, s, MLSTM_HEADS, MLSTM_HEAD_DIM)

    h, c1, n1, m1 = mlstm_cell(heads(q), heads(k) * (MLSTM_HEAD_DIM ** -0.5), heads(v), ig, lf, c0, n0, m0)
    h = head_layer_norm(h, p['mlstm_hn_w'][j]).reshape(bsz, s, MLSTM_INNER).astype(x.dtype)
    h = (h + p['mlstm_skip'][j] * xc) * jax.nn.silu(z)
    new_conv = x_ext[:, x_ext.shape[1] - (CONV_WIDTH - 1):]
    return h @ p['mlstm_w_down'][j], new_conv, c1, n1, m1

def chunk_mlp_mixer(x, p, j):
    bsz, s, _ = x.shape
    zz = jax.nn.gelu(x @ p['cmlp_w_in'][j] + p['cmlp_b_in'][j])
    u, v = jnp.split(zz, 2, axis=-1)
    v = layer_norm(v, p['cmlp_ln_w'][j], p['cmlp_ln_b'][j])
    pad = (-s) % CMLP_CHUNK
    nc = (s + pad) // CMLP_CHUNK
    vp = jnp.pad(v, ((0, 0), (0, pad), (0, 0))).reshape(bsz, nc, CMLP_CHUNK, CMLP_GROUPS, CMLP_GROUP_DIM)
    causal = jnp.tril(jnp.ones((CMLP_CHUNK, CMLP_CHUNK), dtype=bool))
    ws = jnp.where(causal, p['cmlp_w_s'][j], jnp.zeros_like(p['cmlp_w_s'][j]))
    bias = jnp.swapaxes(p['cmlp_b_s'][j], 0, 1)[None, None, :, :, None]
    mixed = jnp.einsum('gts,bcsgd->bctgd', ws, vp) + bias
    mixed = mixed.reshape(bsz, nc * CMLP_CHUNK, CMLP_HALF)[:, :s]
    return (u * mixed) @ p['cmlp_w_out'][j] + p['cmlp_b_out'][j], v

def hier_moe(x, p, i):
    g_prob = jax.nn.softmax((x @ p['moe_w_rg'][i] + p['moe_b_rg'][i]).astype(jnp.float32), axis=-1)
    g_w, g_idx = lax.top_k(g_prob, MOE_TOP_GROUPS)
    g_onehot = jax.nn.one_hot(g_idx[:, 0], MOE_GROUPS, dtype=jnp.float32)
    e_logits = (jnp.einsum('td,gde->tge', x, p['moe_w_re'][i]) + p['moe_b_re'][i]).astype(jnp.float32)
    e_sel = jnp.einsum('tg,tge->te', g_onehot, e_logits)
    e_top, e_idx = lax.top_k(e_sel, MOE_TOP_K)
    e_w = jax.nn.softmax(e_top, axis=-1) * g_w
    within = jnp.sum(jax.nn.one_hot(e_idx, MOE_EXPERTS_PER_GROUP, dtype=jnp.float32) * e_w[..., None], axis=1)
    combine = (g_onehot[:, :, None] * within[:, None, :]).astype(x.dtype)
    y = jnp.zeros_like(x)
    for g in range(MOE_GROUPS):
        a = jnp.einsum('td,edf->tef', x, p['moe_w_gate'][i, g])
        b = jnp.einsum('td,edf->tef', x, p['moe_w_up'][i, g])
        hg = jax.nn.silu(a) * b * combine[:, g, :, None]
        y = y + jnp.einsum('tef,efd->td', hg, p['moe_w_down'][i, g])
    return y

def run_trunk(x, conv_buf, c0, n0, m0, p):
    new_c, new_n, new_m, new_conv, new_v = [], [], [], [], []
    ja = 0
    jb = 0
    for i in range(DEPTH):
        h = rms_norm(x, p['norm_mix'][i])
        if i % N_MIXERS == 0:
            out, cb, c1, n1, m1 = mlstm_mixer(h, conv_buf[ja], c0[ja], n0[ja], m0[ja], p, ja)
            new_c.append(c1)
            new_n.append(n1)
            new_m.append(m1)
            new_conv.append(cb)
            ja += 1
        else:
            out, v = chunk_mlp_mixer(h, p, jb)
            new_v.append(v)
            jb += 1
        x = x + out
        h = rms_norm(x, p['norm_ffn'][i])
        x = x + hier_moe(h.reshape(-1, D_MODEL), p, i).reshape(x.shape)
    y = rms_norm(x, p['norm_final'])
    return y, jnp.stack(new_c), jnp.stack(new_n), jnp.stack(new_m), jnp.stack(new_conv), jnp.stack(new_v)

def setup_inputs(seed: int = 0) -> dict:
    key = jax.random.key(seed)
    ks = iter(jax.random.split(key, 48))

    def nrm(shape, scale):
        return scale * jax.random.normal(next(ks), shape, jnp.float32)

    NA, NC = N_MLSTM_LAYERS, N_CMLP_LAYERS
    H, DH, E = MLSTM_HEADS, MLSTM_HEAD_DIM, MLSTM_INNER
    NG, EPG, F = MOE_GROUPS, MOE_EXPERTS_PER_GROUP, MOE_HIDDEN
    inp = {}
    inp['x_prompt'] = nrm((BATCH, SEQ, D_MODEL), 1.0)
    inp['x_sample'] = nrm((DEC_BATCH, DEC_SEQ, D_MODEL), 1.0)
    inp['state_mlstm_C'] = nrm((NA, DEC_BATCH, H, DH, DH), 0.1)
    inp['state_mlstm_n'] = nrm((NA, DEC_BATCH, H, DH), 0.1)
    inp['state_mlstm_m'] = nrm((NA, DEC_BATCH, H), 0.5)
    inp['state_mlstm_conv'] = nrm((NA, DEC_BATCH, CONV_WIDTH - 1, E), 1.0)
    inp['norm_mix'] = 1.0 + nrm((DEPTH, D_MODEL), 0.01)
    inp['norm_ffn'] = 1.0 + nrm((DEPTH, D_MODEL), 0.01)
    inp['norm_final'] = 1.0 + nrm((D_MODEL,), 0.01)
    inp['mlstm_w_up'] = nrm((NA, D_MODEL, 2 * E), D_MODEL ** -0.5)
    inp['mlstm_conv_w'] = nrm((NA, CONV_WIDTH, E), CONV_WIDTH ** -0.5)
    inp['mlstm_conv_b'] = nrm((NA, E), 0.01)
    inp['mlstm_w_q'] = nrm((NA, N_QKV_BLOCKS, QKV_BLOCK, QKV_BLOCK), QKV_BLOCK ** -0.5)
    inp['mlstm_w_k'] = nrm((NA, N_QKV_BLOCKS, QKV_BLOCK, QKV_BLOCK), QKV_BLOCK ** -0.5)
    inp['mlstm_w_v'] = nrm((NA, N_QKV_BLOCKS, QKV_BLOCK, QKV_BLOCK), QKV_BLOCK ** -0.5)
    inp['mlstm_w_ig'] = nrm((NA, 3 * E, H), (3 * E) ** -0.5)
    inp['mlstm_b_ig'] = nrm((NA, H), 0.1)
    inp['mlstm_w_fg'] = nrm((NA, 3 * E, H), (3 * E) ** -0.5)
    inp['mlstm_b_fg'] = jnp.linspace(3.0, 6.0, H, dtype=jnp.float32)[None, :] + nrm((NA, H), 0.01)
    inp['mlstm_skip'] = 1.0 + nrm((NA, E), 0.01)
    inp['mlstm_hn_w'] = 1.0 + nrm((NA, H, DH), 0.01)
    inp['mlstm_w_down'] = nrm((NA, E, D_MODEL), E ** -0.5)
    inp['cmlp_w_in'] = nrm((NC, D_MODEL, CMLP_HIDDEN), D_MODEL ** -0.5)
    inp['cmlp_b_in'] = nrm((NC, CMLP_HIDDEN), 0.01)
    inp['cmlp_ln_w'] = 1.0 + nrm((NC, CMLP_HALF), 0.01)
    inp['cmlp_ln_b'] = nrm((NC, CMLP_HALF), 0.01)
    inp['cmlp_w_s'] = nrm((NC, CMLP_GROUPS, CMLP_CHUNK, CMLP_CHUNK), CMLP_CHUNK ** -0.5)
    inp['cmlp_b_s'] = 1.0 + nrm((NC, CMLP_GROUPS, CMLP_CHUNK), 0.1)
    inp['cmlp_w_out'] = nrm((NC, CMLP_HALF, D_MODEL), CMLP_HALF ** -0.5)
    inp['cmlp_b_out'] = nrm((NC, D_MODEL), 0.01)
    inp['moe_w_rg'] = nrm((DEPTH, D_MODEL, NG), D_MODEL ** -0.5)
    inp['moe_b_rg'] = nrm((DEPTH, NG), 0.01)
    inp['moe_w_re'] = nrm((DEPTH, NG, D_MODEL, EPG), D_MODEL ** -0.5)
    inp['moe_b_re'] = nrm((DEPTH, NG, EPG), 0.01)
    inp['moe_w_gate'] = nrm((DEPTH, NG, EPG, D_MODEL, F), D_MODEL ** -0.5)
    inp['moe_w_up'] = nrm((DEPTH, NG, EPG, D_MODEL, F), D_MODEL ** -0.5)
    inp['moe_w_down'] = nrm((DEPTH, NG, EPG, F, D_MODEL), F ** -0.5)
    return inp

def reference(x_prompt, x_sample, state_mlstm_C, state_mlstm_n, state_mlstm_m, state_mlstm_conv,
              norm_mix, norm_ffn, norm_final,
              mlstm_w_up, mlstm_conv_w, mlstm_conv_b, mlstm_w_q, mlstm_w_k, mlstm_w_v,
              mlstm_w_ig, mlstm_b_ig, mlstm_w_fg, mlstm_b_fg, mlstm_skip, mlstm_hn_w, mlstm_w_down,
              cmlp_w_in, cmlp_b_in, cmlp_ln_w, cmlp_ln_b, cmlp_w_s, cmlp_b_s, cmlp_w_out, cmlp_b_out,
              moe_w_rg, moe_b_rg, moe_w_re, moe_b_re, moe_w_gate, moe_w_up, moe_w_down):
    p = {
        'norm_mix': norm_mix, 'norm_ffn': norm_ffn, 'norm_final': norm_final,
        'mlstm_w_up': mlstm_w_up, 'mlstm_conv_w': mlstm_conv_w, 'mlstm_conv_b': mlstm_conv_b,
        'mlstm_w_q': mlstm_w_q, 'mlstm_w_k': mlstm_w_k, 'mlstm_w_v': mlstm_w_v,
        'mlstm_w_ig': mlstm_w_ig, 'mlstm_b_ig': mlstm_b_ig, 'mlstm_w_fg': mlstm_w_fg, 'mlstm_b_fg': mlstm_b_fg,
        'mlstm_skip': mlstm_skip, 'mlstm_hn_w': mlstm_hn_w, 'mlstm_w_down': mlstm_w_down,
        'cmlp_w_in': cmlp_w_in, 'cmlp_b_in': cmlp_b_in, 'cmlp_ln_w': cmlp_ln_w, 'cmlp_ln_b': cmlp_ln_b,
        'cmlp_w_s': cmlp_w_s, 'cmlp_b_s': cmlp_b_s, 'cmlp_w_out': cmlp_w_out, 'cmlp_b_out': cmlp_b_out,
        'moe_w_rg': moe_w_rg, 'moe_b_rg': moe_b_rg, 'moe_w_re': moe_w_re, 'moe_b_re': moe_b_re,
        'moe_w_gate': moe_w_gate, 'moe_w_up': moe_w_up, 'moe_w_down': moe_w_down,
    }
    bp = x_prompt.shape[0]
    conv0 = jnp.zeros((N_MLSTM_LAYERS, bp, CONV_WIDTH - 1, MLSTM_INNER), x_prompt.dtype)
    c0 = jnp.zeros((N_MLSTM_LAYERS, bp, MLSTM_HEADS, MLSTM_HEAD_DIM, MLSTM_HEAD_DIM), jnp.float32)
    n0 = jnp.zeros((N_MLSTM_LAYERS, bp, MLSTM_HEADS, MLSTM_HEAD_DIM), jnp.float32)
    m0 = jnp.full((N_MLSTM_LAYERS, bp, MLSTM_HEADS), STAB_INIT, jnp.float32)
    y_prompt, c_p, n_p, m_p, conv_p, _v_p = run_trunk(x_prompt, conv0, c0, n0, m0, p)
    y_sample, c_s, n_s, m_s, conv_s, v_s = run_trunk(x_sample, state_mlstm_conv, state_mlstm_C,
                                                     state_mlstm_n, state_mlstm_m, p)
    return (y_prompt, y_sample, c_p, n_p, m_p, conv_p, c_s, n_s, m_s, conv_s, v_s)


_drawn_inputs = setup_inputs


def setup_inputs(seed=0):
    import zlib

    import numpy as np

    out = dict(_drawn_inputs(seed))
    spreads = {}
    factors = {'norm_final': 200.0,
     'mlstm_skip': 13.224,
     'cmlp_b_in': 4.905,
     'cmlp_ln_w': 92.288,
     'cmlp_ln_b': 103.658,
     'cmlp_b_out': 37.951,
     'norm_ffn': 3.085,
     'mlstm_conv_b': 2.74,
     'mlstm_hn_w': 6.447,
     'moe_b_rg': 6.121,
     'moe_b_re': 3.138,
     'cmlp_b_s': 3.954}
    for name, (base, spread) in spreads.items():
        noise = np.random.default_rng([zlib.crc32(name.encode()), seed]).standard_normal(out[name].shape)
        drawn = base * np.exp(spread * noise) if base else spread * noise
        out[name] = jnp.asarray(drawn.astype(out[name].dtype))
    for name, factor in factors.items():
        out[name] = (out[name] * factor).astype(out[name].dtype)
    return out
```

```python
from contextlib import ExitStack

import concourse.bass as bass
from concourse import mybir

F32 = mybir.dt.float32
BF16 = mybir.dt.bfloat16
I32 = mybir.dt.int32
ALU = mybir.AluOpType
ACT = mybir.ActivationFunctionType
AX = mybir.AxisListType

P = 128
D = 1024
KD = D // P
NPROMPT = 256
NB = 8
SB = 4
NS = NB * SB
NT = NPROMPT + NS
TOK = [(0, 128), (128, 128), (256, NS)]
INNER = 2048
KI = INNER // P
H = 4
DH = INNER // H
MH = DH // P
XE = 3 + NPROMPT + NB * 7
XS = 3 + NPROMPT
KSCALE = DH ** -0.5
G = 4
EPG = 8
NE = G * EPG
F = 512
MF = F // P
CAP = 64
ROUNDS = -(-NT // CAP)
NSLOT = 2 * NT
SLOTS = NSLOT + CAP
QT = [(q, min(P, NSLOT - q)) for q in range(0, NSLOT, P)]
CG = 8
PAGE = 4096
RING = 6
NEG = -1.0e30
UPD = (5, 6, 7, 0)
EARLIER = 1024.0


def build(nc, A, O):
    with ExitStack() as ctx:
        def sb(name, shape, dt=F32):
            return ctx.enter_context(nc.sbuf_tensor(name, shape, dt))

        sems = {}

        def s(name):
            if name not in sems:
                sems[name] = ctx.enter_context(nc.semaphore("s_" + name))
            return sems[name]

        def at(t, off, *dims):
            n = 1
            for d in dims:
                n *= d
            v = t[:, off:off + n]
            if len(dims) == 1:
                return v
            if len(dims) == 2:
                return v.rearrange("p (a b) -> p a b", b=dims[1])
            return v.rearrange("p (a b c) -> p a b c", b=dims[1], c=dims[2])

        B = [ctx.enter_context(nc.psum_tensor(f"bank{i}", [P, 512], F32)) for i in range(8)]
        xT = sb("xT", [P, KD, NT])
        hT = sb("hT", [P, KD, NT])
        ident = sb("ident", [P, P])
        ones = sb("ones", [P, P])
        before = sb("before", [P, P])
        bmask = sb("bmask", [P, 32])
        vecs = sb("vecs", [P, 192])
        wif = sb("wif", [P, 48, 8])
        wr = sb("wr", [P, 2, KD, 36])
        rbias = sb("rbias", [P, 2, 36])
        scratch = sb("scratch", [P, 2 * NT])
        stdv, rstd = scratch[:, 0:NT], scratch[:, NT:2 * NT]
        xms = at(scratch, 0, KI, NS)
        nT = sb("nT", [P, MH, 32])
        rows = sb("rows", [P, NT])
        catA = sb("catA", [4, NT + 8 + NS])
        tm = sb("tm", [P, 3, 12])
        decb = sb("decb", [P, H, NB])
        ibc = sb("ibc", [P, H, NS])
        decn = sb("decn", [NB, H])
        m0 = sb("m0", [4, NB])
        gb = sb("gb", [4, 2])
        nrow = sb("nrow", [NB, 2, DH])
        nst = sb("nst", [1, DH])
        small = sb("small", [P, 64])
        eps6, eps5 = small[:, 0:1], small[:, 1:2]
        rden = small[:, 2:5]
        dden = small[:, 5:8]
        slotw = small[:, 8:20]
        mvsd = small[:, 20:32]
        lnst = small[:, 32:38]
        table = sb("table", [1, ROUNDS * NE + 8], I32)
        arena = sb("arena", [P, 18864])
        ring = sb("ring", [P, RING, PAGE])

        xe = at(arena, 0, KI, XE)
        xc = at(arena, 5040, KI, NT)
        qT = at(arena, 9648, KI, NT)
        kT = at(arena, 14256, KI, NT)
        hhp = [at(arena, 14256 + h * MH * NT, 2, DH) for h in range(H)]
        hhs = [at(arena, 9648 + h * MH * NT, DH) for h in range(H)]
        zs = at(arena, 0, KI, NT)
        xtok = at(arena, 9648, 3, D)
        raw_re = at(arena, 12720, 1024)
        raw_rg = at(arena, 13744, 512)
        raw_if = at(arena, 14256, 2, 512)
        raw_qkv = at(arena, 15280, 512)
        raw_vec = at(arena, 15792, 2, P)
        raw_conv = at(arena, 16048, INNER)
        high = ring[:, 3:6, :].rearrange("p a b -> p (a b)")
        bd = at(high, 0, 3, KI, P)
        z1 = at(high, 0, 2, DH)
        snum = at(high, 1024, DH)
        wk8 = at(high, 2048, 512).bitcast(BF16).rearrange("p (a d) -> p a d", a=2)
        v8 = at(high, 2560, 512).bitcast(BF16).rearrange("p (a d) -> p a d", a=2)
        y16 = at(high, 3072, 512).bitcast(BF16).rearrange("p (a d) -> p a d", a=2)
        spread = at(high, 3584, 2, P)
        fold = at(high, 3840, NS)
        prod = at(high, 3872, 8)
        notp = at(high, 3880, 4)
        cvout = at(high, 0, INNER)
        vtok = at(high, 6144, 3, DH)
        wk = at(high, 7680, 3, DH)
        gt = at(high, 6144, 10, NT)
        stw = at(high, 9216, 416)
        ew = at(high, 9632, 416)
        ctmp = at(high, 9216, 2, 315)
        cv27 = at(high, 9216, KI, 27)
        qz = at(high, 10048, MH, NT)
        vtr = at(high, 10048, 2, NT)
        wqkv = at(high, 10048 + 576, 4, 48)
        nraw = at(high, 11200, 512)
        cst = at(high, 11200, 2, DH)
        xsT = at(arena, 0, KD, SLOTS)
        ystok = at(arena, 0, 5, D)
        htok = at(arena, 5120, 3, D)
        rt = at(arena, 8192, 2048)
        sel = at(arena, 10240, 3, NSLOT)
        wt = at(arena, 10240, 5, NT)
        wsel = at(arena, 11968, 3, NSLOT)
        xcx = at(arena, 13696, 2, KD * CAP)
        sg = at(arena, 5120, 2, F)
        hx = at(arena, 6144, 2, F)
        ysb = at(arena, 7168, 2, F)
        hxT = at(arena, 14720, 2, MF * CAP)
        iota = at(arena, 15744, NSLOT)
        iota32 = at(arena, 16320, NE)
        wtmp = at(arena, 16352, NSLOT)
        uT = at(arena, 0, KI, NT)
        vT = at(arena, 4608, KI, NT)
        lnwb = at(arena, 4608, 2, INNER)
        vtk = at(arena, 9216, 3, INNER)
        raw_ws = at(arena, 9216, CG, P)
        wsT = at(arena, 15360, CG, P)
        bsb = at(arena, 16384, CG, P)
        wsS = at(arena, 17408, CG, NS)
        rep = at(arena, 17664, 32)
        mixt = at(arena, 17696, NT)
        bnst = at(arena, 17984, 3, 4 * 6)
        mvc = at(arena, 18056, 3, 2)
        ytok = at(arena, 0, 3, D)

        V = {}
        vec_rows = [("norm_mix", 16), ("norm_ffn", 16), ("norm_final", 8), ("mlstm_conv_w", 64), ("mlstm_conv_b", 16),
                    ("cmlp_b_out", 8), ("mlstm_skip", 16), ("mlstm_hn_w", 16), ("cmlp_b_in", 32)]
        c = 0
        for name, n in vec_rows:
            V[name] = c
            c += n

        def vec(name, k):
            return vecs[:, V[name] + k:V[name] + k + 1]

        NORM = [V["norm_mix"], V["norm_ffn"], V["norm_mix"] + 8, V["norm_ffn"] + 8, V["norm_final"]]

        place = {}
        count = [0] * RING
        for key, slots in (("up", [0, 1, 2, 0]), ("C", [(4 + p) % 3 for p in range(16)]), ("z", [3, 4, 5, 3]),
                           ("down", [4, 5, 3, 4]), ("in", [0, 1, 2, 3, 4, 5, 0, 1]), ("out", [2, 3, 4, 5])):
            for j, slot in enumerate(slots):
                count[slot] += 2 if key == "C" else 1
                place[key, j] = (slot, 16 * count[slot])

        def page(key, j):
            return ring[:, place[key, j][0], :]

        def landed(eng, key, j):
            slot, n = place[key, j]
            eng.wait_ge(s(f"page_landed{slot}"), n)

        def expert_pages(j):
            return (ring[:, 3 * j, :].rearrange("p (k f) -> p k f", k=KD),
                    ring[:, 3 * j + 1, :].rearrange("p (k f) -> p k f", k=KD),
                    ring[:, 3 * j + 2, :].rearrange("p (k f) -> p k f", k=MF))

        def sample_view(t):
            return t[:, XS:XE].rearrange("p (b x) -> p b x", x=7)

        yslot = nc.dram_tensor("yslot", (SLOTS, D), F32).ap()

        block = ctx.enter_context(nc.Block())

        @block.sync
        def _(sp):
            def load(key, j, src, dst=None):
                slot, _ = place[key, j]
                sp.dma_start(page(key, j) if dst is None else dst, src).then_inc(s(f"page_landed{slot}"), 16)

            w_up = A["mlstm_w_up"][0].rearrange("(k p) n -> p k n", p=P)
            w_dn = A["mlstm_w_down"][0].rearrange("(k p) n -> p k n", p=P)
            w_in = A["cmlp_w_in"][0].rearrange("(k p) n -> p k n", p=P)
            w_out = A["cmlp_w_out"][0].rearrange("(k p) n -> p k n", p=P)

            def k8(v):
                return v.rearrange("p (k n) -> p k n", k=KD)

            def k16(v):
                return v.rearrange("p (k n) -> p k n", k=KI)

            def state(t, p, n):
                h, b = p // 4, 2 * (p % 4) + n
                return t[0, b, h].rearrange("(i p) v -> p i v", p=P)

            def cview(p, n):
                return page("C", p)[:, 2048 * n:2048 * n + 2048].rearrange("p (i v) -> p i v", v=DH)

            def load_state(p):
                for n in range(2):
                    load("C", p, state(A["state_mlstm_C"], p, n), cview(p, n))

            for j in range(3):
                load("up", j, w_up[:, :, 512 * j:512 * j + 512], k8(page("up", j)))
            sp.wait_ge(s("xm_mm"), 4)
            load("up", 3, w_up[:, :, 1536:2048], k8(page("up", 3)))
            for p in range(2):
                sp.wait_ge(s("xm_mm"), 4 * (p + 2))
                load_state(p)
            sp.wait_ge(s("xm_mm"), 16)
            load_state(2)
            for p in range(16):
                sp.wait_ge(s("c_new"), 8 * (p + 1))
                for n in range(2):
                    sp.dma_start(state(O["C_s"], p, n), cview(p, n)).then_inc(s("c_stored"), 16)
                if p + 3 < 16:
                    sp.wait_ge(s("c_stored"), 32 * (p + 1))
                    load_state(p + 3)
            sp.wait_ge(s("num_mm"), 2 * H)
            for i in range(2):
                sp.wait_ge(s(f"cp_stored{i}"), 16 * 8)
            sp.wait_ge(s("cv_stored"), 32)
            for j in range(4):
                if j == 3:
                    sp.wait_ge(s("z_mm"), 4)
                load("z", j, w_up[:, :, 2048 + 512 * j:2560 + 512 * j], k8(page("z", j)))
            for j in range(4):
                if j < 2:
                    sp.wait_ge(s("z_mm"), 4 * (j + 2))
                elif j == 2:
                    sp.wait_ge(s("z_mm"), 16)
                else:
                    sp.wait_ge(s("down_mm"), 2)
                load("down", j, w_dn[:, :, 256 * j:256 * j + 256], k16(page("down", j)))
            sp.wait_ge(s("c_stored"), 32 * 16)

            def experts(L, base):
                gate = A["moe_w_gate"].rearrange("i g e (k p) f -> (i g e) p k f", p=P)
                up = A["moe_w_up"].rearrange("i g e (k p) f -> (i g e) p k f", p=P)
                down = A["moe_w_down"].rearrange("i g e (k p) n -> (i g e) p k n", p=P)
                before_loop = {3: ("down_mm", 6), 4: ("down_mm", 8), 5: ("down_mm", 4)} if L == 0 else \
                    {0: ("in_mm", 28), 1: ("in_mm", 32), 2: ("out_mm", 2), 3: ("out_mm", 4), 4: ("out_mm", 6),
                     5: ("out_mm", 8)}

                def turn(it, pair):
                    for j in range(2):
                        g, u, d = expert_pages(j)
                        for n, (dst, src, used) in enumerate((
                                (g, gate, f"gu_mm{j}"), (u, up, f"gu_mm{j}"), (d, down, f"y_mm{j}"))):
                            slot = 3 * j + n
                            if slot in before_loop:
                                sp.wait_ge(s(before_loop[slot][0]), before_loop[slot][1])
                            sp.wait_ge(s(used), it)
                            sp.dma_start(dst, src[bass.ds(L * NE + 2 * pair + j, 1)].rearrange("a p k f -> p (a k) f")) \
                                .then_inc(s(f"expert_landed{slot}"), 16)

                with sp.Fori(0, 15) as i:
                    turn(i + base, i)
                sp.wait_ge(s("table"), L + 1)
                rounds = sp.value_load(table[0:1, ROUNDS * NE + 1:ROUNDS * NE + 2], min_val=1, max_val=ROUNDS)
                with sp.Fori(15, rounds * 16) as i:
                    turn(i + base, i % 16)
                return base + rounds * 16

            turns = experts(0, 0)
            for j in range(8):
                if j < 6:
                    used = ("gu_mm", "gu_mm", "y_mm")[j % 3]
                    sp.wait_ge(s(f"{used}{j // 3}"), turns)
                else:
                    sp.wait_ge(s("in_mm"), 4 * (j - 5))
                load("in", j, w_in[:, :, 512 * j:512 * j + 512], k8(page("in", j)))
                if j == 0:
                    sp.wait_ge(s("moe_add"), KD)
                    sp.dma_start(raw_ws, A["cmlp_w_s"][0].rearrange("g t s -> t g s")).then_inc(s("ws_landed"), 16)
                    sp.dma_start(bsb.rearrange("p g t -> p (g t)"),
                                 A["cmlp_b_s"].rearrange("o g t -> o (g t)").to_broadcast([P, CG * P])) \
                        .then_inc(s("bs_landed"), 16)
            for j in range(4):
                sp.wait_ge(s("in_mm"), 4 * (j + 3))
                load("out", j, w_out[:, :, 256 * j:256 * j + 256], k16(page("out", j)))
                if j == 2:
                    sp.wait_ge(s("vtok_mm"), 12)
                    for n, name in enumerate(("cmlp_ln_w", "cmlp_ln_b")):
                        sp.dma_start(lnwb[:, n, :], A[name].to_broadcast([P, INNER])).then_inc(s("ln_landed"), 16)
            experts(1, turns)
            sp.wait_ge(s("y_ready"), 6)
            sp.dma_start(O["y_p"][0].rearrange("(j p) n -> p j n", p=P), ytok[:, 0:2, :]).then_inc(s("y_stored"), 16)
            sp.dma_start(O["y_s"].rearrange("b s n -> (b s) n"), ytok[0:NS, 2, :]).then_inc(s("y_stored"), 16)
            sp.wait_ge(s("y_stored"), 32)
            sp.wait_ge(s("np_stored"), 16 * H)

        @block.gpsimd
        def _(pool):
            chain = [0]

            def link(ins):
                chain[0] += 1
                ins.then_inc(s("pool_chain"), 1)
                pool.wait_ge(s("pool_chain"), chain[0])

            def keep(t, pattern, base, mult, fill=0.0, op=ALU.is_ge):
                return pool.affine_select(out=t, in_=t, compare_op=op, fill=fill, base=base,
                                          pattern=pattern, channel_multiplier=mult)

            link(pool.memset(ident[:], 0.0))
            keep(ident[:], [[-1, P]], 0, 1, 1.0, ALU.not_equal).then_inc(s("consts"), 1)
            pool.memset(ones[:], 1.0).then_inc(s("consts"), 1)
            link(pool.memset(bmask[:], 1.0))
            link(keep(bmask[:], [[-4, 32]], 0, 1))
            keep(bmask[:], [[4, 32]], 3, -1).then_inc(s("consts"), 1)
            link(pool.memset(before[:], 1.0))
            keep(before[:], [[1, P]], -1, -1).then_inc(s("consts"), 1)
            pool.memset(xe[:, :, 0:3], 0.0).then_inc(s("consts"), 1)
            link(pool.memset(small[:], 0.0))
            link(pool.memset(eps6, 1e-6))
            pool.memset(eps5, 1e-5).then_inc(s("consts"), 1)
            pool.memset(rows[:], 0.0).then_inc(s("consts"), 1)
            pool.wait_ge(s("consts"), 3)
            pool.wait_ge(s("raw_out"), 7)
            for n in range(3):
                for i in range(4):
                    pool.tensor_tensor(
                        bd[:, n, :, :].rearrange("p m (n d) -> p m n d", d=4)[:, :, :, i],
                        wqkv[:, i, 16 * n:16 * n + 16].unsqueeze(2).to_broadcast([P, KI, 32]),
                        bmask[:].unsqueeze(1).to_broadcast([P, KI, 32]), ALU.mult).then_inc(s("bd"), 1)
            pool.wait_ge(s("gate_part"), KI)
            pool.wait_ge(s("bd"), 12)
            pool.memset(qz, 0.0).then_inc(s("qz_zero"), 1)
            n_in = A["state_mlstm_n"][0].rearrange("b h d -> h b d")
            n_out = O["n_s"][0].rearrange("b h d -> h b d")
            for h in range(2):
                pool.dma_start(nrow[:, h, :], n_in[h]).then_inc(s(f"n_landed{h}"), 16)
            pool.wait_ge(s("cv_out"), 4)
            pool.dma_start(O["conv_p"][0, 0], cvout[0:3]).then_inc(s("cv_stored"), 16)
            pool.dma_start(O["conv_s"][0].rearrange("b c n -> (b c) n"), cvout[3:27]).then_inc(s("cv_stored"), 16)
            pool.wait_ge(s("gates_dve"), 2)
            pool.dma_start(O["m_p"][0].rearrange("o h -> h o"), rows[32:36, NPROMPT - 1:NPROMPT],
                           allow_slow_non_contiguous=True).then_inc(s("m_stored"), 16)
            pool.dma_start(O["m_s"][0].rearrange("b h -> h b"), rows[32:36, NPROMPT + 3:NT:SB],
                           allow_slow_non_contiguous=True).then_inc(s("m_stored"), 16)
            for h in range(H):
                pool.wait_ge(s("e_ready"), 3 * (h + 1))
                keep(ew[:, 0:128], [[1, P]], 0, -1).then_inc(s("e_masked"), 1)
                keep(ew[:, 256:384], [[1, P]], 0, -1).then_inc(s("e_masked"), 1)
                es = ew[0:NS, 384:416].rearrange("p (b t) -> p b t", t=SB)
                link(keep(es, [[SB, NB], [1, SB]], 0, -1))
                keep(es, [[-SB, NB], [0, SB]], 0, 1).then_inc(s("e_masked"), 1)
                pool.wait_ge(s("ns_out"), h + 1)
                pool.dma_start(n_out[h], nrow[:, h % 2, :]).then_inc(s(f"n_stored{h % 2}"), 16)
                if h + 2 < H:
                    pool.wait_ge(s(f"n_stored{h % 2}"), 16 * (h // 2 + 1))
                    pool.dma_start(nrow[:, h % 2, :], n_in[h + 2]).then_inc(s(f"n_landed{h % 2}"), 16)
            for i in range(2):
                pool.wait_ge(s(f"n_stored{i}"), 32)
            pool.wait_ge(s("m_stored"), 32)
            for L in range(2):
                pool.wait_ge(s(("down_add", "out_add")[L]), KD)
                pool.iota(iota, [[1, NSLOT]], base=0, channel_multiplier=0,
                          allow_small_or_imprecise_dtypes=True).then_inc(s("iota"), 1)
                pool.iota(iota32, [[1, NE]], base=0, channel_multiplier=0,
                          allow_small_or_imprecise_dtypes=True).then_inc(s("iota"), 1)
                pool.wait_ge(s("iota"), 2 * L + 2)
                pool.memset(xsT[:, :, NSLOT:SLOTS], 0.0).then_inc(s("xs_pad"), 1)
                pool.wait_ge(s("slots"), 2 * L + 2)
                for j, (_, n) in enumerate(TOK):
                    link(pool.tensor_scalar(wtmp[0:n], iota[0:n], slotw[0:n, j:j + 1], slotw[0:n, 6 + j:7 + j],
                                            ALU.is_equal, ALU.mult))
                    link(pool.tensor_scalar(wsel[0:n, j, :], iota[0:n], slotw[0:n, 3 + j:4 + j], slotw[0:n, 9 + j:10 + j],
                                            ALU.is_equal, ALU.mult))
                    ins = pool.tensor_tensor(wsel[0:n, j, :], wsel[0:n, j, :], wtmp[0:n], ALU.add)
                    ins.then_inc(s("wsel"), 1)
                    pool.wait_ge(s("wsel"), 3 * L + j + 1)
                if L == 0:
                    pool.wait_ge(s("ws_out"), 2)
                    keep(wsT, [[0, CG], [1, P]], 0, -1).then_inc(s("ws_masked"), 1)
                    pool.wait_ge(s("v_norm"), 3)
                    pool.dma_start(O["v_s"][0].rearrange("b s n -> (b s) n"), vtk[0:NS, 2, :]).then_inc(s("v_stored"), 16)
                    pool.wait_ge(s("v_stored"), 16)

        @block.scalar
        def _(act):
            ld = [0]

            def get(dst, src):
                act.dma_start(dst, src, allow_slow_non_contiguous=True).then_inc(s("raw_landed"), 16)

            for j, (t0, n) in enumerate(TOK):
                src = A["x_prompt"][0, t0:t0 + n, :] if j < 2 else A["x_sample"].rearrange("b s n -> (b s) n")
                act.dma_start(xtok[0:n, j, :], src).then_inc(s("x_landed"), 16)
            for name, n in vec_rows:
                c0 = V[name]
                half, r0 = (0, c0) if c0 < 128 else (1, c0 - 128)
                a = A[name]
                flat = a if len(a.shape) == 1 else a.rearrange({2: "a b -> (a b)", 3: "a b c -> (a b c)"}[len(a.shape)])
                get(raw_vec[r0:r0 + n, half, :], flat.rearrange("(r p) -> r p", p=P))
            for n, name in enumerate(("mlstm_w_q", "mlstm_w_k", "mlstm_w_v")):
                get(raw_qkv[16 * n:16 * n + 16], A[name][0].rearrange("(m n) c d -> m (n c d)", m=KI))
            for n, name in enumerate(("mlstm_w_ig", "mlstm_w_fg")):
                get(raw_if[0:48, n, :], A[name][0].rearrange("(t p) h -> t (p h)", p=P))
            get(raw_re[0:64], A["moe_w_re"].rearrange("i g (k p) e -> (i g k) (p e)", p=P))
            get(raw_rg[0:16], A["moe_w_rg"].rearrange("i (k p) g -> (i k) (p g)", p=P))
            get(raw_conv[0:24], A["state_mlstm_conv"][0].rearrange("b c n -> (b c) n"))
            get(nraw[0:32], A["state_mlstm_n"][0].rearrange("b h d -> (b h) d"))
            get(m0[:], A["state_mlstm_m"][0].rearrange("b h -> h b"))
            get(gb[:, 0:1], A["mlstm_b_ig"].rearrange("o h -> h o"))
            get(gb[:, 1:2], A["mlstm_b_fg"].rearrange("o h -> h o"))
            for i in range(2):
                get(rbias[:, i, 0:G], A["moe_b_rg"][i:i + 1].to_broadcast([P, G]))
                get(rbias[:, i, G:36], A["moe_b_re"][i:i + 1].rearrange("o g e -> o (g e)").to_broadcast([P, NE]))

            def norm(n, x_sem, x_count):
                act.wait_ge(s(x_sem), x_count)
                act.activation(hT[:], xT[:], ACT.Square).then_inc(s("sq"), 1)
                act.wait_ge(s("ss"), n + 1)
                act.activation(stdv, B[7][:, 0:NT], ACT.Sqrt, bias=eps6, scale=1.0 / D).then_inc(s("std"), 1)

            for k in range(KD):
                act.wait_ge(s("x_tr"), k + 1)
                act.activation(xT[:, k, :], B[k % 2][:, 0:NT], ACT.Copy).then_inc(s("xT"), 1)
            act.wait_ge(s("consts"), 6)
            norm(0, "xT", KD)
            for m in range(KI + 1):
                if m < KI:
                    act.wait_ge(s("xm_mm"), m + 1)
                    act.activation(xe[:, m, 3:XS], B[m % 4][:, 0:NPROMPT], ACT.Copy).then_inc(s("xm_out"), 1)
                    act.activation(sample_view(xe[:, m, :])[:, :, 3:7],
                                   B[m % 4][:, NPROMPT:NT].rearrange("p (b s) -> p b s", s=SB),
                                   ACT.Copy).then_inc(s("xm_out"), 1)
                    act.activation(xms[:, m, :], B[m % 4][:, NPROMPT:NT], ACT.Copy).then_inc(s("xm_out"), 1)
                if m > 0:
                    c = m - 1
                    act.wait_ge(s("conv"), c + 1)
                    act.activation(xc[:, c, 0:NPROMPT], ctmp[:, c % 2, 0:NPROMPT], ACT.Silu).then_inc(s("xc"), 1)
                    act.activation(xc[:, c, NPROMPT:NT].rearrange("p (b s) -> p b s", s=SB),
                                   sample_view(ctmp[:, c % 2, :])[:, :, 0:4], ACT.Silu).then_inc(s("xc"), 1)
            for m in range(KI):
                act.wait_ge(s("qkv_mm"), m + 1)
                if m == 0:
                    act.wait_ge(s("raw_out"), 7)
                act.activation(qT[:, m, :], B[m % 2][:, 0:NT], ACT.Copy).then_inc(s("q_out"), 1)
                if m >= 2:
                    act.wait_ge(s("gate_part"), m - 1)
                act.activation(vtr[:, m % 2, :], B[4 + m % 2][:, 0:NT], ACT.Copy).then_inc(s("v_out"), 1)
            act.wait_ge(s("gate_part"), KI)
            act.activation(gt[0:8, 0, :], B[6][0:8, 0:NT], ACT.Copy).then_inc(s("gates_act"), 1)
            act.wait_ge(s("gates_pe"), 1)
            act.activation(gt[0:4, 1, :], B[0][0:4, 0:NT], ACT.Identity, bias=gb[:, 0:1]).then_inc(s("gates_act"), 1)
            act.activation(gt[0:4, 2, :], B[1][0:4, 0:NT], ACT.Identity, bias=gb[:, 1:2]).then_inc(s("gates_act"), 1)
            act.wait_ge(s("gates_dve"), 1)
            act.activation(gt[0:4, 4, :], gt[0:4, 3, :], ACT.Exp, scale=-1.0).then_inc(s("gates_act"), 1)
            act.wait_ge(s("gates_act"), 4)
            act.wait_ge(s("consts"), 2)
            act.activation(gt[0:4, 3, :], gt[0:4, 4, :], ACT.Ln, bias=ones[0:4, 0:1]).then_inc(s("gates_act"), 1)
            act.wait_ge(s("gates_pe"), 2)
            for j, (_, n) in enumerate(TOK):
                b = B[2][0:n, 128 * j:128 * j + 128]
                act.activation(tm[0:n, j, 0:4], b[:, 0:4], ACT.Copy).then_inc(s("tm"), 1)
                act.activation(tm[0:n, j, 4:8], b[:, 32:36], ACT.Exp, scale=-1.0).then_inc(s("tm"), 1)
                act.activation(tm[0:n, j, 8:12], b[:, 96:100], ACT.Exp).then_inc(s("tm"), 1)
            act.activation(decn[:], B[3][0:NB, 0:H], ACT.Exp).then_inc(s("tm"), 1)
            act.wait_ge(s("tm"), 10)

            cst_n = 0
            for h in range(H):
                act.wait_ge(s("bc_mm"), h + 1)
                act.activation(decb[:, h, :], B[0][:, NT:NT + 8], ACT.Exp).then_inc(s("bc_exp"), 1)
                act.activation(ibc[:, h, :], B[0][:, NT + 8:NT + 8 + NS], ACT.Exp).then_inc(s("bc_exp"), 1)
                if h > 0:
                    act.wait_ge(s("stw"), 3 * h)
                act.activation(ew[:, 0:256], B[0][:, 0:256], ACT.Exp, scale=-1.0, bias=tm[:, 0, h:h + 1]) \
                    .then_inc(s("e_ready"), 1)
                act.activation(ew[:, 256:384], B[0][:, 128:256], ACT.Exp, scale=-1.0, bias=tm[:, 1, h:h + 1]) \
                    .then_inc(s("e_ready"), 1)
                act.activation(ew[0:NS, 384:416], B[0][0:NS, 256:288], ACT.Exp, scale=-1.0,
                               bias=tm[0:NS, 2, h:h + 1]).then_inc(s("e_ready"), 1)
                act.wait_ge(s("kv_mm"), 2 * h + 2)
                if h > 0:
                    act.wait_ge(s("num_mm"), 2 * h)
                for j, (_, n) in enumerate(TOK):
                    act.activation(vtok[0:n, j, :], B[4 + j][0:n, :], ACT.Copy).then_inc(s("vtok"), 1)
                for n in range(4):
                    act.wait_ge(s("spread_mm"), 4 * h + n + 1)
                    if n < 2 and h > 0:
                        act.wait_ge(s("parts"), 4 * h)
                    elif n >= 2:
                        act.wait_ge(s("parts"), 4 * h + n - 1)
                    act.activation(y16[:, n % 2, :], B[1 + n][:, :], ACT.Copy).then_inc(s("y1"), 1)
                for i in range(MH):
                    act.wait_ge(s("cp_mm"), 4 * h + i + 1)
                    if cst_n >= 2:
                        act.wait_ge(s(f"cp_stored{i % 2}"), 16 * (cst_n // 2))
                    act.activation(cst[:, i % 2, :], B[5 + i % 2][:, :], ACT.Copy).then_inc(s("cp_out"), 1)
                    act.wait_ge(s("cp_out"), cst_n + 1)
                    act.dma_start(O["C_p"][0, 0, h, 128 * i:128 * i + 128, :], cst[:, i % 2, :]) \
                        .then_inc(s(f"cp_stored{i % 2}"), 16)
                    cst_n += 1
                act.wait_ge(s("np_mm"), h + 1)
                if h > 0:
                    act.wait_ge(s("np_stored"), 16 * h)
                act.activation(nst[:], B[0][0:1, :], ACT.Copy).then_inc(s("np_out"), 1)
                act.wait_ge(s("np_out"), h + 1)
                act.dma_start(O["n_p"][0, :, h, :], nst[:]).then_inc(s("np_stored"), 16)
                act.wait_ge(s("rden"), 2 * h + 1)
                for j in range(2):
                    act.activation(hhp[h][:, j, :], B[1 + j][:, :], ACT.Copy, scale=rden[:, j:j + 1]) \
                        .then_inc(s("hh"), 1)
                act.wait_ge(s("c_mm"), 32 * (h + 1))
                act.activation(snum, B[4][:, :], ACT.Copy).then_inc(s("snum"), 1)
                act.wait_ge(s("num_mm"), 2 * h + 2)
                act.wait_ge(s("rden"), 2 * h + 2)
                act.activation(hhs[h][0:NS], B[4][0:NS, :], ACT.Copy, scale=rden[0:NS, 2:3]).then_inc(s("hh"), 1)
            for m in range(KI):
                act.wait_ge(s("z_mm"), m + 1)
                act.activation(zs[:, m, :], B[m % 4][:, 0:NT], ACT.Silu).then_inc(s("zs"), 1)
            act.wait_ge(s("mv"), 12)
            act.activation(mvsd, mvsd, ACT.Sqrt, bias=eps5).then_inc(s("hsd"), 1)

            def moe(L, base):
                norm(1 + 2 * L, ("down_add", "out_add")[L], KD)
                for n in range(6):
                    j, c = divmod(n, 2)
                    t = TOK[j][1]
                    act.wait_ge(s("htok_mm"), 6 * L + n + 1)
                    act.activation(htok[0:t, j, 512 * c:512 * c + 512], B[n][0:t, :], ACT.Copy) \
                        .then_inc(s("htok"), 1)
                act.wait_ge(s("router_dve"), 3 * L + 1)
                act.activation(rt[:, 320:332], rt[:, 300:312], ACT.Exp).then_inc(s("router_act"), 1)
                act.wait_ge(s("router_dve"), 3 * L + 2)
                act.activation(rt[:, 343:346], rt[:, 340:343], ACT.Exp).then_inc(s("router_act"), 1)
                for n in range(1, 16, 2):
                    c, m = divmod(n, 8)
                    act.wait_ge(s("gather_mm"), 16 * L + n + 1)
                    act.activation(xsT[:, m, NT * c:NT * c + NT], B[n % 6][:, 0:NT], ACT.Copy) \
                        .then_inc(s("xs_a"), 1)
                act.wait_ge(s("table"), L + 1)
                rounds = act.value_load(table[0:1, ROUNDS * NE + 1:ROUNDS * NE + 2], min_val=1, max_val=ROUNDS)
                with act.Fori(0, rounds * 16) as i:
                    it = i + base
                    for j in range(2):
                        off = act.value_load(table[0:1, bass.ds(2 * i + j, 1)], min_val=0, max_val=NSLOT)
                        act.wait_ge(s(f"gu_mm{j}"), it + 1)
                        act.activation(sg[CAP:P, j, :], B[j][0:CAP, :], ACT.Silu).then_inc(s(f"sg{j}"), 1)
                        act.wait_ge(s(f"y_mm{j}"), it + 1)
                        act.wait_ge(s("ys"), (2 * it + j) * 32)
                        act.activation(ysb[:, j, :], B[2 + j][:, :], ACT.Copy).then_inc(s(f"y_out{j}"), 1)
                        act.wait_ge(s(f"y_out{j}"), it + 1)
                        for c in range(2):
                            act.dma_start(yslot[bass.ds(off, CAP), F * c:F * c + F], ysb[CAP * c:CAP * c + CAP, j, :]) \
                                .then_inc(s("ys"), 16)
                act.wait_ge(s("ys"), (base + rounds * 16) * 64)
                act.wait_ge(s("xcx0"), (base + rounds * 16) + (L + 1))
                for q, (q0, qn) in enumerate(QT):
                    act.dma_start(ystok[0:qn, q, :], yslot[q0:q0 + qn, :]).then_inc(s("yt_landed"), 16)
                return base + rounds * 16

            turns = moe(0, 0)
            norm(2, "moe_add", KD)
            for m in range(2 * KI):
                act.wait_ge(s("in_mm"), m + 1)
                dst = uT[:, m, :] if m < KI else vT[:, m - KI, :]
                act.activation(dst, B[m % 4][:, 0:NT], ACT.Gelu_apprx_tanh, bias=vec("cmlp_b_in", m)) \
                    .then_inc(s("gelu"), 1)
            for j, (_, n) in enumerate(TOK):
                act.wait_ge(s("vstat"), j + 1)
                act.activation(mvc[0:n, j, 1:2], mvc[0:n, j, 1:2], ACT.Sqrt, bias=eps5[0:n]).then_inc(s("vsd"), 1)
            moe(1, turns)
            norm(4, "moe_add", 2 * KD)
            for n in range(6):
                j, c = divmod(n, 2)
                t = TOK[j][1]
                act.wait_ge(s("y_tr"), n + 1)
                act.activation(ytok[0:t, j, 512 * c:512 * c + 512], B[n][0:t, :], ACT.Copy).then_inc(s("y_ready"), 1)

        @block.tensor
        def _(pe):
            mm, tr = pe.matmul, pe.transpose
            pe.wait_ge(s("consts"), 1)
            pe.wait_ge(s("x_landed"), 48)
            for k in range(KD):
                if k >= 2:
                    pe.wait_ge(s("xT"), k - 1)
                for j, (t0, n) in enumerate(TOK):
                    ins = tr(B[k % 2][:, t0:t0 + n], xtok[0:n, j, 128 * k:128 * k + 128], ident[0:n, 0:n])
                ins.then_inc(s("x_tr"), 1)
            NRAW = 16 * (len(vec_rows) + 3 + 2 + 4 + 3 + 4)
            pe.wait_ge(s("raw_landed"), NRAW)
            tr(B[2][:, 0:128], raw_vec[:, 0, :], ident[:])
            tr(B[2][:, 128:192], raw_vec[0:64, 1, :], ident[0:64, 0:64]).then_inc(s("raw_tr"), 1)
            for i in range(4):
                ins = tr(B[3][:, 48 * i:48 * i + 48], raw_qkv[0:48].rearrange("m (p d) -> m p d", d=4)[:, :, i],
                         ident[0:48, 0:48])
            ins.then_inc(s("raw_tr"), 1)
            for n in range(8):
                ins = tr(B[4][:, 48 * n:48 * n + 48],
                         raw_if[0:48, n // 4, :].rearrange("t (p h) -> t p h", h=4)[:, :, n % 4], ident[0:48, 0:48])
            ins.then_inc(s("raw_tr"), 1)
            for e in range(8):
                ins = tr(B[5][:, 64 * e:64 * e + 64], raw_re[0:64].rearrange("m (p e) -> m p e", e=8)[:, :, e],
                         ident[0:64, 0:64])
            ins.then_inc(s("raw_tr"), 1)
            for g in range(4):
                ins = tr(B[6][:, 16 * g:16 * g + 16], raw_rg[0:16].rearrange("m (p g) -> m p g", g=4)[:, :, g],
                         ident[0:16, 0:16])
            ins.then_inc(s("raw_tr"), 1)
            for m in range(KI):
                ins = tr(B[7][:, 24 * m:24 * m + 24], raw_conv[0:24, 128 * m:128 * m + 128], ident[0:24, 0:24])
            ins.then_inc(s("raw_tr"), 1)
            pe.wait_ge(s("xT"), KD)
            for i in range(MH):
                ins = tr(B[0][:, 32 * i:32 * i + 32], nraw[0:32, 128 * i:128 * i + 128], ident[0:32, 0:32])
            ins.then_inc(s("raw_tr"), 1)
            pe.wait_ge(s("raw_out"), 7)

            def norm(n):
                pe.wait_ge(s("sq"), n + 1)
                for k in range(KD):
                    ins = mm(B[7][:, 0:NT], ones[:], hT[:, k, :], start=(k == 0), stop=(k == KD - 1))
                ins.then_inc(s("ss"), 1)
                pe.wait_ge(s("h_norm"), KD * (n + 1))

            def dense(key, groups, per, width, kt, rhs, done, freed):
                m = 0
                for j in range(groups):
                    landed(pe, key, j)
                    w = page(key, j).rearrange("p (k n) -> p k n", k=kt)
                    for i in range(per):
                        if m >= 4:
                            freed(m - 4)
                        for k in range(kt):
                            ins = mm(B[m % 4][:, 0:NT], w[:, k, 128 * i:128 * i + 128], rhs(k),
                                     start=(k == 0), stop=(k == kt - 1))
                        ins.then_inc(s(done), 1)
                        m += 1

            pe.wait_ge(s("consts"), 2)
            norm(0)
            dense("up", 4, 4, 512, KD, lambda k: hT[:, k, :], "xm_mm", lambda m: pe.wait_ge(s("xm_out"), 3 * m + 3))

            def gate_part(m):
                pe.wait_ge(s("q_out"), m + 1)
                pe.wait_ge(s("k_out"), m + 1)
                pe.wait_ge(s("v_out"), m + 1)
                for n, src in enumerate((qT[:, m, :], kT[:, m, :], vtr[:, m % 2, :])):
                    ins = mm(B[6][0:8, 0:NT], wif[:, 16 * n + m, :], src,
                             start=(m == 0 and n == 0), stop=(m == KI - 1 and n == 2), skip_group_check=True)
                ins.then_inc(s("gate_part"), 1)

            pe.wait_ge(s("bd"), 12)
            pe.wait_ge(s("xm_out"), 3 * KI)
            for m in range(KI):
                pe.wait_ge(s("xc"), 2 * m + 2)
                if m >= 2:
                    pe.wait_ge(s("q_out"), m - 1)
                    pe.wait_ge(s("k_out"), m - 1)
                    pe.wait_ge(s("v_out"), m - 1)
                mm(B[m % 2][:, 0:NT], bd[:, 0, m, :], xc[:, m, :], start=True, stop=True)
                mm(B[2 + m % 2][:, 0:NT], bd[:, 1, m, :], xc[:, m, :], start=True, stop=True)
                mm(B[4 + m % 2][:, 0:NPROMPT], bd[:, 2, m, :], xe[:, m, 3:XS], start=True, stop=True)
                mm(B[4 + m % 2][:, NPROMPT:NT], bd[:, 2, m, :], xms[:, m, :],
                   start=True, stop=True).then_inc(s("qkv_mm"), 1)
                if m >= 1:
                    gate_part(m - 1)
            gate_part(KI - 1)
            pe.wait_ge(s("q_out"), KI)
            pe.wait_ge(s("k_out"), KI)
            pe.wait_ge(s("v_out"), KI)
            pe.wait_ge(s("cv27"), 2)
            for m in range(KI):
                if m in (8, 12):
                    pe.wait_ge(s("cv_out"), m // 4 - 1)
                ins = tr(B[4 + (m // 4) % 2][0:27, 128 * (m % 4):128 * (m % 4) + 128], cv27[:, m, :], ident[:])
                if m % 4 == 3:
                    ins.then_inc(s("cv_tr"), 1)
            pe.wait_ge(s("gates_act"), 1)
            mm(B[0][0:4, 0:NT], ident[0:8, 0:4], gt[0:8, 0, :], start=True, stop=True)
            mm(B[1][0:4, 0:NT], ident[0:8, 4:8], gt[0:8, 0, :], start=True, stop=True).then_inc(s("gates_pe"), 1)
            pe.wait_ge(s("gates_dve"), 2)
            for j, (t0, n) in enumerate(TOK):
                tr(B[2][0:n, 128 * j:128 * j + 128], rows[:, t0:t0 + n], ident[:])
            tr(B[3][0:NB, 0:H], catA[0:4, NT:NT + 8], ident[0:4, 0:4]).then_inc(s("gates_pe"), 1)
            pe.wait_ge(s("tm"), 10)
            pe.wait_ge(s("cv_out"), 4)

            pe.wait_ge(s("part_masks"), 1)
            for h in range(H):
                if h > 0:
                    pe.wait_ge(s("hh"), 3 * h)
                    pe.wait_ge(s("rden"), 2 * h)
                    pe.wait_ge(s("c_new"), 32 * h)
                mm(B[0][:, 0:NT + 8 + NS], ident[0:4, h:h + 1].to_broadcast([4, P]), catA[:, :],
                   start=True, stop=True).then_inc(s("bc_mm"), 1)
                for j, (t0, t) in enumerate(TOK):
                    for i in range(MH):
                        ins = tr(B[1 + j][0:t, 128 * i:128 * i + 128], kT[:, MH * h + i, t0:t0 + t], ident[:])
                ins.then_inc(s("kv_mm"), 1)
                for j, (t0, t) in enumerate(TOK):
                    for i in range(MH):
                        m = MH * h + i
                        lhs = xe[:, m, 3 + t0:3 + t0 + t] if j < 2 else xms[:, m, :]
                        ins = mm(B[4 + j][0:t, 128 * i:128 * i + 128], lhs, bd[:, 2, m, :], start=True, stop=True)
                ins.then_inc(s("kv_mm"), 1)
                for i in range(MH):
                    mm(B[7][:, 0:256], kT[:, MH * h + i, 0:128], qT[:, MH * h + i, 0:256],
                       start=(i == 0), stop=(i == MH - 1))
                for i in range(MH):
                    mm(B[7][:, 256:384], kT[:, MH * h + i, 128:256], qT[:, MH * h + i, 128:256],
                       start=(i == 0), stop=(i == MH - 1))
                for i in range(MH):
                    ins = mm(B[7][0:NS, 384:416], kT[:, MH * h + i, 256:288], qT[:, MH * h + i, 256:288],
                             start=(i == 0), stop=(i == MH - 1))
                ins.then_inc(s("st_mm"), 1)
                pe.wait_ge(s("wk"), 3 * h + 3)
                pe.wait_ge(s("vtok"), 3 * h + 3)
                for n, src in enumerate((wk, vtok)):
                    for half in range(2):
                        mm(B[1 + 2 * n + half][:, :], spread[0:NS, half, :], src[0:NS, 2, :],
                           start=True, stop=True).then_inc(s("spread_mm"), 1)
                for i in range(MH):
                    if i >= 2:
                        pe.wait_ge(s("cp_out"), MH * h + i - 1)
                    for j in range(2):
                        ins = mm(B[5 + i % 2][:, :], wk[:, j, 128 * i:128 * i + 128], vtok[:, j, :],
                                 start=(j == 0), stop=(j == 1))
                    ins.then_inc(s("cp_mm"), 1)
                pe.wait_ge(s("e_ready"), 3 * h + 3)
                for j in range(2):
                    ins = mm(B[0][0:1, :], ones[:, 0:1], wk[:, j, :], start=(j == 0), stop=(j == 1))
                ins.then_inc(s("np_mm"), 1)
                pe.wait_ge(s("stw"), 3 * h + 3)
                pe.wait_ge(s("z1"), 4 * (h + 1))
                mm(B[1][:, :], stw[:, 0:128], vtok[:, 0, :], start=True, stop=True)
                mm(B[2][:, :], stw[:, 128:256], vtok[:, 0, :], start=True, stop=False)
                mm(B[2][:, :], stw[:, 256:384], vtok[:, 1, :], start=False, stop=True)
                mm(B[3][:, 0:1], stw[:, 0:128], ones[:, 0:1], start=True, stop=True)
                mm(B[3][:, 1:2], stw[:, 128:256], ones[:, 0:1], start=True, stop=False)
                mm(B[3][:, 1:2], stw[:, 256:384], ones[:, 0:1], start=False, stop=True).then_inc(s("num_mm"), 1)
                mm(B[7][0:NB, :], bmask[0:NS, 0:NB], wk[0:NS, 2, :], start=True, stop=True).then_inc(s("ns_mm"), 1)
                pe.wait_ge(s("cp_out"), MH * h + MH)
                pe.wait_ge(s("qz"), 2 * h + 1)
                for b in range(NB):
                    p = 4 * h + b // 2
                    if b % 2 == 0:
                        landed(pe, "C", p)
                    cpage = page("C", p).rearrange("p (c v) -> p c v", v=DH)
                    for i in range(MH):
                        mm(B[4][NS * i:NS * i + NS, :], qz[:, i, NS * b:NS * b + NS], cpage[:, MH * (b % 2) + i, :],
                           start=(b == 0), stop=(b == NB - 1), skip_group_check=True)
                    if b == 0:
                        pe.wait_ge(s("parts"), 4 * (h + 1))
                        pe.wait_ge(s("ns_out"), h + 1)
                        pe.wait_ge(s("np_out"), h + 1)
                    g = 32 * (b % 4)
                    for i in range(MH):
                        n = (NB * h + b) * MH + i
                        if n >= 4:
                            pe.wait_ge(s("c_new"), n - 3)
                        mm(B[UPD[i]][:, :], wk8[g:g + 32, b // 4, 128 * i:128 * i + 128], v8[g:g + 32, b // 4, :],
                           start=True, stop=True).then_inc(s("c_mm"), 1)
                pe.wait_ge(s("rden"), 2 * h + 1)
                mm(B[3][0:NS, 2:3], stw[0:NS, 384:416], ones[0:NS, 0:1], start=True, stop=False)
                pe.wait_ge(s("qz"), 2 * h + 2)
                for i in range(MH):
                    mm(B[3][0:NS, 2:3], ew[:, 32 * i:32 * i + 32], ones[:, 0:1], start=False, stop=(i == MH - 1))
                pe.wait_ge(s("snum"), h + 1)
                mm(B[4][0:NS, :], fold, snum, start=True, stop=False)
                mm(B[4][0:NS, :], stw[0:NS, 384:416], vtok[0:NS, 2, :], start=False, stop=True) \
                    .then_inc(s("num_mm"), 1)
            pe.wait_ge(s("hh"), 3 * H)
            pe.wait_ge(s("c_new"), 32 * H)
            pe.wait_ge(s("ns_out"), H)
            dense("z", 4, 4, 512, KD, lambda k: hT[:, k, :], "z_mm", lambda m: pe.wait_ge(s("zs"), m + 1))
            for m in range(KI):
                h, i = divmod(m, MH)
                pe.wait_ge(s("hn"), 3 * h + 3)
                if m >= 2:
                    pe.wait_ge(s("y_in"), m - 1)
                for j, (t0, n) in enumerate(TOK):
                    src = hhp[h][:, j, 128 * i:128 * i + 128] if j < 2 else hhs[h][0:NS, 128 * i:128 * i + 128]
                    ins = tr(B[4 + m % 2][:, t0:t0 + n], src, ident[0:n, 0:n])
                ins.then_inc(s("hn_tr"), 1)
            pe.wait_ge(s("y_mix"), KI)
            dense("down", 4, 2, 256, KI, lambda k: xc[:, k, :], "down_mm", lambda m: pe.wait_ge(s("down_add"), m + 1))
            pe.wait_ge(s("down_add"), KD)

            def moe(L, base):
                norm(1 + 2 * L)
                for n in range(6):
                    j, c = divmod(n, 2)
                    t0, t = TOK[j]
                    for k in range(4):
                        ins = tr(B[n][0:t, 128 * k:128 * k + 128], hT[:, 4 * c + k, t0:t0 + t], ident[:])
                    ins.then_inc(s("htok_mm"), 1)
                for j, (t0, t) in enumerate(TOK):
                    for k in range(KD):
                        ins = mm(B[6][0:t, 36 * j:36 * j + 36], hT[:, k, t0:t0 + t], wr[:, L, k, :],
                                 start=(k == 0), stop=(k == KD - 1))
                ins.then_inc(s("router_pe"), 1)
                pe.wait_ge(s("router_dve"), 3 * L + 3)
                pe.wait_ge(s("consts"), 4)
                m2 = rt[:, 0:96].rearrange("p (j e) -> p j e", j=3)
                for j, (_, t) in enumerate(TOK):
                    for i in range(j):
                        mm(B[7][0:t, 32 * j:32 * j + 32], ones[:, 0:t], m2[:, i, :], start=(i == 0), stop=False)
                    mm(B[7][0:t, 32 * j:32 * j + 32], before[0:t, 0:t], m2[0:t, j, :], start=(j == 0), stop=True)
                for j, (_, t) in enumerate(TOK):
                    ins = mm(B[7][:, 96:128], ones[0:t, :], m2[0:t, j, :], start=(j == 0), stop=(j == 2))
                ins.then_inc(s("router_pe"), 1)
                pe.wait_ge(s("htok"), 6 * L + 6)
                pe.wait_ge(s("sel"), 3 * L + 3)
                for n in range(16):
                    c, m = divmod(n, 8)
                    if n >= 6:
                        o = n - 6
                        pe.wait_ge(s(f"xs_{'ba'[o % 2]}"), 8 * L + o // 2 + 1)
                    for i, (_, t) in enumerate(TOK):
                        ins = mm(B[n % 6][:, 0:NT], htok[0:t, i, 128 * m:128 * m + 128],
                                 sel[0:t, i, NT * c:NT * c + NT], start=(i == 0), stop=(i == 2))
                    ins.then_inc(s("gather_mm"), 1)
                pe.wait_ge(s("wsel"), 3 * L + 3)
                for q, (q0, qn) in enumerate(QT):
                    if q >= 2:
                        pe.wait_ge(s("wt"), 5 * L + q - 1)
                    for j, (t0, t) in enumerate(TOK):
                        ins = tr(B[6 + q % 2][0:qn, t0:t0 + t], wsel[0:t, j, q0:q0 + qn], ident[0:t, 0:t])
                    ins.then_inc(s("wt_mm"), 1)
                pe.wait_ge(s("xs_a"), 8 * L + 8)
                pe.wait_ge(s("xs_b"), 8 * L + 8)
                pe.wait_ge(s("table"), L + 1)
                rounds = pe.value_load(table[0:1, ROUNDS * NE + 1:ROUNDS * NE + 2], min_val=1, max_val=ROUNDS)
                with pe.Fori(0, rounds * 16) as i:
                    it = i + base
                    for j in range(2):
                        gw, uw, dw = expert_pages(j)
                        x = xcx[:, j, :].rearrange("p (k c) -> p k c", k=KD)
                        pe.wait_ge(s(f"expert_landed{3 * j}"), (it + 1) * 16)
                        pe.wait_ge(s(f"expert_landed{3 * j + 1}"), (it + 1) * 16)
                        pe.wait_ge(s(f"xcx{j}"), it + (1 + L * (1 - j)))
                        for k in range(KD):
                            mm(B[j][0:CAP, :], x[:, k, :], gw[:, k, :], start=(k == 0), stop=(k == KD - 1))
                            ins = mm(B[j][CAP:P, :], x[:, k, :], uw[:, k, :], start=(k == 0), stop=(k == KD - 1))
                        ins.then_inc(s(f"gu_mm{j}"), 1)
                        pe.wait_ge(s(f"hx{j}"), it + 1)
                        for f in range(MF):
                            ins = mm(B[4 + j][:, CAP * f:CAP * f + CAP], hx[CAP:P, j, 128 * f:128 * f + 128],
                                     ident[CAP:P, CAP:P], start=True, stop=True)
                        ins.then_inc(s(f"ht_tr{j}"), 1)
                        pe.wait_ge(s(f"expert_landed{3 * j + 2}"), (it + 1) * 16)
                        pe.wait_ge(s(f"y_out{j}"), it)
                        pe.wait_ge(s(f"ht{j}"), it + 1)
                        for f in range(MF):
                            for c in range(2):
                                ins = mm(B[2 + j][CAP * c:CAP * c + CAP, :], hxT[:, j, CAP * f:CAP * f + CAP],
                                         dw[:, f, 512 * c:512 * c + 512], start=(f == 0), stop=(f == MF - 1))
                        ins.then_inc(s(f"y_mm{j}"), 1)
                pe.wait_ge(s("yt_landed"), 16 * 5 * (L + 1))
                pe.wait_ge(s("wt"), 5 * L + 5)
                for m in range(KD):
                    if m >= 2:
                        pe.wait_ge(s("moe_add"), 8 * L + m - 1)
                    for q, (q0, qn) in enumerate(QT):
                        ins = mm(B[4 + m % 2][:, 0:NT], ystok[0:qn, q, 128 * m:128 * m + 128], wt[0:qn, q, :],
                                 start=(q == 0), stop=(q == len(QT) - 1))
                    ins.then_inc(s("comb_mm"), 1)
                pe.wait_ge(s("moe_add"), 8 * L + KD)
                return base + rounds * 16

            turns = moe(0, 0)
            norm(2)
            dense("in", 8, 4, 512, KD, lambda k: hT[:, k, :], "in_mm", lambda m: pe.wait_ge(s("gelu"), m + 1))
            pe.wait_ge(s("ws_landed"), 16)
            for g in range(CG):
                ins = tr(B[4 + g // 4][:, 128 * (g % 4):128 * (g % 4) + 128], raw_ws[:, g, :], ident[:])
                if g % 4 == 3:
                    ins.then_inc(s("ws_tr"), 1)
            pe.wait_ge(s("ws_out"), 2)
            pe.wait_ge(s("gelu"), 2 * KI)
            for n in range(12):
                j, c = divmod(n, 4)
                t0, t = TOK[j]
                if n >= 4:
                    pe.wait_ge(s("vtk"), n - 3)
                for i in range(4):
                    ins = tr(B[4 + n % 4][0:t, 128 * i:128 * i + 128], vT[:, 4 * c + i, t0:t0 + t], ident[:])
                ins.then_inc(s("vtok_mm"), 1)
            pe.wait_ge(s("vtk"), 12)
            pe.wait_ge(s("ws_masked"), 1)
            pe.wait_ge(s("rep"), 1)
            mm(B[4][0:NS, 0:CG * SB], rep[0:4, :], wsT[0:4, :, 0:SB], start=True, stop=True).then_inc(s("wsS_mm"), 1)
            pe.wait_ge(s("wsS"), 1)
            pe.wait_ge(s("v_norm"), 3)
            for m in range(KI):
                if m >= 4:
                    pe.wait_ge(s("mixed"), m - 3)
                for j in range(2):
                    mm(B[m % 4][:, 128 * j:128 * j + 128], vtk[:, j, 128 * m:128 * m + 128], wsT[:, m // 2, :],
                       start=True, stop=True)
                mm(B[m % 4][:, 256:NT], vtk[0:NS, 2, 128 * m:128 * m + 128], wsS[0:NS, m // 2, :],
                   start=True, stop=True).then_inc(s("mix_mm"), 1)
            pe.wait_ge(s("mixed"), KI)
            dense("out", 4, 2, 256, KI, lambda k: uT[:, k, :], "out_mm", lambda m: pe.wait_ge(s("out_add"), m + 1))
            pe.wait_ge(s("out_add"), KD)
            moe(1, turns)
            norm(4)
            for n in range(6):
                j, c = divmod(n, 2)
                t0, t = TOK[j]
                for k in range(4):
                    ins = tr(B[n][0:t, 128 * k:128 * k + 128], hT[:, 4 * c + k, t0:t0 + t], ident[:])
                ins.then_inc(s("y_tr"), 1)

        @block.vector
        def _(dve):
            chain = [0]

            def link(ins):
                chain[0] += 1
                ins.then_inc(s("dve_chain"), 1)
                dve.wait_ge(s("dve_chain"), chain[0])

            tt, ts, stt, copy = dve.tensor_tensor, dve.tensor_scalar, dve.scalar_tensor_tensor, dve.tensor_copy

            raws = [
                (vecs[:], B[2][:, 0:192]),
                (wqkv, B[3][:, 0:192].rearrange("p (i m) -> p i m", i=4)),
                (wif[:].rearrange("p t n -> p n t"), B[4][:, 0:384].rearrange("p (n t) -> p n t", n=8)),
                None, None,
                (sample_view_all(xe), B[7][:, 0:384].rearrange("p (m b c) -> p m b c", m=KI, b=NB)),
                (nT[:], B[0][:, 0:128].rearrange("p (i r) -> p i r", i=MH)),
            ]
            for n in range(7):
                dve.wait_ge(s("raw_tr"), n + 1)
                if n == 3:
                    for i in range(2):
                        for g in range(G):
                            ins = copy(wr[:, i, :, G + EPG * g:G + EPG * g + EPG],
                                       B[5][:, :].rearrange("p (e r k) -> p r k e", e=8, r=8)[:, 4 * i + g, :, :])
                elif n == 4:
                    for i in range(2):
                        ins = copy(wr[:, i, :, 0:G],
                                   B[6][:, 0:64].rearrange("p (g i k) -> p i k g", g=4, i=2)[:, i, :, :])
                else:
                    if n == 5:
                        dve.wait_ge(s("consts"), 5)
                    ins = copy(*raws[n])
                ins.then_inc(s("raw_out"), 1)
            dve.wait_ge(s("raw_out"), 7)

            def norm(n):
                dve.wait_ge(s("std"), n + 1)
                link(dve.reciprocal(rstd, stdv))
                for k in range(KD):
                    stt(hT[:, k, :], xT[:, k, :], vecs[:, NORM[n] + k:NORM[n] + k + 1], rstd, ALU.mult, ALU.mult) \
                        .then_inc(s("h_norm"), 1)

            norm(0)
            W = XE - 3
            for m in range(KI):
                dve.wait_ge(s("xm_out"), 3 * m + 3)
                if m >= 2:
                    dve.wait_ge(s("xc"), 2 * m - 2)
                y = ctmp[:, m % 2, 0:W]
                link(ts(y, xe[:, m, 0:W], vec("mlstm_conv_w", m), vec("mlstm_conv_b", m), ALU.mult, ALU.add))
                for i in range(1, 4):
                    ins = stt(y, xe[:, m, i:i + W], vec("mlstm_conv_w", KI * i + m), y, ALU.mult, ALU.add)
                    if i < 3:
                        link(ins)
                ins.then_inc(s("conv"), 1)
            for m in range(KI):
                dve.wait_ge(s("qkv_mm"), m + 1)
                copy(kT[:, m, :], B[2 + m % 2][:, 0:NT]).then_inc(s("k_out"), 1)
            dve.wait_ge(s("xc"), 2 * KI)
            copy(cv27[:, :, 0:3], xe[:, :, NPROMPT:NPROMPT + 3]).then_inc(s("cv27"), 1)
            copy(cv27[:, :, 3:27].rearrange("p m (b c) -> p m b c", c=3), sample_view_all(xe, 4)).then_inc(s("cv27"), 1)
            for n in range(4):
                dve.wait_ge(s("cv_tr"), n + 1)
                copy(cvout[0:27, 512 * n:512 * n + 512], B[4 + n % 2][0:27, :]).then_inc(s("cv_out"), 1)
            gi, gf, tmp, lf, ones4, fs, a, ap = (gt[0:4, n, :] for n in (1, 2, 3, 4, 5, 6, 7, 8))
            radd = gt[0:4, 9, :]
            dve.wait_ge(s("gates_act"), 1)
            link(dve.memset(ones4, 1.0))
            link(dve.memset(radd, 0.0))
            link(dve.memset(gt[0:4, 5, NPROMPT:NT:SB], 0.0))
            link(dve.memset(gt[0:4, 9, NPROMPT:NT:SB], -1.0e38))
            dve.wait_ge(s("gates_act"), 3)
            link(ts(tmp, gf, -1.0, None, ALU.mult))
            tt(tmp, tmp, gf, ALU.max).then_inc(s("gates_dve"), 1)
            dve.wait_ge(s("gates_act"), 5)
            link(stt(lf, gf, 0.0, tmp, ALU.min, ALU.subtract))
            link(dve.tensor_tensor_scan(fs, ones4, lf, 0.0, ALU.mult, ALU.add))
            link(tt(a, gi, fs, ALU.subtract))
            link(copy(ap, a))
            link(tt(gt[0:4, 8, NPROMPT:NT:SB], gt[0:4, 7, NPROMPT:NT:SB], m0[:], ALU.max))
            Am = catA[:, 0:NT]
            link(dve.tensor_tensor_scan(Am, radd, ap, NEG, ALU.add, ALU.max))
            bs = "p (b s) -> p b s"
            Amb = catA[:, NPROMPT:NT].rearrange(bs, s=SB)
            Alast = catA[:, NPROMPT + 3:NT:SB]
            dve.wait_ge(s("consts"), 7)
            link(tt(catA[:, NT:NT + 8], m0[:], Alast, ALU.subtract))
            link(tt(catA[:, NT + 8:NT + 8 + NS].rearrange(bs, s=SB), m0[:].unsqueeze(2).to_broadcast([4, NB, SB]), Amb,
                    ALU.subtract))
            link(copy(rows[0:4, :], a))
            link(tt(rows[32:36, :], fs, Am, ALU.add))
            link(ts(rows[96:100, 0:NPROMPT], gt[0:4, 7, 0:NPROMPT], catA[:, NPROMPT - 1:NPROMPT], None, ALU.subtract))
            tt(rows[96:100, NPROMPT:NT].rearrange(bs, s=SB), gt[0:4, 7, NPROMPT:NT].rearrange(bs, s=SB),
               Alast.unsqueeze(2).to_broadcast([4, NB, SB]), ALU.subtract).then_inc(s("gates_dve"), 1)
            dve.wait_ge(s("tm"), 10)

            dve.wait_ge(s("cv_stored"), 32)
            for half in range(2):
                copy(spread[0:NS, half, :].rearrange("p (b c s) -> p b c s", b=4, c=8),
                     ident[0:NS, 16 * half:16 * half + 16].rearrange("p (b s) -> p b s", b=4).unsqueeze(2)
                     .to_broadcast([NS, 4, 8, 4]))
            dve.tensor_reduce(fold, ident[:].rearrange("p (i s) -> p s i", i=4), AX.X, ALU.add)
            link(dve.tensor_reduce(prod, ident[:].rearrange("p (b c s) -> p c b s", b=4, c=8), AX.XY, ALU.add))
            link(dve.tensor_reduce(notp[:, 0:1], prod[:, 3:8], AX.X, ALU.add))
            link(dve.tensor_reduce(notp[:, 1:2], prod[:, 6:8], AX.X, ALU.add))
            link(dve.tensor_reduce(notp[:, 3:4], prod[:, 2:6:3], AX.X, ALU.add))
            link(dve.tensor_reduce(notp[:, 2:3], prod[:, 1:8:3], AX.X, ALU.add))
            link(tt(notp[:, 2:3], notp[:, 2:3], notp[:, 3:4], ALU.add))
            ts(notp, notp, -1.0, None, ALU.mult).then_inc(s("part_masks"), 1)
            dve.wait_ge(s("part_masks"), 1)
            for h in range(H):
                dve.wait_ge(s("kv_mm"), 2 * h + 1)
                if h > 0:
                    dve.wait_ge(s("num_mm"), 2 * h)
                for j, (_, n) in enumerate(TOK):
                    ts(wk[0:n, j, :], B[1 + j][0:n, :], tm[0:n, j, 8 + h:9 + h], KSCALE, ALU.mult, ALU.mult) \
                        .then_inc(s("wk"), 1)
                for n in range(4):
                    dst = (wk8, v8)[n // 2]
                    f = notp[:, 2 * (n // 2):2 * (n // 2) + 2]
                    y, z = y16[:, n % 2, :], z1[:, n % 2, :]
                    dve.wait_ge(s("y1"), 4 * h + n + 1)
                    stt(z, y, f[:, 0:1], B[1 + n][:, :], ALU.mult, ALU.add).then_inc(s("z1"), 1)
                    dve.wait_ge(s("z1"), 4 * h + n + 1)
                    link(copy(y, z))
                    stt(dst[:, n % 2, :], y, f[:, 1:2], z, ALU.mult, ALU.add).then_inc(s("parts"), 1)
                    dve.wait_ge(s("parts"), 4 * h + n + 1)
                dve.wait_ge(s("bc_exp"), 2 * h + 2)
                dve.wait_ge(s("qz_zero"), 1)
                qi = qz[:, :, :].rearrange("p i (b x) -> p i b x", x=36)[:, :, :, 0:SB]
                q = qT[:, MH * h:MH * h + MH, NPROMPT:NT].rearrange("p i (b s) -> p i b s", s=SB)
                ib = ibc[:, h, :].rearrange(bs, s=SB)
                for i in range(MH):
                    ins = tt(qi[:, i], q[:, i], ib, ALU.mult)
                ins.then_inc(s("qz"), 1)
                dve.wait_ge(s("st_mm"), h + 1)
                dve.wait_ge(s("e_masked"), 3 * h + 3)
                for p, c0, c1 in ((P, 0, 256), (P, 256, 384), (NS, 384, 416)):
                    stt(stw[0:p, c0:c1], B[7][0:p, c0:c1], KSCALE, ew[0:p, c0:c1], ALU.mult, ALU.mult) \
                        .then_inc(s("stw"), 1)
                dve.wait_ge(s("stw"), 3 * h + 3)
                dve.wait_ge(s("qz"), 2 * h + 1)
                npr = ew[:, 0:128].rearrange("p (i b s) -> p i b s", i=MH, s=SB)
                for i in range(MH):
                    ins = tt(npr[:, i], qi[:, i],
                             nT[:, i, h:32:H].unsqueeze(2).to_broadcast([P, NB, SB]), ALU.mult)
                ins.then_inc(s("qz"), 1)
                dve.wait_ge(s("num_mm"), 2 * h + 1)
                for j in range(2):
                    link(ts(dden[:, j:j + 1], B[3][:, j:j + 1], -1.0, None, ALU.mult))
                    link(stt(dden[:, j:j + 1], dden[:, j:j + 1], tm[:, j, 4 + h:5 + h], B[3][:, j:j + 1],
                             ALU.max, ALU.max))
                dve.reciprocal(rden[:, 0:2], dden[:, 0:2]).then_inc(s("rden"), 1)
                dve.wait_ge(s("ns_mm"), h + 1)
                dve.wait_ge(s(f"n_landed{h % 2}"), 16 * (h // 2 + 1))
                stt(nrow[:, h % 2, :], nrow[:, h % 2, :], decn[:, h:h + 1], B[7][0:NB, :], ALU.mult, ALU.add) \
                    .then_inc(s("ns_out"), 1)
                for b in range(NB):
                    cpage = page("C", 4 * h + b // 2).rearrange("p (c v) -> p c v", v=DH)
                    for i in range(MH):
                        c = cpage[:, MH * (b % 2) + i, :]
                        n = (NB * h + b) * MH + i
                        dve.wait_ge(s("c_mm"), n + 1)
                        stt(c, c, decb[:, h, b:b + 1], B[UPD[i]][:, :], ALU.mult, ALU.add).then_inc(s("c_new"), 1)
                dve.wait_ge(s("num_mm"), 2 * h + 2)
                link(ts(dden[0:NS, 2:3], B[3][0:NS, 2:3], -1.0, None, ALU.mult))
                link(stt(dden[0:NS, 2:3], dden[0:NS, 2:3], tm[0:NS, 2, 4 + h:5 + h], B[3][0:NS, 2:3],
                         ALU.max, ALU.max))
                dve.reciprocal(rden[0:NS, 2:3], dden[0:NS, 2:3]).then_inc(s("rden"), 1)
            def hh(h, j):
                return hhp[h][:, j, :] if j < 2 else hhs[h][0:NS]

            dve.wait_ge(s("hh"), 3 * H)
            mean = rstd[:, 0:12]
            for h in range(H):
                for j, (_, n) in enumerate(TOK):
                    c = 3 * h + j
                    link(dve.bn_stats(lnst[0:n], hh(h, j)))
                    link(dve.bn_aggr(stdv[0:n, 2 * c:2 * c + 2], lnst[0:n]))
                    copy(mvsd[0:n, c:c + 1], stdv[0:n, 2 * c + 1:2 * c + 2]).then_inc(s("mv"), 1)
            dve.wait_ge(s("hsd"), 1)
            link(dve.reciprocal(mean, mvsd))
            for h in range(H):
                for j, (_, n) in enumerate(TOK):
                    c = 3 * h + j
                    ts(hh(h, j), hh(h, j), stdv[0:n, 2 * c:2 * c + 1], mean[0:n, c:c + 1], ALU.subtract, ALU.mult) \
                        .then_inc(s("hn"), 1)
            for m in range(KI):
                dve.wait_ge(s("hn_tr"), m + 1)
                dve.wait_ge(s("zs"), m + 1)
                t = (stdv, rstd)[m % 2]
                if m < 2:
                    dve.wait_ge(s("hn"), 3 * H)
                else:
                    dve.wait_ge(s("y_mix"), m - 1)
                ts(t, B[4 + m % 2][:, 0:NT], vec("mlstm_hn_w", m), None, ALU.mult).then_inc(s("y_in"), 1)
                dve.wait_ge(s("y_in"), m + 1)
                link(stt(t, xc[:, m, :], vec("mlstm_skip", m), t, ALU.mult, ALU.add))
                tt(xc[:, m, :], t, zs[:, m, :], ALU.mult).then_inc(s("y_mix"), 1)
            for m in range(KD):
                dve.wait_ge(s("down_mm"), m + 1)
                tt(xT[:, m, :], xT[:, m, :], B[m % 4][:, 0:NT], ALU.add).then_inc(s("down_add"), 1)

            def moe(L, base):
                norm(1 + 2 * L)

                def v3(o, n):
                    return rt[:, o:o + 3 * n].rearrange("p (j e) -> p j e", j=3)

                def bc(t, n):
                    return t.unsqueeze(2).to_broadcast([P, 3, n])

                def bj(t, n):
                    return t.unsqueeze(1).to_broadcast([P, 3, n])

                M, M0, M1 = v3(0, NE), v3(96, NE), v3(192, NE)
                lg, ge = v3(300, G), v3(320, G)
                gmax, gsum = rt[:, 312:315], rt[:, 332:335]
                diff, ediff = rt[:, 340:343], rt[:, 343:346]
                t1, t2 = rt[:, 346:349], rt[:, 349:352]
                lt = v3(400, 36)
                gm = v3(510, G)
                key = v3(530, NE)
                le = v3(630, NE)
                rank = v3(730, NE)
                nrep = rt[:, 830:990].rearrange("p (r e) -> p r e", r=ROUNDS)
                off = rt[:, 990:1150].rearrange("p (r e) -> p r e", r=ROUNDS)
                one160 = rt[:, 1150:1310]
                doff = rt[:, 1310:1470].rearrange("p (r e) -> p r e", r=ROUNDS)
                cnt = rt[:, 1470:1502]
                thr = rt[:, 1502:1507]
                pos = v3(1510, NE)
                tmp3 = v3(1610, NE)
                mx = rt[:, 1720:1721]
                rmax, rmin = rt[:, 1722:1725], rt[:, 1726:1729]

                dve.wait_ge(s("consts"), 6)
                link(dve.memset(rt, 0.0))
                dve.wait_ge(s("iota"), 2 * L + 2)
                dve.wait_ge(s("router_pe"), 2 * L + 1)
                for j, (_, n) in enumerate(TOK):
                    link(tt(lt[0:n, j, :], B[6][0:n, 36 * j:36 * j + 36], rbias[0:n, L, :], ALU.add))

                def first_max(out, val, vmax, idx, n):
                    link(dve.tensor_reduce(vmax, val, AX.X, ALU.max))
                    link(tt(out, val, bc(vmax, n), ALU.is_equal))
                    k = key[:, :, 0:n]
                    link(stt(k, out, -EARLIER, idx, ALU.mult, ALU.add))
                    link(dve.tensor_reduce(rmin, k, AX.X, ALU.min))
                    link(tt(out, k, bc(rmin, n), ALU.is_equal))

                first_max(gm, lt[:, :, 0:G], gmax, bj(iota32[:, 0:G], G), G)
                tt(lg, lt[:, :, 0:G], bc(gmax, G), ALU.subtract).then_inc(s("router_dve"), 1)
                link(ts(gm, gm, 1.0, 1.0e30, ALU.subtract, ALU.mult))
                for g in range(G):
                    link(tt(le[:, :, EPG * g:EPG * g + EPG], lt[:, :, G + EPG * g:G + EPG * g + EPG],
                            gm[:, :, g:g + 1].to_broadcast([P, 3, EPG]), ALU.add))
                idx32 = bj(iota32, NE)
                first_max(M0, le, rmax, idx32, NE)
                link(stt(le, M0, -2.0e30, le, ALU.mult, ALU.add))
                first_max(M1, le, t1, idx32, NE)
                tt(diff, t1, rmax, ALU.subtract).then_inc(s("router_dve"), 1)
                tt(M, M0, M1, ALU.add).then_inc(s("router_dve"), 1)
                dve.wait_ge(s("router_act"), 2 * L + 1)
                link(dve.tensor_reduce(gsum, ge, AX.X, ALU.add))
                dve.wait_ge(s("router_act"), 2 * L + 2)
                link(ts(t2, ediff, 1.0, None, ALU.add))
                link(tt(t2, t2, gsum, ALU.mult))
                if L == 1:
                    dve.wait_ge(s("wsel"), 3)
                link(dve.reciprocal(slotw[:, 6:9], t2))
                link(tt(slotw[:, 9:12], slotw[:, 6:9], ediff, ALU.mult))
                dve.wait_ge(s("router_pe"), 2 * L + 2)
                link(copy(cnt, B[7][:, 96:128]))
                for j, (_, n) in enumerate(TOK):
                    link(copy(rank[0:n, j, :], B[7][0:n, 32 * j:32 * j + 32]))
                for r in range(ROUNDS):
                    link(ts(nrep[:, r, :], cnt, float(CAP * r), 0.0, ALU.subtract, ALU.max))
                link(ts(nrep, nrep, float(CAP), None, ALU.min))
                link(dve.memset(one160, 1.0))
                nflat, oflat = rt[:, 830:990], rt[:, 990:1150]
                link(dve.tensor_tensor_scan(oflat, one160, nflat, 0.0, ALU.mult, ALU.add))
                link(tt(oflat, oflat, nflat, ALU.subtract))
                link(dve.tensor_reduce(mx, cnt, AX.X, ALU.max))
                for r in range(ROUNDS):
                    link(ts(thr[:, r:r + 1], mx, float(CAP * r), None, ALU.is_gt))
                link(dve.tensor_reduce(rt[:, 1721:1722], thr, AX.X, ALU.add))
                if L == 1:
                    dve.wait_ge(s("moe_add"), KD)
                link(dve.memset(table[:, ROUNDS * NE:ROUNDS * NE + 1], 0))
                link(copy(table[:, 0:ROUNDS * NE], rt[0:1, 990:1150]))
                copy(table[:, ROUNDS * NE + 1:ROUNDS * NE + 2], rt[0:1, 1721:1722]).then_inc(s("table"), 1)
                link(tt(doff[:, 1:ROUNDS, :], off[:, 1:ROUNDS, :], off[:, 0:ROUNDS - 1, :], ALU.subtract))
                link(ts(doff[:, 1:ROUNDS, :], doff[:, 1:ROUNDS, :], float(CAP), None, ALU.subtract))
                link(tt(pos, rank, bj(off[:, 0, :], NE), ALU.add))
                for r in range(1, ROUNDS):
                    link(stt(tmp3, rank, float(CAP * r), bj(doff[:, r, :], NE), ALU.is_ge, ALU.mult))
                    link(tt(pos, pos, tmp3, ALU.add))
                for n, m in enumerate((M0, M1)):
                    link(tt(tmp3, pos, m, ALU.mult))
                    dve.tensor_reduce(slotw[:, 3 * n:3 * n + 3], tmp3, AX.X, ALU.add).then_inc(s("slots"), 1)
                    dve.wait_ge(s("slots"), 2 * L + n + 1)
                for j, (_, n) in enumerate(TOK):
                    link(ts(sel[0:n, j, :], iota[0:n], slotw[0:n, j:j + 1], None, ALU.is_equal))
                    stt(sel[0:n, j, :], iota[0:n], slotw[0:n, 3 + j:4 + j], sel[0:n, j, :], ALU.is_equal, ALU.add) \
                        .then_inc(s("sel"), 1)
                for n in range(0, 16, 2):
                    c, m = divmod(n, 8)
                    dve.wait_ge(s("gather_mm"), 16 * L + n + 1)
                    copy(xsT[:, m, NT * c:NT * c + NT], B[n % 6][:, 0:NT]).then_inc(s("xs_b"), 1)
                for q, (_, qn) in enumerate(QT):
                    dve.wait_ge(s("wt_mm"), 5 * L + q + 1)
                    copy(wt[0:qn, q, :], B[6 + q % 2][0:qn, 0:NT]).then_inc(s("wt"), 1)
                dve.wait_ge(s("xs_a"), 8 * L + 8)
                dve.wait_ge(s("xs_b"), 8 * L + 8)
                dve.wait_ge(s("xs_pad"), L + 1)
                dve.wait_ge(s("table"), L + 1)
                rounds = dve.value_load(table[0:1, ROUNDS * NE + 1:ROUNDS * NE + 2], min_val=1, max_val=ROUNDS)

                def fetch(n, j):
                    o = dve.value_load(table[0:1, bass.ds(n, 1)], min_val=0, max_val=NSLOT)
                    copy(xcx[:, j, :].rearrange("p (k c) -> p k c", k=KD), xsT[:, :, bass.ds(o, CAP)]) \
                        .then_inc(s(f"xcx{j}"), 1)

                fetch(0, 0)
                with dve.Fori(0, rounds * 16) as i:
                    it = i + base
                    for j in range(2):
                        dve.wait_ge(s(f"gu_mm{1 - j}"), it + j)
                        fetch(2 * i + (j + 1), 1 - j)
                        dve.wait_ge(s(f"sg{j}"), it + 1)
                        tt(hx[CAP:P, j, :], sg[CAP:P, j, :], B[j][CAP:P, :], ALU.mult).then_inc(s(f"hx{j}"), 1)
                        dve.wait_ge(s(f"ht_tr{j}"), it + 1)
                        copy(hxT[:, j, :], B[4 + j][:, 0:MF * CAP]).then_inc(s(f"ht{j}"), 1)
                for m in range(KD):
                    dve.wait_ge(s("comb_mm"), 8 * L + m + 1)
                    tt(xT[:, m, :], xT[:, m, :], B[4 + m % 2][:, 0:NT], ALU.add).then_inc(s("moe_add"), 1)
                return base + rounds * 16

            turns = moe(0, 0)
            norm(2)
            for n in range(2):
                dve.wait_ge(s("ws_tr"), n + 1)
                copy(wsT[:, 4 * n:4 * n + 4, :], B[4 + n][:, :].rearrange("p (g t) -> p g t", g=4)) \
                    .then_inc(s("ws_out"), 1)
            dve.wait_ge(s("consts"), 1)
            copy(rep[0:4, :].rearrange("p (b s) -> p b s", s=SB), ident[0:4, 0:4].unsqueeze(1).to_broadcast([4, NB, SB])) \
                .then_inc(s("rep"), 1)
            for n in range(12):
                j, c = divmod(n, 4)
                t = TOK[j][1]
                dve.wait_ge(s("vtok_mm"), n + 1)
                copy(vtk[0:t, j, 512 * c:512 * c + 512], B[4 + n % 4][0:t, :]).then_inc(s("vtk"), 1)
                dve.wait_ge(s("vtk"), n + 1)
                link(dve.bn_stats(bnst[0:t, j, 6 * c:6 * c + 6], vtk[0:t, j, 512 * c:512 * c + 512]))
                if c == 3:
                    dve.bn_aggr(mvc[0:t, j, :], bnst[0:t, j, :]).then_inc(s("vstat"), 1)
            dve.wait_ge(s("wsS_mm"), 1)
            tt(wsS[0:NS].rearrange("p g (b t) -> p g b t", t=SB),
               B[4][0:NS, 0:CG * SB].rearrange("p (g t) -> p g t", t=SB).unsqueeze(2).to_broadcast([NS, CG, NB, SB]),
               bmask[0:NS, 0:NB].unsqueeze(1).unsqueeze(3).to_broadcast([NS, CG, NB, SB]), ALU.mult) \
                .then_inc(s("wsS"), 1)
            dve.wait_ge(s("ln_landed"), 32)
            for j, (_, n) in enumerate(TOK):
                dve.wait_ge(s("vsd"), j + 1)
                link(dve.reciprocal(mvc[0:n, j, 1:2], mvc[0:n, j, 1:2]))
                link(ts(vtk[0:n, j, :], vtk[0:n, j, :], mvc[0:n, j, 0:1], mvc[0:n, j, 1:2], ALU.subtract, ALU.mult))
                link(tt(vtk[0:n, j, :], vtk[0:n, j, :], lnwb[0:n, 0, :], ALU.mult))
                tt(vtk[0:n, j, :], vtk[0:n, j, :], lnwb[0:n, 1, :], ALU.add).then_inc(s("v_norm"), 1)
            dve.wait_ge(s("bs_landed"), 16)
            for m in range(KI):
                g = m // 2
                dve.wait_ge(s("mix_mm"), m + 1)
                link(tt(mixt[:, 0:256].rearrange("p (j t) -> p j t", j=2), B[m % 4][:, 0:256].rearrange("p (j t) -> p j t", j=2),
                        bsb[:, g, :].unsqueeze(1).to_broadcast([P, 2, P]), ALU.add))
                link(tt(mixt[:, 256:NT].rearrange(bs, s=SB), B[m % 4][:, 256:NT].rearrange(bs, s=SB),
                        bsb[:, g, 0:SB].unsqueeze(1).to_broadcast([P, NB, SB]), ALU.add))
                ins = tt(uT[:, m, :], uT[:, m, :], mixt, ALU.mult)
                ins.then_inc(s("mixed"), 1)
                dve.wait_ge(s("mixed"), m + 1)
            for m in range(KD):
                dve.wait_ge(s("out_mm"), m + 1)
                stt(xT[:, m, :], B[m % 4][:, 0:NT], vec("cmlp_b_out", m), xT[:, m, :], ALU.add, ALU.add) \
                    .then_inc(s("out_add"), 1)
            moe(1, turns)
            norm(4)


def sample_view_all(xe, first=0):
    return xe[:, :, XS:XE].rearrange("p m (b x) -> p m b x", x=7)[:, :, :, first:first + 3]


_INS = ["x_prompt", "x_sample", "state_mlstm_C", "state_mlstm_n", "state_mlstm_m", "state_mlstm_conv",
        "norm_mix", "norm_ffn", "norm_final", "mlstm_w_up", "mlstm_conv_w", "mlstm_conv_b", "mlstm_w_q", "mlstm_w_k",
        "mlstm_w_v", "mlstm_w_ig", "mlstm_b_ig", "mlstm_w_fg", "mlstm_b_fg", "mlstm_skip", "mlstm_hn_w",
        "mlstm_w_down", "cmlp_w_in", "cmlp_b_in", "cmlp_ln_w", "cmlp_ln_b", "cmlp_w_s", "cmlp_b_s", "cmlp_w_out",
        "cmlp_b_out", "moe_w_rg", "moe_b_rg", "moe_w_re", "moe_b_re", "moe_w_gate", "moe_w_up", "moe_w_down"]
_OUTS = [("y_p", (1, NPROMPT, D)), ("y_s", (NB, SB, D)), ("C_p", (1, 1, H, DH, DH)), ("n_p", (1, 1, H, DH)),
         ("m_p", (1, 1, H)), ("conv_p", (1, 1, 3, INNER)), ("C_s", (1, NB, H, DH, DH)), ("n_s", (1, NB, H, DH)),
         ("m_s", (1, NB, H)), ("conv_s", (1, NB, 3, INNER)), ("v_s", (1, NB, SB, INNER))]


def kernel(**inputs):
    import numpy as _np
    import concourse.bacc as _bacc
    from concourse import mybir as _mybir
    from concourse.bass_utils import run_bass_kernel_spmd as _run

    nc = _bacc.Bacc("TRN2", target_bir_lowering=False, num_devices=1)
    arrays, ins, outs = {}, {}, {}
    for name in _INS:
        a = _np.ascontiguousarray(inputs[name])
        arrays[f"in_{name}"] = a
        ins[name] = nc.dram_tensor(f"in_{name}", a.shape, _mybir.dt.from_np(a.dtype), kind="ExternalInput").ap()
    for name, shape in _OUTS:
        outs[name] = nc.dram_tensor(f"out_{name}", shape, F32, kind="ExternalOutput").ap()
    build(nc, ins, outs)
    r = _run(nc, [arrays], core_ids=[0])
    return tuple(r.results[0][f"out_{name}"] for name, _ in _OUTS)
```

```python
from contextlib import ExitStack

import concourse.bass as bass
from concourse import mybir

F32 = mybir.dt.float32
BF16 = mybir.dt.bfloat16
I32 = mybir.dt.int32
ALU = mybir.AluOpType
ACT = mybir.ActivationFunctionType
AX = mybir.AxisListType

P = 128
D = 1024
KD = D // P
NPROMPT = 256
NB = 8
SB = 4
NS = NB * SB
NT = NPROMPT + NS
TOK = [(0, 128), (128, 128), (256, NS)]
INNER = 2048
KI = INNER // P
H = 4
DH = INNER // H
MH = DH // P
XE = 3 + NPROMPT + NB * 7
XS = 3 + NPROMPT
KSCALE = DH ** -0.5
G = 4
EPG = 8
NE = G * EPG
F = 512
MF = F // P
CAP = 64
ROUNDS = -(-NT // CAP)
NSLOT = 2 * NT
SLOTS = NSLOT + CAP
CG = 8
PAGE = 4096
RING = 6
NEG = -1.0e30
ZLAG = 9
UPD = (5, 6, 7, 0)
EARLIER = 1024.0


def build(nc, A, O):
    with ExitStack() as ctx:
        def sb(name, shape, dt=F32):
            return ctx.enter_context(nc.sbuf_tensor(name, shape, dt))

        sems = {}

        def s(name):
            if name not in sems:
                sems[name] = ctx.enter_context(nc.semaphore("s_" + name))
            return sems[name]

        def at(t, off, *dims):
            n = 1
            for d in dims:
                n *= d
            v = t[:, off:off + n]
            if len(dims) == 1:
                return v
            if len(dims) == 2:
                return v.rearrange("p (a b) -> p a b", b=dims[1])
            return v.rearrange("p (a b c) -> p a b c", b=dims[1], c=dims[2])

        B = [ctx.enter_context(nc.psum_tensor(f"bank{i}", [P, 512], F32)) for i in range(8)]
        xT = sb("xT", [P, KD, NT])
        hT = sb("hT", [P, KD, NT])
        ident = sb("ident", [P, P])
        ones = sb("ones", [P, P])
        before = sb("before", [P, P])
        bmask = sb("bmask", [P, 32])
        vecs = sb("vecs", [P, 192])
        wif = sb("wif", [P, 48, 8])
        wr = sb("wr", [P, 2, KD, 36])
        rbias = sb("rbias", [P, 2, 36])
        scratch = sb("scratch", [P, 2 * NT])
        stdv, rstd = scratch[:, 0:NT], scratch[:, NT:2 * NT]
        xms = at(scratch, 0, KI, NS)
        nT = sb("nT", [P, MH, 32])
        rows = sb("rows", [P, NT])
        catA = sb("catA", [4, NT + 8 + NS])
        tm = sb("tm", [P, 3, 12])
        decb = sb("decb", [P, H, NB])
        ibc = sb("ibc", [P, H, NS])
        decn = sb("decn", [NB, H])
        m0 = sb("m0", [4, NB])
        gb = sb("gb", [4, 2])
        nrow = sb("nrow", [NB, 2, DH])
        nst = sb("nst", [1, DH])
        small = sb("small", [P, 64])
        eps6, eps5 = small[:, 0:1], small[:, 1:2]
        rden = small[:, 2:5]
        dden = small[:, 5:8]
        slotw = small[:, 8:20]
        mvsd = small[:, 20:32]
        gfold = small[:, 50:58]
        placew = small[:, 38:50]
        lnst = small[:, 32:38]
        table = sb("table", [1, ROUNDS * NE + 8], I32)
        arena = sb("arena", [P, 18864])
        ring = sb("ring", [P, RING, PAGE])

        xe = at(arena, 0, KI, XE)
        xc = at(arena, 5040, KI, NT)
        qT = at(arena, 9648, KI, NT)
        kT = at(arena, 14256, KI, NT)
        hhp = [at(arena, 14256 + h * MH * NT, 2, DH) for h in range(H)]
        hhs = [at(arena, 9648 + h * MH * NT, DH) for h in range(H)]
        zs = at(arena, 0, KI, NT)
        xtok = at(arena, 9648, 3, D)
        raw_re = at(arena, 12720, 1024)
        raw_rg = at(arena, 13744, 512)
        raw_if = at(arena, 14256, 2, 512)
        raw_qkv = at(arena, 15280, 512)
        raw_vec = at(arena, 15792, 2, P)
        raw_conv = at(arena, 16048, INNER)
        high = ring[:, 3:6, :].rearrange("p a b -> p (a b)")
        bd = at(high, 0, 3, KI, P)
        z1 = at(high, 0, 2, DH)
        snum = at(high, 1024, DH)
        wk8 = at(high, 2048, 512).bitcast(BF16).rearrange("p (a d) -> p a d", a=2)
        v8 = at(high, 2560, 512).bitcast(BF16).rearrange("p (a d) -> p a d", a=2)
        y16 = at(high, 3072, 512).bitcast(BF16).rearrange("p (a d) -> p a d", a=2)
        spread = at(high, 3584, 2, P)
        fold = at(high, 3840, NS)
        prod = at(high, 3872, 8)
        notp = at(high, 3880, 4)
        cvout = at(high, 0, INNER)
        vtok = at(high, 6144, 3, DH)
        wk = at(high, 7680, 3, DH)
        gt = at(high, 6144, 10, NT)
        stw = at(high, 9216, 416)
        ew = at(high, 9632, 416)
        ctmp = at(high, 9216, 2, 315)
        cv27 = at(high, 9216, KI, 27)
        qz = at(high, 10048, MH, NT)
        vtr = at(high, 10048, 2, NT)
        wqkv = at(high, 10048 + 576, 4, 48)
        nraw = at(high, 11200, 512)
        cst = at(high, 11200, 2, DH)
        xsT = at(arena, 0, KD, SLOTS)
        htok = at(arena, 5120, 3, D)
        sg = at(arena, 5120, 2, F)
        hx = at(arena, 6144, 2, F)
        ysb = at(arena, 7168, D)
        rt = at(arena, 8192, 2048)
        sel = at(arena, 10240, 3, NSLOT)
        tokrow = at(arena, 11968, 4, NT)
        wpart = at(arena, 13120, NT)
        wpair = at(arena, 13408, NT)
        xcx = at(arena, 13696, 2, KD * CAP)
        hxT = at(arena, 14720, 2, MF * CAP)
        iota = at(arena, 15744, NSLOT)
        iota32 = at(arena, 16320, NE)
        rowplace = at(arena, 16352, ROUNDS * NE // 2)
        uT = at(arena, 0, KI, NT)
        vT = at(arena, 4608, KI, NT)
        lnwb = at(arena, 4608, 2, INNER)
        vtk = at(arena, 9216, 3, INNER)
        raw_ws = at(arena, 9216, CG, P)
        wsT = at(arena, 15360, CG, P)
        bsb = at(arena, 16384, CG, P)
        wsS = at(arena, 17408, CG, NS)
        rep = at(arena, 17664, 32)
        mixt = at(arena, 17696, NT)
        bnst = at(arena, 17984, 3, 4 * 6)
        mvc = at(arena, 18056, 3, 2)
        ytok = at(arena, 0, 3, D)

        V = {}
        vec_rows = [("norm_mix", 16), ("norm_ffn", 16), ("norm_final", 8), ("mlstm_conv_w", 64), ("mlstm_conv_b", 16),
                    ("cmlp_b_out", 8), ("mlstm_skip", 16), ("mlstm_hn_w", 16), ("cmlp_b_in", 32)]
        c = 0
        for name, n in vec_rows:
            V[name] = c
            c += n

        def vec(name, k):
            return vecs[:, V[name] + k:V[name] + k + 1]

        NORM = [V["norm_mix"], V["norm_ffn"], V["norm_mix"] + 8, V["norm_ffn"] + 8, V["norm_final"]]

        place = {}
        count = [0] * RING
        for key, slots in (("up", [0, 1, 2, 0]), ("C", [(4 + p) % 3 for p in range(16)]), ("z", [2, 0, 1, 3]),
                           ("down", [4, 5, 3, 4]), ("in", [0, 1, 2, 3, 4, 5, 0, 1]), ("out", [2, 3, 4, 5])):
            for j, slot in enumerate(slots):
                count[slot] += 2 if key == "C" else 1
                place[key, j] = (slot, 16 * count[slot])

        def page(key, j):
            return ring[:, place[key, j][0], :]

        def landed(eng, key, j):
            slot, n = place[key, j]
            eng.wait_ge(s(f"page_landed{slot}"), n)

        def expert_pages(j):
            return (ring[:, 2 * j, :].rearrange("p (k f) -> p k f", k=KD),
                    ring[:, 2 * j + 1, :].rearrange("p (k f) -> p k f", k=KD),
                    ring[:, 4 + j, :].rearrange("p (k f) -> p k f", k=MF))

        def sample_view(t):
            return t[:, XS:XE].rearrange("p (b x) -> p b x", x=7)

        block = ctx.enter_context(nc.Block())

        @block.sync
        def _(sp):
            def load(key, j, src, dst=None):
                slot, _ = place[key, j]
                sp.dma_start(page(key, j) if dst is None else dst, src).then_inc(s(f"page_landed{slot}"), 16)

            w_up = A["mlstm_w_up"][0].rearrange("(k p) n -> p k n", p=P)
            w_dn = A["mlstm_w_down"][0].rearrange("(k p) n -> p k n", p=P)
            w_in = A["cmlp_w_in"][0].rearrange("(k p) n -> p k n", p=P)
            w_out = A["cmlp_w_out"][0].rearrange("(k p) n -> p k n", p=P)

            def k8(v):
                return v.rearrange("p (k n) -> p k n", k=KD)

            def k16(v):
                return v.rearrange("p (k n) -> p k n", k=KI)

            def state(t, p, n):
                h, b = p // 4, 2 * (p % 4) + n
                return t[0, b, h].rearrange("(i p) v -> p i v", p=P)

            def cview(p, n):
                return page("C", p)[:, 2048 * n:2048 * n + 2048].rearrange("p (i v) -> p i v", v=DH)

            def load_state(p):
                for n in range(2):
                    load("C", p, state(A["state_mlstm_C"], p, n), cview(p, n))

            for j, (t0, n) in enumerate(TOK):
                src = A["x_prompt"][0, t0:t0 + n, :] if j < 2 else A["x_sample"].rearrange("b s n -> (b s) n")
                sp.dma_start(xtok[0:n, j, :], src).then_inc(s("x_landed"), 16)
            def load_z(j):
                load("z", j, w_up[:, :, 2048 + 512 * j:2560 + 512 * j], k8(page("z", j)))

            for j in range(3):
                load("up", j, w_up[:, :, 512 * j:512 * j + 512], k8(page("up", j)))
            sp.wait_ge(s("xm_mm"), 4)
            load("up", 3, w_up[:, :, 1536:2048], k8(page("up", 3)))
            for p in range(2):
                sp.wait_ge(s("xm_mm"), 4 * (p + 2))
                load_state(p)
            sp.wait_ge(s("xm_mm"), 16)
            load_state(2)
            for p in range(16):
                sp.wait_ge(s("c_new"), 8 * (p + 1))
                for n in range(2):
                    sp.dma_start(state(O["C_s"], p, n), cview(p, n)).then_inc(s("c_stored"), 16)
                sp.wait_ge(s("c_stored"), 32 * (p + 1))
                if p + 3 < 16:
                    load_state(p + 3)
                else:
                    load_z(p - 13)
            sp.wait_ge(s("num_mm"), 2 * H)
            for i in range(2):
                sp.wait_ge(s(f"cp_stored{i}"), 16 * 8)
            sp.wait_ge(s("cv_stored"), 32)
            load_z(3)
            for j in range(4):
                if j == 2:
                    sp.wait_ge(s("z_mm"), 16)
                elif j == 3:
                    sp.wait_ge(s("down_mm"), 2)
                load("down", j, w_dn[:, :, 256 * j:256 * j + 256], k16(page("down", j)))
            def experts(L, base):
                gate = A["moe_w_gate"].rearrange("i g e (k p) f -> (i g e) p k f", p=P)
                up = A["moe_w_up"].rearrange("i g e (k p) f -> (i g e) p k f", p=P)
                down = A["moe_w_down"].rearrange("i g e (k p) n -> (i g e) p k n", p=P)
                before_loop = {0: ("z_mm", 8), 1: ("z_mm", 12), 2: ("z_mm", 4), 3: ("down_mm", 6), 4: ("down_mm", 8),
                               5: ("down_mm", 4)} if L == 0 else \
                    {0: ("in_mm", 28), 1: ("in_mm", 32), 2: ("out_mm", 2), 3: ("out_mm", 4), 4: ("out_mm", 6),
                     5: ("out_mm", 8)}

                def turn(it, pair):
                    (g0, u0, d0), (g1, u1, d1) = expert_pages(0), expert_pages(1)
                    for slot, (dst, src, used) in enumerate((
                            (g0, gate, "gu_mm0"), (u0, up, "gu_mm0"), (g1, gate, "gu_mm1"), (u1, up, "gu_mm1"),
                            (d0, down, "y_mm"), (d1, down, "y_mm"))):
                        j = slot // 2 if slot < 4 else slot - 4
                        if slot in before_loop:
                            sp.wait_ge(s(before_loop[slot][0]), before_loop[slot][1])
                        sp.wait_ge(s(used), it)
                        sp.dma_start(dst, src[bass.ds(L * NE + 2 * pair + j, 1)].rearrange("a p k f -> p (a k) f")) \
                            .then_inc(s(f"expert_landed{slot}"), 16)

                with sp.Fori(0, 15) as i:
                    turn(i + base, i)
                sp.wait_ge(s("table"), L + 1)
                rounds = sp.value_load(table[0:1, ROUNDS * NE + 1:ROUNDS * NE + 2], min_val=1, max_val=ROUNDS)
                with sp.Fori(15, rounds * 16) as i:
                    turn(i + base, i % 16)
                return base + rounds * 16

            turns = experts(0, 0)
            for j in range(8):
                if j < 6:
                    sp.wait_ge(s(("gu_mm0", "gu_mm1", "y_mm")[j // 2]), turns)
                else:
                    sp.wait_ge(s("in_mm"), 4 * (j - 5))
                c = 512 * ((j + 4) % 8)
                load("in", j, w_in[:, :, c:c + 512], k8(page("in", j)))
                if j == 0:
                    sp.wait_ge(s("moe_add"), turns * KD)
                    sp.dma_start(raw_ws, A["cmlp_w_s"][0].rearrange("g t s -> t g s")).then_inc(s("ws_landed"), 16)
                    sp.dma_start(bsb.rearrange("p g t -> p (g t)"),
                                 A["cmlp_b_s"].rearrange("o g t -> o (g t)").to_broadcast([P, CG * P])) \
                        .then_inc(s("bs_landed"), 16)
            for j in range(4):
                sp.wait_ge(s("in_mm"), 4 * (j + 3))
                load("out", j, w_out[:, :, 256 * j:256 * j + 256], k16(page("out", j)))
                if j == 1:
                    sp.wait_ge(s("vtok_mm"), 12)
                    for n, name in enumerate(("cmlp_ln_w", "cmlp_ln_b")):
                        sp.dma_start(lnwb[:, n, :], A[name].to_broadcast([P, INNER])).then_inc(s("ln_landed"), 16)
            experts(1, turns)
            sp.wait_ge(s("y_ready"), 6)
            sp.dma_start(O["y_p"][0].rearrange("(j p) n -> p j n", p=P), ytok[:, 0:2, :]).then_inc(s("y_stored"), 16)
            sp.dma_start(O["y_s"].rearrange("b s n -> (b s) n"), ytok[0:NS, 2, :]).then_inc(s("y_stored"), 16)
            sp.wait_ge(s("y_stored"), 32)
            sp.wait_ge(s("np_stored"), 16 * H)

        @block.gpsimd
        def _(pool):
            chain = [0]

            def link(ins):
                chain[0] += 1
                ins.then_inc(s("pool_chain"), 1)
                pool.wait_ge(s("pool_chain"), chain[0])

            def keep(t, pattern, base, mult, fill=0.0, op=ALU.is_ge):
                return pool.affine_select(out=t, in_=t, compare_op=op, fill=fill, base=base,
                                          pattern=pattern, channel_multiplier=mult)

            link(pool.memset(ident[:], 0.0))
            keep(ident[:], [[-1, P]], 0, 1, 1.0, ALU.not_equal).then_inc(s("consts"), 1)
            pool.memset(ones[:], 1.0).then_inc(s("consts"), 1)
            link(pool.memset(bmask[:], 1.0))
            link(keep(bmask[:], [[-4, 32]], 0, 1))
            keep(bmask[:], [[4, 32]], 3, -1).then_inc(s("consts"), 1)
            link(pool.memset(before[:], 1.0))
            keep(before[:], [[1, P]], -1, -1).then_inc(s("consts"), 1)
            pool.memset(xe[:, :, 0:3], 0.0).then_inc(s("consts"), 1)
            link(pool.memset(small[:], 0.0))
            link(pool.memset(eps6, 1e-6))
            pool.memset(eps5, 1e-5).then_inc(s("consts"), 1)
            pool.memset(rows[:], 0.0).then_inc(s("consts"), 1)
            pool.memset(gt[0:96, 0, :], 0.0).then_inc(s("consts"), 1)
            pool.wait_ge(s("consts"), 3)
            pool.wait_ge(s("raw_out"), 7)
            for n in range(3):
                for i in range(4):
                    pool.tensor_tensor(
                        bd[:, n, :, :].rearrange("p m (n d) -> p m n d", d=4)[:, :, :, i],
                        wqkv[:, i, 16 * n:16 * n + 16].unsqueeze(2).to_broadcast([P, KI, 32]),
                        bmask[:].unsqueeze(1).to_broadcast([P, KI, 32]), ALU.mult).then_inc(s("bd"), 1)
            pool.wait_ge(s("gate_part"), KI)
            pool.wait_ge(s("bd"), 12)
            pool.memset(qz, 0.0).then_inc(s("qz_zero"), 1)
            n_in = A["state_mlstm_n"][0].rearrange("b h d -> h b d")
            n_out = O["n_s"][0].rearrange("b h d -> h b d")
            for h in range(2):
                pool.dma_start(nrow[:, h, :], n_in[h]).then_inc(s(f"n_landed{h}"), 16)
            pool.wait_ge(s("cv_out"), 4)
            pool.dma_start(O["conv_p"][0, 0], cvout[0:3]).then_inc(s("cv_stored"), 16)
            pool.dma_start(O["conv_s"][0].rearrange("b c n -> (b c) n"), cvout[3:27]).then_inc(s("cv_stored"), 16)
            pool.wait_ge(s("gates_dve"), 2)
            pool.dma_start(O["m_p"][0].rearrange("o h -> h o"), rows[32:36, NPROMPT - 1:NPROMPT],
                           allow_slow_non_contiguous=True).then_inc(s("m_stored"), 16)
            pool.dma_start(O["m_s"][0].rearrange("b h -> h b"), rows[32:36, NPROMPT + 3:NT:SB],
                           allow_slow_non_contiguous=True).then_inc(s("m_stored"), 16)
            for h in range(H):
                pool.wait_ge(s("e_ready"), 3 * (h + 1))
                keep(ew[:, 0:128], [[1, P]], 0, -1).then_inc(s("e_masked"), 1)
                keep(ew[:, 256:384], [[1, P]], 0, -1).then_inc(s("e_masked"), 1)
                es = ew[0:NS, 384:416].rearrange("p (b t) -> p b t", t=SB)
                link(keep(es, [[SB, NB], [1, SB]], 0, -1))
                keep(es, [[-SB, NB], [0, SB]], 0, 1).then_inc(s("e_masked"), 1)
                pool.wait_ge(s("ns_out"), h + 1)
                pool.dma_start(n_out[h], nrow[:, h % 2, :]).then_inc(s(f"n_stored{h % 2}"), 16)
                if h + 2 < H:
                    pool.wait_ge(s(f"n_stored{h % 2}"), 16 * (h // 2 + 1))
                    pool.dma_start(nrow[:, h % 2, :], n_in[h + 2]).then_inc(s(f"n_landed{h % 2}"), 16)
            for i in range(2):
                pool.wait_ge(s(f"n_stored{i}"), 32)
            pool.wait_ge(s("m_stored"), 32)
            for L in range(2):
                pool.wait_ge(s(("down_add", "out_add")[L]), KD)
                pool.iota(iota, [[1, NSLOT]], base=0, channel_multiplier=0,
                          allow_small_or_imprecise_dtypes=True).then_inc(s("iota"), 1)
                pool.iota(iota32, [[1, NE]], base=0, channel_multiplier=0,
                          allow_small_or_imprecise_dtypes=True).then_inc(s("iota"), 1)
                pool.iota(rowplace, [[2 * CAP, ROUNDS * NE // 2]], base=0, channel_multiplier=1,
                          allow_small_or_imprecise_dtypes=True).then_inc(s("iota"), 1)
                pool.wait_ge(s("iota"), 3 * L + 3)
                pool.memset(xsT[:, :, NSLOT:SLOTS], 0.0).then_inc(s("xs_pad"), 1)
                if L == 0:
                    pool.wait_ge(s("ws_out"), 2)
                    keep(wsT, [[0, CG], [1, P]], 0, -1).then_inc(s("ws_masked"), 1)
                    pool.wait_ge(s("v_norm"), 3)
                    pool.dma_start(O["v_s"][0].rearrange("b s n -> (b s) n"), vtk[0:NS, 2, :]).then_inc(s("v_stored"), 16)
                    pool.wait_ge(s("v_stored"), 16)

        @block.scalar
        def _(act):
            ld = [0]

            def get(dst, src):
                act.dma_start(dst, src, allow_slow_non_contiguous=True).then_inc(s("raw_landed"), 16)

            for name, n in vec_rows:
                c0 = V[name]
                half, r0 = (0, c0) if c0 < 128 else (1, c0 - 128)
                a = A[name]
                flat = a if len(a.shape) == 1 else a.rearrange({2: "a b -> (a b)", 3: "a b c -> (a b c)"}[len(a.shape)])
                act.dma_start(raw_vec[r0:r0 + n, half, :], flat.rearrange("(r p) -> r p", p=P)) \
                    .then_inc(s("vec_landed"), 16)
            for n, name in enumerate(("mlstm_w_q", "mlstm_w_k", "mlstm_w_v")):
                get(raw_qkv[16 * n:16 * n + 16], A[name][0].rearrange("(m n) c d -> m (n c d)", m=KI))
            for n, name in enumerate(("mlstm_w_ig", "mlstm_w_fg")):
                get(raw_if[0:48, n, :], A[name][0].rearrange("(t p) h -> t (p h)", p=P))
            get(raw_re[0:64], A["moe_w_re"].rearrange("i g (k p) e -> (i g k) (p e)", p=P))
            get(raw_rg[0:16], A["moe_w_rg"].rearrange("i (k p) g -> (i k) (p g)", p=P))
            get(raw_conv[0:24], A["state_mlstm_conv"][0].rearrange("b c n -> (b c) n"))
            get(nraw[0:32], A["state_mlstm_n"][0].rearrange("b h d -> (b h) d"))
            get(m0[:], A["state_mlstm_m"][0].rearrange("b h -> h b"))
            get(gb[:, 0:1], A["mlstm_b_ig"].rearrange("o h -> h o"))
            get(gb[:, 1:2], A["mlstm_b_fg"].rearrange("o h -> h o"))
            for i in range(2):
                get(rbias[:, i, 0:G], A["moe_b_rg"][i:i + 1].to_broadcast([P, G]))
                get(rbias[:, i, G:36], A["moe_b_re"][i:i + 1].rearrange("o g e -> o (g e)").to_broadcast([P, NE]))

            def square(k):
                act.activation(hT[:, k, :], xT[:, k, :], ACT.Square).then_inc(s("sq"), 1)

            def norm(n, x_sem=None, x_before=0):
                if x_sem:
                    for k in range(KD):
                        act.wait_ge(s(x_sem), x_before + k + 1)
                        square(k)
                act.wait_ge(s("ss"), n + 1)
                act.activation(stdv, B[7][:, 0:NT], ACT.Sqrt, bias=eps6, scale=1.0 / D).then_inc(s("std"), 1)

            for k in range(KD):
                act.wait_ge(s("x_tr"), k + 1)
                act.activation(xT[:, k, :], B[k % 2][:, 0:NT], ACT.Copy).then_inc(s("xT"), 1)
                act.wait_ge(s("xT"), k + 1)
                square(k)
            act.wait_ge(s("consts"), 6)
            norm(0)
            for m in range(KI + 1):
                if m < KI:
                    act.wait_ge(s("xm_mm"), m + 1)
                    act.activation(xe[:, m, 3:XS], B[m % 4][:, 0:NPROMPT], ACT.Copy).then_inc(s("xm_out"), 1)
                    act.activation(sample_view(xe[:, m, :])[:, :, 3:7],
                                   B[m % 4][:, NPROMPT:NT].rearrange("p (b s) -> p b s", s=SB),
                                   ACT.Copy).then_inc(s("xm_out"), 1)
                    act.activation(xms[:, m, :], B[m % 4][:, NPROMPT:NT], ACT.Copy).then_inc(s("xm_out"), 1)
                if m > 0:
                    c = m - 1
                    act.wait_ge(s("conv"), c + 1)
                    act.activation(xc[:, c, 0:NPROMPT], ctmp[:, c % 2, 0:NPROMPT], ACT.Silu).then_inc(s("xc"), 1)
                    act.activation(xc[:, c, NPROMPT:NT].rearrange("p (b s) -> p b s", s=SB),
                                   sample_view(ctmp[:, c % 2, :])[:, :, 0:4], ACT.Silu).then_inc(s("xc"), 1)
            for m in range(KI):
                act.wait_ge(s("qkv_mm"), m + 1)
                if m == 0:
                    act.wait_ge(s("raw_out"), 7)
                act.activation(qT[:, m, :], B[m % 2][:, 0:NT], ACT.Copy).then_inc(s("q_out"), 1)
                if m >= 2:
                    act.wait_ge(s("gate_part"), m - 1)
                act.activation(vtr[:, m % 2, :], B[4 + m % 2][:, 0:NT], ACT.Copy).then_inc(s("v_out"), 1)
            act.wait_ge(s("gate_part"), KI)
            act.wait_ge(s("consts"), 8)
            for n in range(3):
                ins = act.activation(gt[32 * n:32 * n + 8, 0, :], B[6][32 * n:32 * n + 8, 0:NT], ACT.Copy)
            ins.then_inc(s("gates_act"), 1)
            act.wait_ge(s("gates_pe"), 1)
            act.activation(gt[0:4, 1, :], B[0][0:4, 0:NT], ACT.Identity, bias=gb[:, 0:1]).then_inc(s("gates_act"), 1)
            act.activation(gt[0:4, 2, :], B[1][0:4, 0:NT], ACT.Identity, bias=gb[:, 1:2]).then_inc(s("gates_act"), 1)
            act.wait_ge(s("gates_dve"), 1)
            act.activation(gt[0:4, 4, :], gt[0:4, 3, :], ACT.Exp, scale=-1.0).then_inc(s("gates_act"), 1)
            act.wait_ge(s("gates_act"), 4)
            act.wait_ge(s("consts"), 2)
            act.activation(gt[0:4, 3, :], gt[0:4, 4, :], ACT.Ln, bias=ones[0:4, 0:1]).then_inc(s("gates_act"), 1)
            act.wait_ge(s("gates_pe"), 2)
            for j, (_, n) in enumerate(TOK):
                b = B[2][0:n, 128 * j:128 * j + 128]
                act.activation(tm[0:n, j, 0:4], b[:, 0:4], ACT.Copy).then_inc(s("tm"), 1)
                act.activation(tm[0:n, j, 4:8], b[:, 32:36], ACT.Exp, scale=-1.0).then_inc(s("tm"), 1)
                act.activation(tm[0:n, j, 8:12], b[:, 96:100], ACT.Exp).then_inc(s("tm"), 1)
            act.activation(decn[:], B[3][0:NB, 0:H], ACT.Exp).then_inc(s("tm"), 1)
            act.wait_ge(s("tm"), 10)

            cst_n = 0
            for h in range(H):
                act.wait_ge(s("bc_mm"), h + 1)
                act.activation(decb[:, h, :], B[0][:, NT:NT + 8], ACT.Exp).then_inc(s("bc_exp"), 1)
                act.activation(ibc[:, h, :], B[0][:, NT + 8:NT + 8 + NS], ACT.Exp).then_inc(s("bc_exp"), 1)
                if h > 0:
                    act.wait_ge(s("stw"), 3 * h)
                act.activation(ew[:, 0:256], B[0][:, 0:256], ACT.Exp, scale=-1.0, bias=tm[:, 0, h:h + 1]) \
                    .then_inc(s("e_ready"), 1)
                act.activation(ew[:, 256:384], B[0][:, 128:256], ACT.Exp, scale=-1.0, bias=tm[:, 1, h:h + 1]) \
                    .then_inc(s("e_ready"), 1)
                act.activation(ew[0:NS, 384:416], B[0][0:NS, 256:288], ACT.Exp, scale=-1.0,
                               bias=tm[0:NS, 2, h:h + 1]).then_inc(s("e_ready"), 1)
                act.wait_ge(s("v_mm"), h + 1)
                if h > 0:
                    act.wait_ge(s("num_mm"), 2 * h)
                for j, (_, n) in enumerate(TOK):
                    act.activation(vtok[0:n, j, :], B[4 + j][0:n, :], ACT.Copy).then_inc(s("vtok"), 1)
                for n in range(4):
                    act.wait_ge(s("spread_mm"), 4 * h + n + 1)
                    if n < 2 and h > 0:
                        act.wait_ge(s("parts"), 4 * h)
                    elif n >= 2:
                        act.wait_ge(s("parts"), 4 * h + n - 1)
                    act.activation(y16[:, n % 2, :], B[1 + n][:, :], ACT.Copy).then_inc(s("y1"), 1)
                for i in range(MH):
                    act.wait_ge(s("cp_mm"), 4 * h + i + 1)
                    if cst_n >= 2:
                        act.wait_ge(s(f"cp_stored{i % 2}"), 16 * (cst_n // 2))
                    act.activation(cst[:, i % 2, :], B[5 + i % 2][:, :], ACT.Copy).then_inc(s("cp_out"), 1)
                    act.wait_ge(s("cp_out"), cst_n + 1)
                    act.dma_start(O["C_p"][0, 0, h, 128 * i:128 * i + 128, :], cst[:, i % 2, :]) \
                        .then_inc(s(f"cp_stored{i % 2}"), 16)
                    cst_n += 1
                act.wait_ge(s("np_mm"), h + 1)
                if h > 0:
                    act.wait_ge(s("np_stored"), 16 * h)
                act.activation(nst[:], B[0][0:1, :], ACT.Copy).then_inc(s("np_out"), 1)
                act.wait_ge(s("np_out"), h + 1)
                act.dma_start(O["n_p"][0, :, h, :], nst[:]).then_inc(s("np_stored"), 16)
                act.wait_ge(s("rden"), 2 * h + 1)
                for j in range(2):
                    act.activation(hhp[h][:, j, :], B[1 + j][:, :], ACT.Copy, scale=rden[:, j:j + 1]) \
                        .then_inc(s("hh"), 1)
                act.wait_ge(s("c_mm"), 32 * (h + 1))
                act.activation(snum, B[4][:, :], ACT.Copy).then_inc(s("snum"), 1)
                act.wait_ge(s("num_mm"), 2 * h + 2)
                act.wait_ge(s("rden"), 2 * h + 2)
                act.activation(hhs[h][0:NS], B[4][0:NS, :], ACT.Copy, scale=rden[0:NS, 2:3]).then_inc(s("hh"), 1)
            for m in range(KI):
                act.wait_ge(s("z_mm"), m + 1)
                act.activation(zs[:, m, :], B[m % 4][:, 0:NT], ACT.Silu).then_inc(s("zs"), 1)
                if m == 3:
                    act.wait_ge(s("mv"), 12)
                    act.activation(mvsd, mvsd, ACT.Sqrt, bias=eps5).then_inc(s("hsd"), 1)

            def moe(L, base):
                norm(1 + 2 * L, ("down_add", "out_add")[L])
                for n in range(6):
                    j, c = divmod(n, 2)
                    t = TOK[j][1]
                    act.wait_ge(s("htok_mm"), 6 * L + n + 1)
                    act.activation(htok[0:t, j, 512 * c:512 * c + 512], B[n][0:t, :], ACT.Copy) \
                        .then_inc(s("htok"), 1)
                act.wait_ge(s("router_dve"), 3 * L + 1)
                act.activation(rt[:, 320:332], rt[:, 300:312], ACT.Exp).then_inc(s("router_act"), 1)
                act.wait_ge(s("router_dve"), 3 * L + 2)
                act.activation(rt[:, 343:346], rt[:, 340:343], ACT.Exp).then_inc(s("router_act"), 1)
                for n in range(1, 16, 2):
                    c, m = divmod(n, 8)
                    act.wait_ge(s("gather_mm"), 16 * L + n + 1)
                    act.activation(xsT[:, m, NT * c:NT * c + NT], B[n % 6][:, 0:NT], ACT.Copy) \
                        .then_inc(s("xs_a"), 1)
                act.wait_ge(s("table"), L + 1)
                rounds = act.value_load(table[0:1, ROUNDS * NE + 1:ROUNDS * NE + 2], min_val=1, max_val=ROUNDS)
                with act.Fori(0, rounds * 16) as i:
                    it = i + base
                    for j in range(2):
                        act.wait_ge(s(f"gu_mm{j}"), it + 1)
                        act.activation(sg[CAP:P, j, :], B[j][0:CAP, :], ACT.Silu).then_inc(s(f"sg{j}"), 1)
                    act.wait_ge(s("y_mm"), it + 1)
                    act.wait_ge(s("scatter_mm"), it * KD)
                    for c in range(2):
                        act.activation(ysb[:, F * c:F * c + F], B[2 + c][:, :], ACT.Copy).then_inc(s("y_out"), 1)
                last = act.value_load(table[0:1, ROUNDS * NE + 2:ROUNDS * NE + 3], min_val=0, max_val=ROUNDS * 16)
                return base + rounds * 16, base + last

            turns, last = moe(0, 0)
            norm(2, "moe_add", last * KD)
            for m in range(2 * KI):
                act.wait_ge(s("in_mm"), m + 1)
                dst = vT[:, m, :] if m < KI else uT[:, m - KI, :]
                act.activation(dst, B[m % 4][:, 0:NT], ACT.Gelu_apprx_tanh, bias=vec("cmlp_b_in", (m + KI) % (2 * KI))) \
                    .then_inc(s("gelu"), 1)
                if m == KI + 3:
                    for j, (_, n) in enumerate(TOK):
                        act.wait_ge(s("vstat"), j + 1)
                        act.activation(mvc[0:n, j, 1:2], mvc[0:n, j, 1:2], ACT.Sqrt, bias=eps5[0:n]) \
                            .then_inc(s("vsd"), 1)
            _, last = moe(1, turns)
            norm(4, "moe_add", last * KD)
            for n in range(6):
                j, c = divmod(n, 2)
                t = TOK[j][1]
                act.wait_ge(s("y_tr"), n + 1)
                act.activation(ytok[0:t, j, 512 * c:512 * c + 512], B[n][0:t, :], ACT.Copy).then_inc(s("y_ready"), 1)

        @block.tensor
        def _(pe):
            mm, tr = pe.matmul, pe.transpose

            def sum_squares(n, k):
                pe.wait_ge(s("sq"), KD * n + k + 1)
                ins = mm(B[7][:, 0:NT], ones[:], hT[:, k, :], start=(k == 0), stop=(k == KD - 1),
                         skip_group_check=True)
                if k == KD - 1:
                    ins.then_inc(s("ss"), 1)

            pe.wait_ge(s("consts"), 1)
            pe.wait_ge(s("x_landed"), 48)
            for k in range(KD):
                if k >= 2:
                    pe.wait_ge(s("xT"), k - 1)
                for j, (t0, n) in enumerate(TOK):
                    ins = tr(B[k % 2][:, t0:t0 + n], xtok[0:n, j, 128 * k:128 * k + 128], ident[0:n, 0:n])
                ins.then_inc(s("x_tr"), 1)
            pe.wait_ge(s("vec_landed"), 16 * len(vec_rows))
            tr(B[2][:, 0:128], raw_vec[:, 0, :], ident[:])
            tr(B[2][:, 128:192], raw_vec[0:64, 1, :], ident[0:64, 0:64]).then_inc(s("raw_tr"), 1)
            pe.wait_ge(s("consts"), 2)
            for k in range(KD):
                sum_squares(0, k)
            pe.wait_ge(s("raw_landed"), 16 * (3 + 2 + 4 + 3 + 4))
            for i in range(4):
                ins = tr(B[3][:, 48 * i:48 * i + 48], raw_qkv[0:48].rearrange("m (p d) -> m p d", d=4)[:, :, i],
                         ident[0:48, 0:48])
            ins.then_inc(s("raw_tr"), 1)
            for n in range(8):
                ins = tr(B[4][:, 48 * n:48 * n + 48],
                         raw_if[0:48, n // 4, :].rearrange("t (p h) -> t p h", h=4)[:, :, n % 4], ident[0:48, 0:48])
            ins.then_inc(s("raw_tr"), 1)
            for e in range(8):
                ins = tr(B[5][:, 64 * e:64 * e + 64], raw_re[0:64].rearrange("m (p e) -> m p e", e=8)[:, :, e],
                         ident[0:64, 0:64])
            ins.then_inc(s("raw_tr"), 1)
            for g in range(4):
                ins = tr(B[6][:, 16 * g:16 * g + 16], raw_rg[0:16].rearrange("m (p g) -> m p g", g=4)[:, :, g],
                         ident[0:16, 0:16])
            ins.then_inc(s("raw_tr"), 1)
            pe.wait_ge(s("xT"), KD)
            for m in range(KI):
                ins = tr(B[1][:, 24 * m:24 * m + 24], raw_conv[0:24, 128 * m:128 * m + 128], ident[0:24, 0:24])
            ins.then_inc(s("raw_tr"), 1)
            for i in range(MH):
                ins = tr(B[0][:, 32 * i:32 * i + 32], nraw[0:32, 128 * i:128 * i + 128], ident[0:32, 0:32])
            ins.then_inc(s("raw_tr"), 1)
            pe.wait_ge(s("raw_out"), 7)

            def dense(key, groups, per, width, kt, rhs, done, freed, first=None, after=None):
                m = 0
                for j in range(groups):
                    landed(pe, key, j)
                    w = page(key, j).rearrange("p (k n) -> p k n", k=kt)
                    for i in range(per):
                        if m >= 4:
                            freed(m - 4)
                        for k in range(kt):
                            if m == 0 and first:
                                first(k)
                            ins = mm(B[m % 4][:, 0:NT], w[:, k, 128 * i:128 * i + 128], rhs(k),
                                     start=(k == 0), stop=(k == kt - 1))
                        ins.then_inc(s(done), 1)
                        if after:
                            after(m)
                        m += 1

            def normed(n):
                return lambda k: pe.wait_ge(s("h_norm"), KD * n + k + 1)

            def squares_behind(n):
                def after(m):
                    if m > 0:
                        sum_squares(n, m - 1)
                    if m == KD - 1:
                        sum_squares(n, m)
                return after

            dense("up", 4, 4, 512, KD, lambda k: hT[:, k, :], "xm_mm", lambda m: pe.wait_ge(s("xm_out"), 3 * m + 3),
                  first=normed(0))

            def gate_part(m):
                pe.wait_ge(s("q_out"), m + 1)
                pe.wait_ge(s("k_out"), m + 1)
                pe.wait_ge(s("v_out"), m + 1)
                for n, src in enumerate((qT[:, m, :], kT[:, m, :], vtr[:, m % 2, :])):
                    ins = mm(B[6][32 * n:32 * n + 8, 0:NT], wif[:, 16 * n + m, :], src,
                             start=(m == 0), stop=(m == KI - 1), skip_group_check=True)
                ins.then_inc(s("gate_part"), 1)

            pe.wait_ge(s("bd"), 12)
            pe.wait_ge(s("xm_out"), 3 * KI)
            for m in range(KI):
                pe.wait_ge(s("xc"), 2 * m + 2)
                if m >= 2:
                    pe.wait_ge(s("q_out"), m - 1)
                    pe.wait_ge(s("k_out"), m - 1)
                    pe.wait_ge(s("v_out"), m - 1)
                mm(B[m % 2][:, 0:NT], bd[:, 0, m, :], xc[:, m, :], start=True, stop=True)
                mm(B[2 + m % 2][:, 0:NT], bd[:, 1, m, :], xc[:, m, :], start=True, stop=True)
                mm(B[4 + m % 2][:, 0:NPROMPT], bd[:, 2, m, :], xe[:, m, 3:XS], start=True, stop=True)
                mm(B[4 + m % 2][:, NPROMPT:NT], bd[:, 2, m, :], xms[:, m, :],
                   start=True, stop=True).then_inc(s("qkv_mm"), 1)
                if m >= 1:
                    gate_part(m - 1)
            gate_part(KI - 1)
            pe.wait_ge(s("gates_act"), 1)
            pe.wait_ge(s("gfold"), 1)
            mm(B[0][0:4, 0:NT], gfold[0:96, 0:4], gt[0:96, 0, :], start=True, stop=True)
            mm(B[1][0:4, 0:NT], gfold[0:96, 4:8], gt[0:96, 0, :], start=True, stop=True).then_inc(s("gates_pe"), 1)
            pe.wait_ge(s("q_out"), KI)
            pe.wait_ge(s("k_out"), KI)
            pe.wait_ge(s("v_out"), KI)
            pe.wait_ge(s("cv27"), 2)
            for m in range(KI):
                if m in (8, 12):
                    pe.wait_ge(s("cv_out"), m // 4 - 1)
                ins = tr(B[4 + (m // 4) % 2][0:27, 128 * (m % 4):128 * (m % 4) + 128], cv27[:, m, :], ident[:])
                if m % 4 == 3:
                    ins.then_inc(s("cv_tr"), 1)
            def values_by_token(h):
                for j, (t0, t) in enumerate(TOK):
                    for i in range(MH):
                        m = MH * h + i
                        lhs = xe[:, m, 3 + t0:3 + t0 + t] if j < 2 else xms[:, m, :]
                        ins = mm(B[4 + j][0:t, 128 * i:128 * i + 128], lhs, bd[:, 2, m, :], start=True, stop=True)
                ins.then_inc(s("v_mm"), 1)
                for i in range(MH):
                    mm(B[7][:, 0:256], kT[:, MH * h + i, 0:128], qT[:, MH * h + i, 0:256],
                       start=(i == 0), stop=(i == MH - 1))
                for i in range(MH):
                    mm(B[7][:, 256:384], kT[:, MH * h + i, 128:256], qT[:, MH * h + i, 128:256],
                       start=(i == 0), stop=(i == MH - 1))
                for i in range(MH):
                    ins = mm(B[7][0:NS, 384:416], kT[:, MH * h + i, 256:288], qT[:, MH * h + i, 256:288],
                             start=(i == 0), stop=(i == MH - 1))
                ins.then_inc(s("st_mm"), 1)

            pe.wait_ge(s("cv_out"), 4)
            values_by_token(0)
            pe.wait_ge(s("gates_dve"), 2)
            for j, (t0, n) in enumerate(TOK):
                tr(B[2][0:n, 128 * j:128 * j + 128], rows[:, t0:t0 + n], ident[:])
            tr(B[3][0:NB, 0:H], catA[0:4, NT:NT + 8], ident[0:4, 0:4]).then_inc(s("gates_pe"), 1)
            pe.wait_ge(s("tm"), 10)

            pe.wait_ge(s("part_masks"), 1)
            for h in range(H):
                if h > 0:
                    pe.wait_ge(s("hh"), 3 * h)
                    pe.wait_ge(s("rden"), 2 * h)
                    pe.wait_ge(s("c_new"), 32 * h)
                mm(B[0][:, 0:NT + 8 + NS], ident[0:4, h:h + 1].to_broadcast([4, P]), catA[:, :],
                   start=True, stop=True).then_inc(s("bc_mm"), 1)
                for j, (t0, t) in enumerate(TOK):
                    for i in range(MH):
                        ins = tr(B[1 + j][0:t, 128 * i:128 * i + 128], kT[:, MH * h + i, t0:t0 + t], ident[:])
                ins.then_inc(s("k_mm"), 1)
                if h > 0:
                    values_by_token(h)
                pe.wait_ge(s("wk"), 3 * h + 3)
                pe.wait_ge(s("vtok"), 3 * h + 3)
                for n, src in enumerate((wk, vtok)):
                    for half in range(2):
                        mm(B[1 + 2 * n + half][:, :], spread[0:NS, half, :], src[0:NS, 2, :],
                           start=True, stop=True).then_inc(s("spread_mm"), 1)
                for i in range(MH):
                    if i >= 2:
                        pe.wait_ge(s("cp_out"), MH * h + i - 1)
                    for j in range(2):
                        ins = mm(B[5 + i % 2][:, :], wk[:, j, 128 * i:128 * i + 128], vtok[:, j, :],
                                 start=(j == 0), stop=(j == 1))
                    ins.then_inc(s("cp_mm"), 1)
                pe.wait_ge(s("e_ready"), 3 * h + 3)
                for j in range(2):
                    ins = mm(B[0][0:1, :], ones[:, 0:1], wk[:, j, :], start=(j == 0), stop=(j == 1))
                ins.then_inc(s("np_mm"), 1)
                pe.wait_ge(s("stw"), 3 * h + 3)
                pe.wait_ge(s("z1"), 4 * (h + 1))
                mm(B[1][:, :], stw[:, 0:128], vtok[:, 0, :], start=True, stop=True)
                mm(B[2][:, :], stw[:, 128:256], vtok[:, 0, :], start=True, stop=False)
                mm(B[2][:, :], stw[:, 256:384], vtok[:, 1, :], start=False, stop=True)
                mm(B[3][:, 0:1], stw[:, 0:128], ones[:, 0:1], start=True, stop=True)
                mm(B[3][:, 1:2], stw[:, 128:256], ones[:, 0:1], start=True, stop=False)
                mm(B[3][:, 1:2], stw[:, 256:384], ones[:, 0:1], start=False, stop=True).then_inc(s("num_mm"), 1)
                mm(B[7][0:NB, :], bmask[0:NS, 0:NB], wk[0:NS, 2, :], start=True, stop=True).then_inc(s("ns_mm"), 1)
                pe.wait_ge(s("cp_out"), MH * h + MH)
                pe.wait_ge(s("qz"), 2 * h + 1)
                for b in range(NB):
                    p = 4 * h + b // 2
                    if b % 2 == 0:
                        landed(pe, "C", p)
                    cpage = page("C", p).rearrange("p (c v) -> p c v", v=DH)
                    for i in range(MH):
                        mm(B[4][NS * i:NS * i + NS, :], qz[:, i, NS * b:NS * b + NS], cpage[:, MH * (b % 2) + i, :],
                           start=(b == 0), stop=(b == NB - 1), skip_group_check=True)
                    if b == 0:
                        pe.wait_ge(s("parts"), 4 * (h + 1))
                        pe.wait_ge(s("ns_out"), h + 1)
                        pe.wait_ge(s("np_out"), h + 1)
                    g = 32 * (b % 4)
                    for i in range(MH):
                        n = (NB * h + b) * MH + i
                        if n >= 4:
                            pe.wait_ge(s("c_new"), n - 3)
                        mm(B[UPD[i]][:, :], wk8[g:g + 32, b // 4, 128 * i:128 * i + 128], v8[g:g + 32, b // 4, :],
                           start=True, stop=True).then_inc(s("c_mm"), 1)
                pe.wait_ge(s("rden"), 2 * h + 1)
                mm(B[3][0:NS, 2:3], stw[0:NS, 384:416], ones[0:NS, 0:1], start=True, stop=False)
                pe.wait_ge(s("qz"), 2 * h + 2)
                for i in range(MH):
                    mm(B[3][0:NS, 2:3], ew[:, 32 * i:32 * i + 32], ones[:, 0:1], start=False, stop=(i == MH - 1))
                pe.wait_ge(s("snum"), h + 1)
                mm(B[4][0:NS, :], fold, snum, start=True, stop=False)
                mm(B[4][0:NS, :], stw[0:NS, 384:416], vtok[0:NS, 2, :], start=False, stop=True) \
                    .then_inc(s("num_mm"), 1)
            pe.wait_ge(s("hh"), 3 * H)
            pe.wait_ge(s("c_new"), 32 * H)
            pe.wait_ge(s("ns_out"), H)
            def hidden(m):
                h, i = divmod(m, MH)
                pe.wait_ge(s("hn"), 3 * h + 3)
                if m >= 2:
                    pe.wait_ge(s("y_in"), m - 1)
                for j, (t0, n) in enumerate(TOK):
                    src = hhp[h][:, j, 128 * i:128 * i + 128] if j < 2 else hhs[h][0:NS, 128 * i:128 * i + 128]
                    ins = tr(B[4 + m % 2][:, t0:t0 + n], src, ident[0:n, 0:n])
                ins.then_inc(s("hn_tr"), 1)

            dense("z", 4, 4, 512, KD, lambda k: hT[:, k, :], "z_mm", lambda m: pe.wait_ge(s("zs"), m + 1),
                  after=lambda m: hidden(m - ZLAG) if m >= ZLAG else None)
            for m in range(KI - ZLAG, KI):
                hidden(m)
            dense("down", 4, 2, 256, KI, lambda k: xc[:, k, :], "down_mm", lambda m: pe.wait_ge(s("down_add"), m + 1),
                  first=lambda k: pe.wait_ge(s("y_mix"), k + 1), after=squares_behind(1))

            def moe(L, base):
                for j, (t0, t) in enumerate(TOK):
                    for k in range(KD):
                        if j == 0:
                            normed(1 + 2 * L)(k)
                        ins = mm(B[6][0:t, 36 * j:36 * j + 36], hT[:, k, t0:t0 + t], wr[:, L, k, :],
                                 start=(k == 0), stop=(k == KD - 1))
                ins.then_inc(s("router_pe"), 1)
                for n in range(6):
                    j, c = divmod(n, 2)
                    t0, t = TOK[j]
                    for k in range(4):
                        ins = tr(B[n][0:t, 128 * k:128 * k + 128], hT[:, 4 * c + k, t0:t0 + t], ident[:])
                    ins.then_inc(s("htok_mm"), 1)
                pe.wait_ge(s("router_dve"), 3 * L + 3)
                pe.wait_ge(s("consts"), 4)
                m2 = rt[:, 0:96].rearrange("p (j e) -> p j e", j=3)
                for j, (_, t) in enumerate(TOK):
                    for i in range(j):
                        mm(B[7][0:t, 32 * j:32 * j + 32], ones[:, 0:t], m2[:, i, :], start=(i == 0), stop=False)
                    mm(B[7][0:t, 32 * j:32 * j + 32], before[0:t, 0:t], m2[0:t, j, :], start=(j == 0), stop=True)
                for j, (_, t) in enumerate(TOK):
                    ins = mm(B[7][:, 96:128], ones[0:t, :], m2[0:t, j, :], start=(j == 0), stop=(j == 2))
                ins.then_inc(s("router_pe"), 1)
                pe.wait_ge(s("htok"), 6 * L + 6)
                pe.wait_ge(s("sel"), 3 * L + 3)
                for n in range(16):
                    c, m = divmod(n, 8)
                    if n >= 6:
                        o = n - 6
                        pe.wait_ge(s(f"xs_{'ba'[o % 2]}"), 8 * L + o // 2 + 1)
                    for i, (_, t) in enumerate(TOK):
                        ins = mm(B[n % 6][:, 0:NT], htok[0:t, i, 128 * m:128 * m + 128],
                                 sel[0:t, i, NT * c:NT * c + NT], start=(i == 0), stop=(i == 2))
                    ins.then_inc(s("gather_mm"), 1)
                pe.wait_ge(s("placew"), L + 1)
                for n in range(4):
                    if n >= 2:
                        pe.wait_ge(s("tokrow"), 4 * L + n - 1)
                    for j, (t0, t) in enumerate(TOK):
                        ins = mm(B[6 + n % 2][:, t0:t0 + t], placew[0:t, 3 * n + j:3 * n + j + 1].to_broadcast([t, P]),
                                 ident[0:t, 0:t], start=True, stop=True)
                    ins.then_inc(s("tokrow_mm"), 1)
                pe.wait_ge(s("tokrow"), 4 * L + 4)
                pe.wait_ge(s("xs_a"), 8 * L + 8)
                pe.wait_ge(s("xs_b"), 8 * L + 8)
                pe.wait_ge(s("table"), L + 1)
                rounds = pe.value_load(table[0:1, ROUNDS * NE + 1:ROUNDS * NE + 2], min_val=1, max_val=ROUNDS)
                with pe.Fori(0, rounds * 16) as i:
                    it = i + base
                    for j in range(2):
                        gw, uw, _ = expert_pages(j)
                        x = xcx[:, j, :].rearrange("p (k c) -> p k c", k=KD)
                        pe.wait_ge(s(f"expert_landed{2 * j}"), (it + 1) * 16)
                        pe.wait_ge(s(f"expert_landed{2 * j + 1}"), (it + 1) * 16)
                        pe.wait_ge(s(f"xcx{j}"), it + (1 + L * (1 - j)))
                        for k in range(KD):
                            mm(B[j][0:CAP, :], x[:, k, :], gw[:, k, :], start=(k == 0), stop=(k == KD - 1))
                            ins = mm(B[j][CAP:P, :], x[:, k, :], uw[:, k, :], start=(k == 0), stop=(k == KD - 1))
                        ins.then_inc(s(f"gu_mm{j}"), 1)
                    for j in range(2):
                        pe.wait_ge(s(f"hx{j}"), it + 1)
                        for f in range(MF):
                            ins = mm(B[4 + 3 * j][:, CAP * f:CAP * f + CAP], hx[CAP:P, j, 128 * f:128 * f + 128],
                                     ident[CAP:P, CAP:P], start=True, stop=True)
                        ins.then_inc(s(f"ht_tr{j}"), 1)
                    for j in range(2):
                        pe.wait_ge(s(f"expert_landed{4 + j}"), (it + 1) * 16)
                        pe.wait_ge(s(f"ht{j}"), it + 1)
                    pe.wait_ge(s("y_out"), it * 2)
                    for c in range(2):
                        for f in range(MF):
                            for j in range(2):
                                dw = expert_pages(j)[2]
                                ins = mm(B[2 + c][CAP * j:CAP * j + CAP, :], hxT[:, j, CAP * f:CAP * f + CAP],
                                         dw[:, f, 512 * c:512 * c + 512], start=(f == 0), stop=(f == MF - 1))
                    ins.then_inc(s("y_mm"), 1)
                    pe.wait_ge(s("wpair"), it + 1)
                    for m in range(KD):
                        if m % 4 == 0:
                            pe.wait_ge(s("y_out"), it * 2 + (m // 4 + 1))
                        if m >= 2:
                            pe.wait_ge(s("moe_add"), it * KD + (m - 1))
                        else:
                            pe.wait_ge(s("moe_add"), it * KD)
                        mm(B[5 + m % 2][:, 0:NT], ysb[:, 128 * m:128 * m + 128], wpair, start=True, stop=True) \
                            .then_inc(s("scatter_mm"), 1)
                turns = base + rounds * 16
                for k in range(KD):
                    sum_squares(2 + 2 * L, k)
                return turns

            turns = moe(0, 0)
            def v_by_token(m):
                c = (m - 5) // 4
                if m == 5:
                    pe.wait_ge(s("ws_landed"), 16)
                    for g in range(CG):
                        ins = tr(B[4 + g // 4][:, 128 * (g % 4):128 * (g % 4) + 128], raw_ws[:, g, :], ident[:])
                        if g % 4 == 3:
                            ins.then_inc(s("ws_tr"), 1)
                    pe.wait_ge(s("ws_out"), 2)
                if m in (5, 9, 13, 17):
                    pe.wait_ge(s("gelu"), 4 * c + 4)
                    for j, (t0, t) in enumerate(TOK):
                        n = 3 * c + j
                        if n >= 4:
                            pe.wait_ge(s("vtk"), n - 3)
                        for i in range(4):
                            ins = tr(B[4 + n % 4][0:t, 128 * i:128 * i + 128], vT[:, 4 * c + i, t0:t0 + t], ident[:])
                        ins.then_inc(s("vtok_mm"), 1)

            dense("in", 8, 4, 512, KD, lambda k: hT[:, k, :], "in_mm", lambda m: pe.wait_ge(s("gelu"), m + 1),
                  first=normed(2), after=v_by_token)
            pe.wait_ge(s("vtk"), 12)
            pe.wait_ge(s("ws_masked"), 1)
            pe.wait_ge(s("rep"), 1)
            mm(B[4][0:NS, 0:CG * SB], rep[0:4, :], wsT[0:4, :, 0:SB], start=True, stop=True).then_inc(s("wsS_mm"), 1)
            pe.wait_ge(s("wsS"), 1)
            pe.wait_ge(s("v_norm"), 3)
            for m in range(KI):
                if m >= 4:
                    pe.wait_ge(s("mixed"), m - 3)
                for j in range(2):
                    mm(B[4 + m % 4][:, 128 * j:128 * j + 128], vtk[:, j, 128 * m:128 * m + 128], wsT[:, m // 2, :],
                       start=True, stop=True)
                mm(B[4 + m % 4][:, 256:NT], vtk[0:NS, 2, 128 * m:128 * m + 128], wsS[0:NS, m // 2, :],
                   start=True, stop=True).then_inc(s("mix_mm"), 1)
            pe.wait_ge(s("gelu"), 2 * KI)
            dense("out", 4, 2, 256, KI, lambda k: uT[:, k, :], "out_mm", lambda m: pe.wait_ge(s("out_add"), m + 1),
                  first=lambda k: pe.wait_ge(s("mixed"), k + 1), after=squares_behind(3))
            moe(1, turns)
            for n in range(6):
                j, c = divmod(n, 2)
                t0, t = TOK[j]
                for k in range(4):
                    if j == 0:
                        normed(4)(4 * c + k)
                    ins = tr(B[n][0:t, 128 * k:128 * k + 128], hT[:, 4 * c + k, t0:t0 + t], ident[:])
                ins.then_inc(s("y_tr"), 1)

        @block.vector
        def _(dve):
            chain = [0]

            def link(ins):
                chain[0] += 1
                ins.then_inc(s("dve_chain"), 1)
                dve.wait_ge(s("dve_chain"), chain[0])

            tt, ts, stt, copy = dve.tensor_tensor, dve.tensor_scalar, dve.scalar_tensor_tensor, dve.tensor_copy

            raws = [
                (vecs[:], B[2][:, 0:192]),
                (wqkv, B[3][:, 0:192].rearrange("p (i m) -> p i m", i=4)),
                (wif[:].rearrange("p t n -> p n t"), B[4][:, 0:384].rearrange("p (n t) -> p n t", n=8)),
                None, None,
                (sample_view_all(xe), B[1][:, 0:384].rearrange("p (m b c) -> p m b c", m=KI, b=NB)),
                (nT[:], B[0][:, 0:128].rearrange("p (i r) -> p i r", i=MH)),
            ]
            def norm(n):
                dve.wait_ge(s("std"), n + 1)
                link(dve.reciprocal(rstd, stdv))
                for k in range(KD):
                    stt(hT[:, k, :], xT[:, k, :], vecs[:, NORM[n] + k:NORM[n] + k + 1], rstd, ALU.mult, ALU.mult) \
                        .then_inc(s("h_norm"), 1)

            for n in range(7):
                dve.wait_ge(s("raw_tr"), n + 1)
                if n == 3:
                    for i in range(2):
                        for g in range(G):
                            ins = copy(wr[:, i, :, G + EPG * g:G + EPG * g + EPG],
                                       B[5][:, :].rearrange("p (e r k) -> p r k e", e=8, r=8)[:, 4 * i + g, :, :])
                elif n == 4:
                    for i in range(2):
                        ins = copy(wr[:, i, :, 0:G],
                                   B[6][:, 0:64].rearrange("p (g i k) -> p i k g", g=4, i=2)[:, i, :, :])
                else:
                    if n == 5:
                        dve.wait_ge(s("consts"), 5)
                    ins = copy(*raws[n])
                ins.then_inc(s("raw_out"), 1)
                if n == 0:
                    dve.wait_ge(s("raw_out"), 1)
                    norm(0)
            dve.wait_ge(s("raw_out"), 7)
            dve.wait_ge(s("consts"), 6)
            dve.tensor_reduce(gfold, ident[:, 0:96].rearrange("p (g c) -> p c g", g=3)[:, 0:8, :], AX.X, ALU.add) \
                .then_inc(s("gfold"), 1)
            W = XE - 3
            for m in range(KI):
                dve.wait_ge(s("xm_out"), 3 * m + 3)
                if m >= 2:
                    dve.wait_ge(s("xc"), 2 * m - 2)
                y = ctmp[:, m % 2, 0:W]
                link(ts(y, xe[:, m, 0:W], vec("mlstm_conv_w", m), vec("mlstm_conv_b", m), ALU.mult, ALU.add))
                for i in range(1, 4):
                    ins = stt(y, xe[:, m, i:i + W], vec("mlstm_conv_w", KI * i + m), y, ALU.mult, ALU.add)
                    if i < 3:
                        link(ins)
                ins.then_inc(s("conv"), 1)
            for m in range(KI):
                dve.wait_ge(s("qkv_mm"), m + 1)
                copy(kT[:, m, :], B[2 + m % 2][:, 0:NT]).then_inc(s("k_out"), 1)
            dve.wait_ge(s("xc"), 2 * KI)
            copy(cv27[:, :, 0:3], xe[:, :, NPROMPT:NPROMPT + 3]).then_inc(s("cv27"), 1)
            copy(cv27[:, :, 3:27].rearrange("p m (b c) -> p m b c", c=3), sample_view_all(xe, 4)).then_inc(s("cv27"), 1)
            for n in range(4):
                dve.wait_ge(s("cv_tr"), n + 1)
                copy(cvout[0:27, 512 * n:512 * n + 512], B[4 + n % 2][0:27, :]).then_inc(s("cv_out"), 1)
            gi, gf, tmp, lf, ones4, fs, a, ap = (gt[0:4, n, :] for n in (1, 2, 3, 4, 5, 6, 7, 8))
            radd = gt[0:4, 9, :]
            dve.wait_ge(s("gates_act"), 1)
            link(dve.memset(ones4, 1.0))
            link(dve.memset(radd, 0.0))
            link(dve.memset(gt[0:4, 5, NPROMPT:NT:SB], 0.0))
            link(dve.memset(gt[0:4, 9, NPROMPT:NT:SB], -1.0e38))
            dve.wait_ge(s("gates_act"), 3)
            link(ts(tmp, gf, -1.0, None, ALU.mult))
            tt(tmp, tmp, gf, ALU.max).then_inc(s("gates_dve"), 1)
            dve.wait_ge(s("gates_act"), 5)
            link(stt(lf, gf, 0.0, tmp, ALU.min, ALU.subtract))
            link(dve.tensor_tensor_scan(fs, ones4, lf, 0.0, ALU.mult, ALU.add))
            link(tt(a, gi, fs, ALU.subtract))
            link(copy(ap, a))
            link(tt(gt[0:4, 8, NPROMPT:NT:SB], gt[0:4, 7, NPROMPT:NT:SB], m0[:], ALU.max))
            Am = catA[:, 0:NT]
            link(dve.tensor_tensor_scan(Am, radd, ap, NEG, ALU.add, ALU.max))
            bs = "p (b s) -> p b s"
            Amb = catA[:, NPROMPT:NT].rearrange(bs, s=SB)
            Alast = catA[:, NPROMPT + 3:NT:SB]
            dve.wait_ge(s("consts"), 7)
            link(tt(catA[:, NT:NT + 8], m0[:], Alast, ALU.subtract))
            link(tt(catA[:, NT + 8:NT + 8 + NS].rearrange(bs, s=SB), m0[:].unsqueeze(2).to_broadcast([4, NB, SB]), Amb,
                    ALU.subtract))
            link(copy(rows[0:4, :], a))
            link(tt(rows[32:36, :], fs, Am, ALU.add))
            link(ts(rows[96:100, 0:NPROMPT], gt[0:4, 7, 0:NPROMPT], catA[:, NPROMPT - 1:NPROMPT], None, ALU.subtract))
            tt(rows[96:100, NPROMPT:NT].rearrange(bs, s=SB), gt[0:4, 7, NPROMPT:NT].rearrange(bs, s=SB),
               Alast.unsqueeze(2).to_broadcast([4, NB, SB]), ALU.subtract).then_inc(s("gates_dve"), 1)
            for half in range(2):
                copy(spread[0:NS, half, :].rearrange("p (b c s) -> p b c s", b=4, c=8),
                     ident[0:NS, 16 * half:16 * half + 16].rearrange("p (b s) -> p b s", b=4).unsqueeze(2)
                     .to_broadcast([NS, 4, 8, 4]))
            dve.tensor_reduce(fold, ident[:].rearrange("p (i s) -> p s i", i=4), AX.X, ALU.add)
            link(dve.tensor_reduce(prod, ident[:].rearrange("p (b c s) -> p c b s", b=4, c=8), AX.XY, ALU.add))
            link(dve.tensor_reduce(notp[:, 0:1], prod[:, 3:8], AX.X, ALU.add))
            link(dve.tensor_reduce(notp[:, 1:2], prod[:, 6:8], AX.X, ALU.add))
            link(dve.tensor_reduce(notp[:, 3:4], prod[:, 2:6:3], AX.X, ALU.add))
            link(dve.tensor_reduce(notp[:, 2:3], prod[:, 1:8:3], AX.X, ALU.add))
            link(tt(notp[:, 2:3], notp[:, 2:3], notp[:, 3:4], ALU.add))
            ts(notp, notp, -1.0, None, ALU.mult).then_inc(s("part_masks"), 1)
            dve.wait_ge(s("part_masks"), 1)
            dve.wait_ge(s("tm"), 10)

            for h in range(H):
                dve.wait_ge(s("k_mm"), h + 1)
                if h > 0:
                    dve.wait_ge(s("num_mm"), 2 * h)
                for j, (_, n) in enumerate(TOK):
                    ts(wk[0:n, j, :], B[1 + j][0:n, :], tm[0:n, j, 8 + h:9 + h], KSCALE, ALU.mult, ALU.mult) \
                        .then_inc(s("wk"), 1)
                if h == 0:
                    dve.wait_ge(s("cv_stored"), 32)
                for n in range(4):
                    dst = (wk8, v8)[n // 2]
                    f = notp[:, 2 * (n // 2):2 * (n // 2) + 2]
                    y, z = y16[:, n % 2, :], z1[:, n % 2, :]
                    dve.wait_ge(s("y1"), 4 * h + n + 1)
                    stt(z, y, f[:, 0:1], B[1 + n][:, :], ALU.mult, ALU.add).then_inc(s("z1"), 1)
                    dve.wait_ge(s("z1"), 4 * h + n + 1)
                    link(copy(y, z))
                    stt(dst[:, n % 2, :], y, f[:, 1:2], z, ALU.mult, ALU.add).then_inc(s("parts"), 1)
                    dve.wait_ge(s("parts"), 4 * h + n + 1)
                dve.wait_ge(s("bc_exp"), 2 * h + 2)
                dve.wait_ge(s("qz_zero"), 1)
                qi = qz[:, :, :].rearrange("p i (b x) -> p i b x", x=36)[:, :, :, 0:SB]
                q = qT[:, MH * h:MH * h + MH, NPROMPT:NT].rearrange("p i (b s) -> p i b s", s=SB)
                ib = ibc[:, h, :].rearrange(bs, s=SB)
                for i in range(MH):
                    ins = tt(qi[:, i], q[:, i], ib, ALU.mult)
                ins.then_inc(s("qz"), 1)
                dve.wait_ge(s("st_mm"), h + 1)
                dve.wait_ge(s("e_masked"), 3 * h + 3)
                for p, c0, c1 in ((P, 0, 256), (P, 256, 384), (NS, 384, 416)):
                    stt(stw[0:p, c0:c1], B[7][0:p, c0:c1], KSCALE, ew[0:p, c0:c1], ALU.mult, ALU.mult) \
                        .then_inc(s("stw"), 1)
                dve.wait_ge(s("stw"), 3 * h + 3)
                dve.wait_ge(s("qz"), 2 * h + 1)
                npr = ew[:, 0:128].rearrange("p (i b s) -> p i b s", i=MH, s=SB)
                for i in range(MH):
                    ins = tt(npr[:, i], qi[:, i],
                             nT[:, i, h:32:H].unsqueeze(2).to_broadcast([P, NB, SB]), ALU.mult)
                ins.then_inc(s("qz"), 1)
                dve.wait_ge(s("num_mm"), 2 * h + 1)
                for j in range(2):
                    link(ts(dden[:, j:j + 1], B[3][:, j:j + 1], -1.0, None, ALU.mult))
                    link(stt(dden[:, j:j + 1], dden[:, j:j + 1], tm[:, j, 4 + h:5 + h], B[3][:, j:j + 1],
                             ALU.max, ALU.max))
                dve.reciprocal(rden[:, 0:2], dden[:, 0:2]).then_inc(s("rden"), 1)
                dve.wait_ge(s("ns_mm"), h + 1)
                dve.wait_ge(s(f"n_landed{h % 2}"), 16 * (h // 2 + 1))
                stt(nrow[:, h % 2, :], nrow[:, h % 2, :], decn[:, h:h + 1], B[7][0:NB, :], ALU.mult, ALU.add) \
                    .then_inc(s("ns_out"), 1)
                for b in range(NB):
                    cpage = page("C", 4 * h + b // 2).rearrange("p (c v) -> p c v", v=DH)
                    for i in range(MH):
                        c = cpage[:, MH * (b % 2) + i, :]
                        n = (NB * h + b) * MH + i
                        dve.wait_ge(s("c_mm"), n + 1)
                        stt(c, c, decb[:, h, b:b + 1], B[UPD[i]][:, :], ALU.mult, ALU.add).then_inc(s("c_new"), 1)
                dve.wait_ge(s("num_mm"), 2 * h + 2)
                link(ts(dden[0:NS, 2:3], B[3][0:NS, 2:3], -1.0, None, ALU.mult))
                link(stt(dden[0:NS, 2:3], dden[0:NS, 2:3], tm[0:NS, 2, 4 + h:5 + h], B[3][0:NS, 2:3],
                         ALU.max, ALU.max))
                dve.reciprocal(rden[0:NS, 2:3], dden[0:NS, 2:3]).then_inc(s("rden"), 1)
            def hh(h, j):
                return hhp[h][:, j, :] if j < 2 else hhs[h][0:NS]

            dve.wait_ge(s("hh"), 3 * H)
            mean = rstd[:, 0:12]
            for h in range(H):
                for j, (_, n) in enumerate(TOK):
                    c = 3 * h + j
                    link(dve.bn_stats(lnst[0:n], hh(h, j)))
                    link(dve.bn_aggr(stdv[0:n, 2 * c:2 * c + 2], lnst[0:n]))
                    copy(mvsd[0:n, c:c + 1], stdv[0:n, 2 * c + 1:2 * c + 2]).then_inc(s("mv"), 1)
            dve.wait_ge(s("hsd"), 1)
            link(dve.reciprocal(mean, mvsd))
            for h in range(H):
                for j, (_, n) in enumerate(TOK):
                    c = 3 * h + j
                    ts(hh(h, j), hh(h, j), stdv[0:n, 2 * c:2 * c + 1], mean[0:n, c:c + 1], ALU.subtract, ALU.mult) \
                        .then_inc(s("hn"), 1)
            for m in range(KI):
                dve.wait_ge(s("hn_tr"), m + 1)
                dve.wait_ge(s("zs"), m + 1)
                t = (stdv, rstd)[m % 2]
                if m < 2:
                    dve.wait_ge(s("hn"), 3 * H)
                else:
                    dve.wait_ge(s("y_mix"), m - 1)
                ts(t, B[4 + m % 2][:, 0:NT], vec("mlstm_hn_w", m), None, ALU.mult).then_inc(s("y_in"), 1)
                dve.wait_ge(s("y_in"), m + 1)
                link(stt(t, xc[:, m, :], vec("mlstm_skip", m), t, ALU.mult, ALU.add))
                tt(xc[:, m, :], t, zs[:, m, :], ALU.mult).then_inc(s("y_mix"), 1)
            for m in range(KD):
                dve.wait_ge(s("down_mm"), m + 1)
                tt(xT[:, m, :], xT[:, m, :], B[m % 4][:, 0:NT], ALU.add).then_inc(s("down_add"), 1)

            def moe(L, base):
                norm(1 + 2 * L)

                def v3(o, n):
                    return rt[:, o:o + 3 * n].rearrange("p (j e) -> p j e", j=3)

                def bc(t, n):
                    return t.unsqueeze(2).to_broadcast([P, 3, n])

                def bj(t, n):
                    return t.unsqueeze(1).to_broadcast([P, 3, n])

                M, M0, M1 = v3(0, NE), v3(96, NE), v3(192, NE)
                lg, ge = v3(300, G), v3(320, G)
                gmax, gsum = rt[:, 312:315], rt[:, 332:335]
                diff, ediff = rt[:, 340:343], rt[:, 343:346]
                t1, t2 = rt[:, 346:349], rt[:, 349:352]
                lt = v3(400, 36)
                gm = v3(510, G)
                key = v3(530, NE)
                le = v3(630, NE)
                rank = v3(730, NE)
                nrep = rt[:, 830:990].rearrange("p (r e) -> p r e", r=ROUNDS)
                off = rt[:, 990:1150].rearrange("p (r e) -> p r e", r=ROUNDS)
                one160 = rt[:, 1150:1310]
                doff = rt[:, 1310:1470].rearrange("p (r e) -> p r e", r=ROUNDS)
                cnt = rt[:, 1470:1502]
                thr = rt[:, 1502:1507]
                pos = v3(1510, NE)
                tmp3 = v3(1610, NE)
                mx = rt[:, 1720:1721]
                rmax, rmin = rt[:, 1722:1725], rt[:, 1726:1729]

                dve.wait_ge(s("consts"), 6)
                link(dve.memset(rt, 0.0))
                dve.wait_ge(s("iota"), 3 * L + 3)
                dve.wait_ge(s("router_pe"), 2 * L + 1)
                for j, (_, n) in enumerate(TOK):
                    link(tt(lt[0:n, j, :], B[6][0:n, 36 * j:36 * j + 36], rbias[0:n, L, :], ALU.add))

                def first_max(out, val, vmax, idx, n):
                    link(dve.tensor_reduce(vmax, val, AX.X, ALU.max))
                    link(tt(out, val, bc(vmax, n), ALU.is_equal))
                    k = key[:, :, 0:n]
                    link(stt(k, out, -EARLIER, idx, ALU.mult, ALU.add))
                    link(dve.tensor_reduce(rmin, k, AX.X, ALU.min))
                    link(tt(out, k, bc(rmin, n), ALU.is_equal))

                first_max(gm, lt[:, :, 0:G], gmax, bj(iota32[:, 0:G], G), G)
                tt(lg, lt[:, :, 0:G], bc(gmax, G), ALU.subtract).then_inc(s("router_dve"), 1)
                link(ts(gm, gm, 1.0, 1.0e30, ALU.subtract, ALU.mult))
                for g in range(G):
                    link(tt(le[:, :, EPG * g:EPG * g + EPG], lt[:, :, G + EPG * g:G + EPG * g + EPG],
                            gm[:, :, g:g + 1].to_broadcast([P, 3, EPG]), ALU.add))
                idx32 = bj(iota32, NE)
                first_max(M0, le, rmax, idx32, NE)
                link(stt(le, M0, -2.0e30, le, ALU.mult, ALU.add))
                first_max(M1, le, t1, idx32, NE)
                tt(diff, t1, rmax, ALU.subtract).then_inc(s("router_dve"), 1)
                tt(M, M0, M1, ALU.add).then_inc(s("router_dve"), 1)
                dve.wait_ge(s("router_act"), 2 * L + 1)
                link(dve.tensor_reduce(gsum, ge, AX.X, ALU.add))
                dve.wait_ge(s("router_act"), 2 * L + 2)
                link(ts(t2, ediff, 1.0, None, ALU.add))
                link(tt(t2, t2, gsum, ALU.mult))
                link(dve.reciprocal(placew[:, 6:9], t2))
                link(tt(placew[:, 9:12], placew[:, 6:9], ediff, ALU.mult))
                dve.wait_ge(s("router_pe"), 2 * L + 2)
                link(copy(cnt, B[7][:, 96:128]))
                for j, (_, n) in enumerate(TOK):
                    link(copy(rank[0:n, j, :], B[7][0:n, 32 * j:32 * j + 32]))
                for r in range(ROUNDS):
                    link(ts(nrep[:, r, :], cnt, float(CAP * r), 0.0, ALU.subtract, ALU.max))
                link(ts(nrep, nrep, float(CAP), None, ALU.min))
                link(dve.memset(one160, 1.0))
                nflat, oflat = rt[:, 830:990], rt[:, 990:1150]
                link(dve.tensor_tensor_scan(oflat, one160, nflat, 0.0, ALU.mult, ALU.add))
                link(tt(oflat, oflat, nflat, ALU.subtract))
                link(dve.tensor_reduce(mx, cnt, AX.X, ALU.max))
                for r in range(ROUNDS):
                    link(ts(thr[:, r:r + 1], mx, float(CAP * r), None, ALU.is_gt))
                link(dve.tensor_reduce(rt[:, 1721:1722], thr, AX.X, ALU.add))
                dve.wait_ge(s("moe_add"), base * KD)
                link(dve.memset(table[:, ROUNDS * NE:ROUNDS * NE + 1], 0))
                link(copy(table[:, 0:ROUNDS * NE], rt[0:1, 990:1150]))
                link(ts(table[:, ROUNDS * NE + 2:ROUNDS * NE + 3], rt[0:1, 1721:1722], float(NE // 2), -1.0, ALU.mult,
                        ALU.add))
                copy(table[:, ROUNDS * NE + 1:ROUNDS * NE + 2], rt[0:1, 1721:1722]).then_inc(s("table"), 1)
                link(tt(doff[:, 1:ROUNDS, :], off[:, 1:ROUNDS, :], off[:, 0:ROUNDS - 1, :], ALU.subtract))
                link(ts(doff[:, 1:ROUNDS, :], doff[:, 1:ROUNDS, :], float(CAP), None, ALU.subtract))
                link(tt(pos, rank, bj(off[:, 0, :], NE), ALU.add))
                for r in range(1, ROUNDS):
                    link(stt(tmp3, rank, float(CAP * r), bj(doff[:, r, :], NE), ALU.is_ge, ALU.mult))
                    link(tt(pos, pos, tmp3, ALU.add))
                for n, m in enumerate((M0, M1)):
                    link(tt(tmp3, pos, m, ALU.mult))
                    dve.tensor_reduce(slotw[:, 3 * n:3 * n + 3], tmp3, AX.X, ALU.add).then_inc(s("slots"), 1)
                    dve.wait_ge(s("slots"), 2 * L + n + 1)
                for j, (_, n) in enumerate(TOK):
                    link(ts(sel[0:n, j, :], iota[0:n], slotw[0:n, j:j + 1], None, ALU.is_equal))
                    stt(sel[0:n, j, :], iota[0:n], slotw[0:n, 3 + j:4 + j], sel[0:n, j, :], ALU.is_equal, ALU.add) \
                        .then_inc(s("sel"), 1)
                link(stt(pos, idx32, float(CAP), rank, ALU.mult, ALU.add))
                for r in range(1, ROUNDS):
                    link(ts(tmp3, rank, float(CAP * r), float(CAP * (NE - 1)), ALU.is_ge, ALU.mult))
                    link(tt(pos, pos, tmp3, ALU.add))
                link(tt(tmp3, pos, M0, ALU.mult))
                link(dve.tensor_reduce(placew[:, 0:3], tmp3, AX.X, ALU.add))
                link(tt(tmp3, pos, M1, ALU.mult))
                dve.tensor_reduce(placew[:, 3:6], tmp3, AX.X, ALU.add).then_inc(s("placew"), 1)
                for n in range(0, 16, 2):
                    c, m = divmod(n, 8)
                    dve.wait_ge(s("gather_mm"), 16 * L + n + 1)
                    copy(xsT[:, m, NT * c:NT * c + NT], B[n % 6][:, 0:NT]).then_inc(s("xs_b"), 1)
                for n in range(4):
                    dve.wait_ge(s("tokrow_mm"), 4 * L + n + 1)
                    copy(tokrow[:, n, :], B[6 + n % 2][:, 0:NT]).then_inc(s("tokrow"), 1)
                dve.wait_ge(s("tokrow"), 4 * L + 4)
                dve.wait_ge(s("xs_a"), 8 * L + 8)
                dve.wait_ge(s("xs_b"), 8 * L + 8)
                dve.wait_ge(s("xs_pad"), L + 1)
                dve.wait_ge(s("table"), L + 1)
                rounds = dve.value_load(table[0:1, ROUNDS * NE + 1:ROUNDS * NE + 2], min_val=1, max_val=ROUNDS)

                def fetch(n, j):
                    o = dve.value_load(table[0:1, bass.ds(n, 1)], min_val=0, max_val=NSLOT)
                    copy(xcx[:, j, :].rearrange("p (k c) -> p k c", k=KD), xsT[:, :, bass.ds(o, CAP)]) \
                        .then_inc(s(f"xcx{j}"), 1)

                fetch(0, 0)
                with dve.Fori(0, rounds * 16) as i:
                    it = i + base
                    for j in range(2):
                        dve.wait_ge(s(f"gu_mm{1 - j}"), it + j)
                        fetch(2 * i + (j + 1), 1 - j)
                        dve.wait_ge(s(f"sg{j}"), it + 1)
                        tt(hx[CAP:P, j, :], sg[CAP:P, j, :], B[j][CAP:P, :], ALU.mult).then_inc(s(f"hx{j}"), 1)
                    for j in range(2):
                        dve.wait_ge(s(f"ht_tr{j}"), it + 1)
                        copy(hxT[:, j, :], B[4 + 3 * j][:, 0:MF * CAP]).then_inc(s(f"ht{j}"), 1)
                    dve.wait_ge(s("scatter_mm"), it * KD)
                    place_n = rowplace[:, bass.ds(i, 1)]
                    stt(wpart, tokrow[:, 0, :], place_n, tokrow[:, 2, :], ALU.is_equal, ALU.mult) \
                        .then_inc(s("wparts"), 1)
                    stt(wpair, tokrow[:, 1, :], place_n, tokrow[:, 3, :], ALU.is_equal, ALU.mult) \
                        .then_inc(s("wparts"), 1)
                    dve.wait_ge(s("wparts"), it * 2 + 2)
                    tt(wpair, wpair, wpart, ALU.add).then_inc(s("wpair"), 1)
                    for m in range(KD):
                        dve.wait_ge(s("scatter_mm"), it * KD + (m + 1))
                        tt(xT[:, m, :], xT[:, m, :], B[5 + m % 2][:, 0:NT], ALU.add).then_inc(s("moe_add"), 1)
                return base + rounds * 16

            turns = moe(0, 0)
            norm(2)
            for n in range(2):
                dve.wait_ge(s("ws_tr"), n + 1)
                copy(wsT[:, 4 * n:4 * n + 4, :], B[4 + n][:, :].rearrange("p (g t) -> p g t", g=4)) \
                    .then_inc(s("ws_out"), 1)
            dve.wait_ge(s("consts"), 1)
            copy(rep[0:4, :].rearrange("p (b s) -> p b s", s=SB), ident[0:4, 0:4].unsqueeze(1).to_broadcast([4, NB, SB])) \
                .then_inc(s("rep"), 1)
            for n in range(12):
                c, j = divmod(n, 3)
                t = TOK[j][1]
                dve.wait_ge(s("vtok_mm"), n + 1)
                copy(vtk[0:t, j, 512 * c:512 * c + 512], B[4 + n % 4][0:t, :]).then_inc(s("vtk"), 1)
                dve.wait_ge(s("vtk"), n + 1)
                link(dve.bn_stats(bnst[0:t, j, 6 * c:6 * c + 6], vtk[0:t, j, 512 * c:512 * c + 512]))
                if c == 3:
                    dve.bn_aggr(mvc[0:t, j, :], bnst[0:t, j, :]).then_inc(s("vstat"), 1)
            dve.wait_ge(s("ln_landed"), 32)
            for j, (_, n) in enumerate(TOK):
                dve.wait_ge(s("vsd"), j + 1)
                link(dve.reciprocal(mvc[0:n, j, 1:2], mvc[0:n, j, 1:2]))
                link(ts(vtk[0:n, j, :], vtk[0:n, j, :], mvc[0:n, j, 0:1], mvc[0:n, j, 1:2], ALU.subtract, ALU.mult))
                link(tt(vtk[0:n, j, :], vtk[0:n, j, :], lnwb[0:n, 0, :], ALU.mult))
                tt(vtk[0:n, j, :], vtk[0:n, j, :], lnwb[0:n, 1, :], ALU.add).then_inc(s("v_norm"), 1)
            dve.wait_ge(s("wsS_mm"), 1)
            tt(wsS[0:NS].rearrange("p g (b t) -> p g b t", t=SB),
               B[4][0:NS, 0:CG * SB].rearrange("p (g t) -> p g t", t=SB).unsqueeze(2).to_broadcast([NS, CG, NB, SB]),
               bmask[0:NS, 0:NB].unsqueeze(1).unsqueeze(3).to_broadcast([NS, CG, NB, SB]), ALU.mult) \
                .then_inc(s("wsS"), 1)
            dve.wait_ge(s("bs_landed"), 16)
            for m in range(KI):
                g = m // 2
                dve.wait_ge(s("mix_mm"), m + 1)
                dve.wait_ge(s("gelu"), KI + m + 1)
                link(tt(mixt[:, 0:256].rearrange("p (j t) -> p j t", j=2), B[4 + m % 4][:, 0:256].rearrange("p (j t) -> p j t", j=2),
                        bsb[:, g, :].unsqueeze(1).to_broadcast([P, 2, P]), ALU.add))
                link(tt(mixt[:, 256:NT].rearrange(bs, s=SB), B[4 + m % 4][:, 256:NT].rearrange(bs, s=SB),
                        bsb[:, g, 0:SB].unsqueeze(1).to_broadcast([P, NB, SB]), ALU.add))
                ins = tt(uT[:, m, :], uT[:, m, :], mixt, ALU.mult)
                ins.then_inc(s("mixed"), 1)
                dve.wait_ge(s("mixed"), m + 1)
            for m in range(KD):
                dve.wait_ge(s("out_mm"), m + 1)
                stt(xT[:, m, :], B[m % 4][:, 0:NT], vec("cmlp_b_out", m), xT[:, m, :], ALU.add, ALU.add) \
                    .then_inc(s("out_add"), 1)
            moe(1, turns)
            norm(4)


def sample_view_all(xe, first=0):
    return xe[:, :, XS:XE].rearrange("p m (b x) -> p m b x", x=7)[:, :, :, first:first + 3]


_INS = ["x_prompt", "x_sample", "state_mlstm_C", "state_mlstm_n", "state_mlstm_m", "state_mlstm_conv",
        "norm_mix", "norm_ffn", "norm_final", "mlstm_w_up", "mlstm_conv_w", "mlstm_conv_b", "mlstm_w_q", "mlstm_w_k",
        "mlstm_w_v", "mlstm_w_ig", "mlstm_b_ig", "mlstm_w_fg", "mlstm_b_fg", "mlstm_skip", "mlstm_hn_w",
        "mlstm_w_down", "cmlp_w_in", "cmlp_b_in", "cmlp_ln_w", "cmlp_ln_b", "cmlp_w_s", "cmlp_b_s", "cmlp_w_out",
        "cmlp_b_out", "moe_w_rg", "moe_b_rg", "moe_w_re", "moe_b_re", "moe_w_gate", "moe_w_up", "moe_w_down"]
_OUTS = [("y_p", (1, NPROMPT, D)), ("y_s", (NB, SB, D)), ("C_p", (1, 1, H, DH, DH)), ("n_p", (1, 1, H, DH)),
         ("m_p", (1, 1, H)), ("conv_p", (1, 1, 3, INNER)), ("C_s", (1, NB, H, DH, DH)), ("n_s", (1, NB, H, DH)),
         ("m_s", (1, NB, H)), ("conv_s", (1, NB, 3, INNER)), ("v_s", (1, NB, SB, INNER))]


def kernel(**inputs):
    import numpy as _np
    import concourse.bacc as _bacc
    from concourse import mybir as _mybir
    from concourse.bass_utils import run_bass_kernel_spmd as _run

    nc = _bacc.Bacc("TRN2", target_bir_lowering=False, num_devices=1)
    arrays, ins, outs = {}, {}, {}
    for name in _INS:
        a = _np.ascontiguousarray(inputs[name])
        arrays[f"in_{name}"] = a
        ins[name] = nc.dram_tensor(f"in_{name}", a.shape, _mybir.dt.from_np(a.dtype), kind="ExternalInput").ap()
    for name, shape in _OUTS:
        outs[name] = nc.dram_tensor(f"out_{name}", shape, F32, kind="ExternalOutput").ap()
    build(nc, ins, outs)
    r = _run(nc, [arrays], core_ids=[0])
    return tuple(r.results[0][f"out_{name}"] for name, _ in _OUTS)
```

```python
from contextlib import ExitStack

import concourse.bass as bass
from concourse import mybir

F32 = mybir.dt.float32
BF16 = mybir.dt.bfloat16
I32 = mybir.dt.int32
ALU = mybir.AluOpType
ACT = mybir.ActivationFunctionType
AX = mybir.AxisListType

P = 128
D = 1024
KD = D // P
NPROMPT = 256
NB = 8
SB = 4
NS = NB * SB
NT = NPROMPT + NS
TOK = [(0, 128), (128, 128), (256, NS)]
INNER = 2048
KI = INNER // P
H = 4
DH = INNER // H
MH = DH // P
XE = 3 + NPROMPT + NB * 7
XS = 3 + NPROMPT
KSCALE = DH ** -0.5
G = 4
EPG = 8
NE = G * EPG
F = 512
MF = F // P
CAP = 64
ROUNDS = -(-NT // CAP)
NSLOT = 2 * NT
SLOTS = NSLOT + CAP
GATHER = [n % 6 for n in range(8)] + [(0, 1, 5, 6)[n % 4] for n in range(8)]
SCATTER = (5, 6, 4)
CG = 8
PAGE = 4096
RING = 6
NEG = -1.0e30
ZLAG = 9
UPD = [(5, 6, 1, 2)[n % 4] for n in range(28)] + [5, 6, 5, 6]
UPD_BEFORE = [max([m for m in range(n) if UPD[m] == UPD[n]], default=None) for n in range(32)]
SPREAD = (1, 2, 3, 0)
EARLIER = 1024.0


def build(nc, A, O):
    with ExitStack() as ctx:
        def sb(name, shape, dt=F32):
            return ctx.enter_context(nc.sbuf_tensor(name, shape, dt))

        sems = {}

        def s(name):
            if name not in sems:
                sems[name] = ctx.enter_context(nc.semaphore("s_" + name))
            return sems[name]

        def at(t, off, *dims):
            n = 1
            for d in dims:
                n *= d
            v = t[:, off:off + n]
            if len(dims) == 1:
                return v
            if len(dims) == 2:
                return v.rearrange("p (a b) -> p a b", b=dims[1])
            return v.rearrange("p (a b c) -> p a b c", b=dims[1], c=dims[2])

        B = [ctx.enter_context(nc.psum_tensor(f"bank{i}", [P, 512], F32)) for i in range(8)]
        xT = sb("xT", [P, KD, NT])
        hT = sb("hT", [P, KD, NT])
        ident = sb("ident", [P, P])
        ones = sb("ones", [P, P])
        before = sb("before", [P, P])
        bmask = sb("bmask", [P, 32])
        vecs = sb("vecs", [P, 192])
        wif = sb("wif", [P, 48, 8])
        wr = sb("wr", [P, 2, KD, 36])
        rbias = sb("rbias", [P, 2, 36])
        scratch = sb("scratch", [P, 2 * NT])
        stdv, rstd = scratch[:, 0:NT], scratch[:, NT:2 * NT]
        xms = at(scratch, 0, KI, NS)
        nT = sb("nT", [P, MH, 32])
        rows = sb("rows", [P, NT])
        catA = sb("catA", [4, NT + 8 + NS])
        tm = sb("tm", [P, 3, 12])
        decb = sb("decb", [P, H, NB])
        ibc = sb("ibc", [P, H, NS])
        decn = sb("decn", [NB, H])
        m0 = sb("m0", [4, NB])
        gb = sb("gb", [4, 2])
        nrow = sb("nrow", [NB, 2, DH])
        nst = sb("nst", [1, DH])
        small = sb("small", [P, 64])
        eps6, eps5 = small[:, 0:1], small[:, 1:2]
        rden = small[:, 2:5]
        dden = small[:, 5:8]
        slotw = small[:, 8:20]
        mvsd = small[:, 20:32]
        gfold = small[:, 50:58]
        placew = small[:, 38:50]
        lnst = small[:, 32:38]
        table = sb("table", [1, ROUNDS * NE + 8], I32)
        arena = sb("arena", [P, 18864])
        ring = sb("ring", [P, RING, PAGE])

        xe = at(arena, 0, KI, XE)
        xc = at(arena, 5040, KI, NT)
        qT = at(arena, 9648, KI, NT)
        kT = at(arena, 14256, KI, NT)
        hhp = [at(arena, 14256 + h * MH * NT, 2, DH) for h in range(H)]
        hhs = [at(arena, 9648 + h * MH * NT, DH) for h in range(H)]
        zs = at(arena, 0, KI, NT)
        xtok = at(arena, 9648, 3, D)
        raw_re = at(arena, 12720, 1024)
        raw_rg = at(arena, 13744, 512)
        raw_if = at(arena, 14256, 2, 512)
        raw_qkv = at(arena, 15280, 512)
        raw_vec = at(arena, 15792, 2, P)
        raw_conv = at(arena, 16048, INNER)
        high = ring[:, 3:6, :].rearrange("p a b -> p (a b)")
        bd = at(high, 0, 3, KI, P)
        z1 = at(high, 0, 2, DH)
        snum = at(high, 1024, DH)
        wk8 = at(high, 2048, 512).bitcast(BF16).rearrange("p (a d) -> p a d", a=2)
        v8 = at(high, 2560, 512).bitcast(BF16).rearrange("p (a d) -> p a d", a=2)
        y16 = at(high, 3072, 512).bitcast(BF16).rearrange("p (a d) -> p a d", a=2)
        spread = at(high, 3584, 2, P)
        fold = at(high, 3840, NS)
        prod = at(high, 3872, 8)
        notp = at(high, 3880, 4)
        cvout = at(high, 0, INNER)
        vtok = at(high, 6144, 3, DH)
        wk = at(high, 7680, 3, DH)
        gt = at(high, 6144, 10, NT)
        stw = at(high, 9216, 416)
        ew = at(high, 9632, 416)
        ctmp = at(high, 9216, 2, 315)
        cv27 = at(high, 9216, KI, 27)
        qz = at(high, 10048, MH, NT)
        vtr = at(high, 10048, 2, NT)
        wqkv = at(high, 10048 + 576, 4, 48)
        nraw = at(high, 11200, 512)
        cst = at(high, 11200, 2, DH)
        xsT = at(arena, 0, KD, SLOTS)
        htok = at(arena, 5120, 3, D)
        sg = at(arena, 16432, 2, F)
        hx = at(arena, 17456, 2, F)
        ysb = at(arena, 7168, D)
        rt = at(arena, 8192, 2048)
        sel = at(arena, 10240, 3, NSLOT)
        tokrow = at(arena, 11968, 4, NT)
        wpart = at(arena, 13120, NT)
        wpair = at(arena, 13408, NT)
        xcx = at(arena, 13696, 2, KD * CAP)
        hxT = at(arena, 14720, 2, MF * CAP)
        iota = at(arena, 15744, NSLOT)
        iota32 = at(arena, 16320, NE)
        rowplace = at(arena, 16352, ROUNDS * NE // 2)
        uT = at(arena, 0, KI, NT)
        vT = at(arena, 4608, KI, NT)
        lnwb = at(arena, 4608, 2, INNER)
        vtk = at(arena, 9216, 3, INNER)
        raw_ws = at(arena, 9216, CG, P)
        wsT = at(arena, 15360, CG, P)
        bsb = at(arena, 16384, CG, P)
        wsS = at(arena, 17408, CG, NS)
        rep = at(arena, 17664, 32)
        mixt = at(arena, 17696, NT)
        bnst = at(arena, 17984, 3, 4 * 6)
        mvc = at(arena, 18056, 3, 2)
        ytok = at(arena, 0, 3, D)

        V = {}
        vec_rows = [("norm_mix", 16), ("norm_ffn", 16), ("norm_final", 8), ("mlstm_conv_w", 64), ("mlstm_conv_b", 16),
                    ("cmlp_b_out", 8), ("mlstm_skip", 16), ("mlstm_hn_w", 16), ("cmlp_b_in", 32)]
        c = 0
        for name, n in vec_rows:
            V[name] = c
            c += n

        def vec(name, k):
            return vecs[:, V[name] + k:V[name] + k + 1]

        NORM = [V["norm_mix"], V["norm_ffn"], V["norm_mix"] + 8, V["norm_ffn"] + 8, V["norm_final"]]

        place = {}
        count = [0] * RING
        for key, slots in (("up", [0, 1, 2, 0]), ("z", [2, 0, 1, 3]),
                           ("down", [4, 5, 3, 4]), ("in", [0, 1, 2, 3, 4, 5, 0, 1]), ("out", [2, 3, 4, 5])):
            for j, slot in enumerate(slots):
                count[slot] += 1
                place[key, j] = (slot, 16 * count[slot])

        def page(key, j):
            return ring[:, place[key, j][0], :]

        def landed(eng, key, j):
            slot, n = place[key, j]
            eng.wait_ge(s(f"page_landed{slot}"), n)

        def expert_pages(j):
            return (ring[:, 2 * j, :].rearrange("p (k f) -> p k f", k=KD),
                    ring[:, 2 * j + 1, :].rearrange("p (k f) -> p k f", k=KD),
                    ring[:, 4 + j, :].rearrange("p (k f) -> p k f", k=MF))

        def state(t, q):
            return t[0, q % NB, q // NB].rearrange("(i p) v -> p i v", p=P)

        def cview(q):
            o = PAGE // 2 * (q % 2)
            return ring[:, ((2 + q) % 6) // 2, o:o + PAGE // 2].rearrange("p (i v) -> p i v", v=DH)

        def sample_view(t):
            return t[:, XS:XE].rearrange("p (b x) -> p b x", x=7)

        block = ctx.enter_context(nc.Block())

        @block.sync
        def _(sp):
            def load(key, j, src, dst=None):
                slot, _ = place[key, j]
                sp.dma_start(page(key, j) if dst is None else dst, src).then_inc(s(f"page_landed{slot}"), 16)

            w_up = A["mlstm_w_up"][0].rearrange("(k p) n -> p k n", p=P)
            w_dn = A["mlstm_w_down"][0].rearrange("(k p) n -> p k n", p=P)
            w_in = A["cmlp_w_in"][0].rearrange("(k p) n -> p k n", p=P)
            w_out = A["cmlp_w_out"][0].rearrange("(k p) n -> p k n", p=P)

            def k8(v):
                return v.rearrange("p (k n) -> p k n", k=KD)

            def k16(v):
                return v.rearrange("p (k n) -> p k n", k=KI)

            def load_state(q):
                sp.dma_start(cview(q), state(A["state_mlstm_C"], q)).then_inc(s(f"c_landed{q % 6}"), 16)

            for j, (t0, n) in enumerate(TOK):
                src = A["x_prompt"][0, t0:t0 + n, :] if j < 2 else A["x_sample"].rearrange("b s n -> (b s) n")
                sp.dma_start(xtok[0:n, j, :], src).then_inc(s("x_landed"), 16)
            for name, n in vec_rows:
                c0 = V[name]
                half, r0 = (0, c0) if c0 < 128 else (1, c0 - 128)
                a = A[name]
                flat = a if len(a.shape) == 1 else a.rearrange({2: "a b -> (a b)", 3: "a b c -> (a b c)"}[len(a.shape)])
                sp.dma_start(raw_vec[r0:r0 + n, half, :], flat.rearrange("(r p) -> r p", p=P)) \
                    .then_inc(s("vec_landed"), 16)
            def load_z(j):
                load("z", j, w_up[:, :, 2048 + 512 * j:2560 + 512 * j], k8(page("z", j)))

            for j in range(3):
                load("up", j, w_up[:, :, 512 * j:512 * j + 512], k8(page("up", j)))
            sp.wait_ge(s("xm_mm"), 4)
            load("up", 3, w_up[:, :, 1536:2048], k8(page("up", 3)))
            for q in range(6):
                sp.wait_ge(s("xm_mm"), 4 * (q // 2 + 2))
                load_state(q)
            for q in range(NB * H + 1):
                if q < NB * H:
                    sp.wait_ge(s("c_new"), MH * (q + 1))
                    sp.dma_start(state(O["C_s"], q), cview(q)).then_inc(s(f"c_stored{q % 2}"), 16)
                if q > 0:
                    r = q - 1
                    sp.wait_ge(s(f"c_stored{r % 2}"), 16 * (r // 2 + 1))
                    if r + 6 < NB * H:
                        load_state(r + 6)
                    elif r % 2 == 1:
                        load_z((r - 27) // 2)
            sp.wait_ge(s("num_mm"), 2 * H)
            for i in range(2):
                sp.wait_ge(s(f"cp_stored{i}"), 16 * 8)
            sp.wait_ge(s("cv_stored"), 32)
            load_z(3)
            for j in range(4):
                if j == 2:
                    sp.wait_ge(s("z_mm"), 16)
                elif j == 3:
                    sp.wait_ge(s("down_mm"), 2)
                load("down", j, w_dn[:, :, 256 * j:256 * j + 256], k16(page("down", j)))
            def experts(L, base):
                gate = A["moe_w_gate"].rearrange("i g e (k p) f -> (i g e) p k f", p=P)
                up = A["moe_w_up"].rearrange("i g e (k p) f -> (i g e) p k f", p=P)
                down = A["moe_w_down"].rearrange("i g e (k p) n -> (i g e) p k n", p=P)
                before_loop = {0: ("z_mm", 8), 1: ("z_mm", 12), 2: ("z_mm", 4), 3: ("down_mm", 6), 4: ("down_mm", 8),
                               5: ("down_mm", 4)} if L == 0 else \
                    {0: ("in_mm", 28), 1: ("in_mm", 32), 2: ("out_mm", 2), 3: ("out_mm", 4), 4: ("out_mm", 6),
                     5: ("out_mm", 8)}

                def turn(it, pair):
                    (g0, u0, d0), (g1, u1, d1) = expert_pages(0), expert_pages(1)
                    for slot, (dst, src, used) in enumerate((
                            (g0, gate, "gu_mm0"), (u0, up, "gu_mm0"), (g1, gate, "gu_mm1"), (u1, up, "gu_mm1"),
                            (d0, down, "y_mm"), (d1, down, "y_mm"))):
                        j = slot // 2 if slot < 4 else slot - 4
                        if slot in before_loop:
                            sp.wait_ge(s(before_loop[slot][0]), before_loop[slot][1])
                        sp.wait_ge(s(used), it)
                        if slot < 4:
                            sp.dma_start(dst, src[bass.ds(L * NE + 2 * pair + j, 1)].rearrange("a p k f -> p (a k) f")) \
                                .then_inc(s(f"expert_landed{slot}"), 16)
                    for half in range(2):
                        for j, dst in enumerate((d0, d1)):
                            src = down[bass.ds(L * NE + 2 * pair + j, 1)].rearrange("a p k f -> p (a k) f")
                            sp.dma_start(dst[:, 2 * half:2 * half + 2, :], src[:, 2 * half:2 * half + 2, :]) \
                                .then_inc(s(f"expert_landed{4 + 2 * half + j}"), 16)

                with sp.Fori(0, 15) as i:
                    turn(i + base, i)
                sp.wait_ge(s("table"), L + 1)
                rounds = sp.value_load(table[0:1, ROUNDS * NE + 1:ROUNDS * NE + 2], min_val=1, max_val=ROUNDS)
                with sp.Fori(15, rounds * 16) as i:
                    turn(i + base, i % 16)
                return base + rounds * 16

            turns = experts(0, 0)
            for j in range(8):
                if j < 6:
                    sp.wait_ge(s(("gu_mm0", "gu_mm1", "y_mm")[j // 2]), turns)
                else:
                    sp.wait_ge(s("in_mm"), 4 * (j - 5))
                c = 512 * ((j + 4) % 8)
                load("in", j, w_in[:, :, c:c + 512], k8(page("in", j)))
                if j == 3:
                    sp.wait_ge(s("moe_add"), turns * KD)
                    sp.dma_start(raw_ws, A["cmlp_w_s"][0].rearrange("g t s -> t g s")).then_inc(s("ws_landed"), 16)
                    sp.dma_start(bsb.rearrange("p g t -> p (g t)"),
                                 A["cmlp_b_s"].rearrange("o g t -> o (g t)").to_broadcast([P, CG * P])) \
                        .then_inc(s("bs_landed"), 16)
            for j in range(4):
                sp.wait_ge(s("in_mm"), 4 * (j + 3))
                load("out", j, w_out[:, :, 256 * j:256 * j + 256], k16(page("out", j)))
                if j == 1:
                    sp.wait_ge(s("vtok_mm"), 12)
                    for n, name in enumerate(("cmlp_ln_w", "cmlp_ln_b")):
                        sp.dma_start(lnwb[:, n, :], A[name].to_broadcast([P, INNER])).then_inc(s("ln_landed"), 16)
            experts(1, turns)
            for j in range(2):
                sp.wait_ge(s("y_ready"), 2 * j + 2)
                sp.dma_start(O["y_p"][0, P * j:P * j + P, :], ytok[:, j, :]).then_inc(s("y_stored"), 16)
            sp.wait_ge(s("y_ready"), 6)
            sp.dma_start(O["y_s"].rearrange("b s n -> (b s) n"), ytok[0:NS, 2, :]).then_inc(s("y_stored"), 16)
            sp.wait_ge(s("y_stored"), 48)
            sp.wait_ge(s("np_stored"), 16 * H)

        @block.gpsimd
        def _(pool):
            chain = [0]

            def link(ins):
                chain[0] += 1
                ins.then_inc(s("pool_chain"), 1)
                pool.wait_ge(s("pool_chain"), chain[0])

            def keep(t, pattern, base, mult, fill=0.0, op=ALU.is_ge):
                return pool.affine_select(out=t, in_=t, compare_op=op, fill=fill, base=base,
                                          pattern=pattern, channel_multiplier=mult)

            link(pool.memset(ident[:], 0.0))
            keep(ident[:], [[-1, P]], 0, 1, 1.0, ALU.not_equal).then_inc(s("consts"), 1)
            pool.memset(ones[:], 1.0).then_inc(s("consts"), 1)
            link(pool.memset(bmask[:], 1.0))
            link(keep(bmask[:], [[-4, 32]], 0, 1))
            keep(bmask[:], [[4, 32]], 3, -1).then_inc(s("consts"), 1)
            link(pool.memset(before[:], 1.0))
            keep(before[:], [[1, P]], -1, -1).then_inc(s("consts"), 1)
            pool.memset(xe[:, :, 0:3], 0.0).then_inc(s("consts"), 1)
            link(pool.memset(small[:], 0.0))
            link(pool.memset(eps6, 1e-6))
            pool.memset(eps5, 1e-5).then_inc(s("consts"), 1)
            pool.memset(rows[:], 0.0).then_inc(s("consts"), 1)
            pool.memset(gt[0:96, 0, :], 0.0).then_inc(s("consts"), 1)
            pool.wait_ge(s("consts"), 3)
            pool.wait_ge(s("raw_out"), 2)
            for n in range(3):
                for i in range(4):
                    pool.tensor_tensor(
                        bd[:, n, :, :].rearrange("p m (n d) -> p m n d", d=4)[:, :, :, i],
                        wqkv[:, i, 16 * n:16 * n + 16].unsqueeze(2).to_broadcast([P, KI, 32]),
                        bmask[:].unsqueeze(1).to_broadcast([P, KI, 32]), ALU.mult).then_inc(s("bd"), 1)
            pool.wait_ge(s("gate_part"), KI)
            pool.wait_ge(s("bd"), 12)
            pool.memset(qz, 0.0).then_inc(s("qz_zero"), 1)
            n_in = A["state_mlstm_n"][0].rearrange("b h d -> h b d")
            n_out = O["n_s"][0].rearrange("b h d -> h b d")
            for h in range(2):
                pool.dma_start(nrow[:, h, :], n_in[h]).then_inc(s(f"n_landed{h}"), 16)
            pool.wait_ge(s("cv_out"), 4)
            pool.dma_start(O["conv_p"][0, 0], cvout[0:3]).then_inc(s("cv_stored"), 16)
            pool.dma_start(O["conv_s"][0].rearrange("b c n -> (b c) n"), cvout[3:27]).then_inc(s("cv_stored"), 16)
            pool.wait_ge(s("gates_dve"), 2)
            pool.dma_start(O["m_p"][0].rearrange("o h -> h o"), rows[32:36, NPROMPT - 1:NPROMPT],
                           allow_slow_non_contiguous=True).then_inc(s("m_stored"), 16)
            pool.dma_start(O["m_s"][0].rearrange("b h -> h b"), rows[32:36, NPROMPT + 3:NT:SB],
                           allow_slow_non_contiguous=True).then_inc(s("m_stored"), 16)
            for h in range(H):
                pool.wait_ge(s("e_ready"), 3 * (h + 1))
                keep(ew[:, 0:128], [[1, P]], 0, -1).then_inc(s("e_masked"), 1)
                keep(ew[:, 256:384], [[1, P]], 0, -1).then_inc(s("e_masked"), 1)
                es = ew[0:NS, 384:416].rearrange("p (b t) -> p b t", t=SB)
                link(keep(es, [[SB, NB], [1, SB]], 0, -1))
                keep(es, [[-SB, NB], [0, SB]], 0, 1).then_inc(s("e_masked"), 1)
                pool.wait_ge(s("ns_out"), h + 1)
                pool.dma_start(n_out[h], nrow[:, h % 2, :]).then_inc(s(f"n_stored{h % 2}"), 16)
                if h + 2 < H:
                    pool.wait_ge(s(f"n_stored{h % 2}"), 16 * (h // 2 + 1))
                    pool.dma_start(nrow[:, h % 2, :], n_in[h + 2]).then_inc(s(f"n_landed{h % 2}"), 16)
            for i in range(2):
                pool.wait_ge(s(f"n_stored{i}"), 32)
            pool.wait_ge(s("m_stored"), 32)
            for L in range(2):
                pool.wait_ge(s(("down_add", "out_add")[L]), KD)
                pool.iota(iota, [[1, NSLOT]], base=0, channel_multiplier=0,
                          allow_small_or_imprecise_dtypes=True).then_inc(s("iota"), 1)
                pool.iota(iota32, [[1, NE]], base=0, channel_multiplier=0,
                          allow_small_or_imprecise_dtypes=True).then_inc(s("iota"), 1)
                pool.iota(rowplace, [[2 * CAP, ROUNDS * NE // 2]], base=0, channel_multiplier=1,
                          allow_small_or_imprecise_dtypes=True).then_inc(s("iota"), 1)
                pool.wait_ge(s("iota"), 3 * L + 3)
                pool.memset(xsT[:, :, NSLOT:SLOTS], 0.0).then_inc(s("xs_pad"), 1)
                if L == 0:
                    pool.wait_ge(s("ws_out"), 2)
                    keep(wsT, [[0, CG], [1, P]], 0, -1).then_inc(s("ws_masked"), 1)
                    pool.wait_ge(s("v_norm"), 3)
                    pool.dma_start(O["v_s"][0].rearrange("b s n -> (b s) n"), vtk[0:NS, 2, :]).then_inc(s("v_stored"), 16)
                    pool.wait_ge(s("v_stored"), 16)

        @block.scalar
        def _(act):

            def get(dst, src):
                act.dma_start(dst, src, allow_slow_non_contiguous=True).then_inc(s("raw_landed"), 16)

            for n, name in enumerate(("mlstm_w_q", "mlstm_w_k", "mlstm_w_v")):
                get(raw_qkv[16 * n:16 * n + 16], A[name][0].rearrange("(m n) c d -> m (n c d)", m=KI))
            for n, name in enumerate(("mlstm_w_ig", "mlstm_w_fg")):
                get(raw_if[0:48, n, :], A[name][0].rearrange("(t p) h -> t (p h)", p=P))
            get(raw_re[0:64], A["moe_w_re"].rearrange("i g (k p) e -> (i g k) (p e)", p=P))
            get(raw_rg[0:16], A["moe_w_rg"].rearrange("i (k p) g -> (i k) (p g)", p=P))
            get(raw_conv[0:24], A["state_mlstm_conv"][0].rearrange("b c n -> (b c) n"))
            get(nraw[0:32], A["state_mlstm_n"][0].rearrange("b h d -> (b h) d"))
            get(m0[:], A["state_mlstm_m"][0].rearrange("b h -> h b"))
            get(gb[:, 0:1], A["mlstm_b_ig"].rearrange("o h -> h o"))
            get(gb[:, 1:2], A["mlstm_b_fg"].rearrange("o h -> h o"))
            for i in range(2):
                get(rbias[:, i, 0:G], A["moe_b_rg"][i:i + 1].to_broadcast([P, G]))
                get(rbias[:, i, G:36], A["moe_b_re"][i:i + 1].rearrange("o g e -> o (g e)").to_broadcast([P, NE]))

            def norm(n, x_sem=None, x_before=0):
                if x_sem:
                    for k in range(KD):
                        act.wait_ge(s(x_sem), x_before + k + 1)
                        act.activation(hT[:, k, :], xT[:, k, :], ACT.Square).then_inc(s("sq"), 1)
                act.wait_ge(s("ss"), n + 1)
                act.activation(stdv, B[7][:, 0:NT], ACT.Sqrt, bias=eps6, scale=1.0 / D).then_inc(s("std"), 1)

            act.wait_ge(s("consts"), 6)
            norm(0)
            for m in range(KI + 1):
                if m < KI:
                    act.wait_ge(s("xm_mm"), m + 1)
                    act.activation(xe[:, m, 3:XS], B[m % 4][:, 0:NPROMPT], ACT.Copy).then_inc(s("xm_out"), 1)
                    act.activation(sample_view(xe[:, m, :])[:, :, 3:7],
                                   B[m % 4][:, NPROMPT:NT].rearrange("p (b s) -> p b s", s=SB),
                                   ACT.Copy).then_inc(s("xm_out"), 1)
                    act.activation(xms[:, m, :], B[m % 4][:, NPROMPT:NT], ACT.Copy).then_inc(s("xm_out"), 1)
                if m > 0:
                    c = m - 1
                    act.wait_ge(s("conv"), c + 1)
                    act.activation(xc[:, c, 0:NPROMPT], ctmp[:, c % 2, 0:NPROMPT], ACT.Silu).then_inc(s("xc"), 1)
                    act.activation(xc[:, c, NPROMPT:NT].rearrange("p (b s) -> p b s", s=SB),
                                   sample_view(ctmp[:, c % 2, :])[:, :, 0:4], ACT.Silu).then_inc(s("xc"), 1)
            for m in range(KI):
                act.wait_ge(s("qkv_mm"), m + 1)
                if m == 0:
                    act.wait_ge(s("raw_tr"), 5)
                act.activation(qT[:, m, :], B[m % 2][:, 0:NT], ACT.Copy).then_inc(s("q_out"), 1)
                if m >= 2:
                    act.wait_ge(s("gate_part"), m - 1)
                act.activation(vtr[:, m % 2, :], B[4 + m % 2][:, 0:NT], ACT.Copy).then_inc(s("v_out"), 1)
            act.wait_ge(s("gate_part"), KI)
            act.wait_ge(s("consts"), 8)
            for n in range(3):
                ins = act.activation(gt[32 * n:32 * n + 8, 0, :], B[6][32 * n:32 * n + 8, 0:NT], ACT.Copy)
            ins.then_inc(s("gates_act"), 1)
            act.wait_ge(s("gates_pe"), 1)
            act.activation(gt[0:4, 1, :], B[0][0:4, 0:NT], ACT.Identity, bias=gb[:, 0:1]).then_inc(s("gates_act"), 1)
            act.activation(gt[0:4, 2, :], B[1][0:4, 0:NT], ACT.Identity, bias=gb[:, 1:2]).then_inc(s("gates_act"), 1)
            act.wait_ge(s("gates_dve"), 1)
            act.activation(gt[0:4, 4, :], gt[0:4, 3, :], ACT.Exp, scale=-1.0).then_inc(s("gates_act"), 1)
            act.wait_ge(s("gates_act"), 4)
            act.wait_ge(s("consts"), 2)
            act.activation(gt[0:4, 3, :], gt[0:4, 4, :], ACT.Ln, bias=ones[0:4, 0:1]).then_inc(s("gates_act"), 1)
            act.wait_ge(s("gates_pe"), 2)
            for j, (_, n) in enumerate(TOK):
                b = B[2][0:n, 128 * j:128 * j + 128]
                act.activation(tm[0:n, j, 0:4], b[:, 0:4], ACT.Copy).then_inc(s("tm"), 1)
                act.activation(tm[0:n, j, 4:8], b[:, 32:36], ACT.Exp, scale=-1.0).then_inc(s("tm"), 1)
                act.activation(tm[0:n, j, 8:12], b[:, 96:100], ACT.Exp).then_inc(s("tm"), 1)
            act.activation(decn[:], B[3][0:NB, 0:H], ACT.Exp).then_inc(s("tm"), 1)
            act.wait_ge(s("tm"), 10)

            for h in range(H):
                act.wait_ge(s("bc_mm"), h + 1)
                act.activation(decb[:, h, :], B[0][:, NT:NT + 8], ACT.Exp).then_inc(s("bc_exp"), 1)
                act.activation(ibc[:, h, :], B[0][:, NT + 8:NT + 8 + NS], ACT.Exp).then_inc(s("bc_exp"), 1)
                if h > 0:
                    act.wait_ge(s("stw"), 3 * h)
                act.activation(ew[:, 0:256], B[0][:, 0:256], ACT.Exp, scale=-1.0, bias=tm[:, 0, h:h + 1]) \
                    .then_inc(s("e_ready"), 1)
                act.activation(ew[:, 256:384], B[0][:, 128:256], ACT.Exp, scale=-1.0, bias=tm[:, 1, h:h + 1]) \
                    .then_inc(s("e_ready"), 1)
                act.activation(ew[0:NS, 384:416], B[0][0:NS, 256:288], ACT.Exp, scale=-1.0,
                               bias=tm[0:NS, 2, h:h + 1]).then_inc(s("e_ready"), 1)
                act.wait_ge(s("v_mm"), h + 1)
                if h > 0:
                    act.wait_ge(s("num_mm"), 2 * h)
                for j, (_, n) in enumerate(TOK):
                    act.activation(vtok[0:n, j, :], B[4 + j][0:n, :], ACT.Copy).then_inc(s("vtok"), 1)
                for n in range(4):
                    act.wait_ge(s("spread_mm"), 4 * h + n + 1)
                    if n < 2 and h > 0:
                        act.wait_ge(s("parts"), 8 * h)
                    elif n >= 2:
                        act.wait_ge(s("parts"), 8 * h + 2 * (n - 1))
                    act.activation(y16[:, n % 2, :], B[SPREAD[n]][:, :], ACT.Copy).then_inc(s("y1"), 1)

                def prompt_state_out(i):
                    n = MH * h + i
                    act.wait_ge(s("cp_mm"), n + 1)
                    if n >= 2:
                        act.wait_ge(s(f"cp_stored{i % 2}"), 16 * (n // 2))
                    act.activation(cst[:, i % 2, :], B[(0, 7)[i % 2]][:, :], ACT.Copy).then_inc(s("cp_out"), 1)
                    act.wait_ge(s("cp_out"), n + 1)
                    act.dma_start(O["C_p"][0, 0, h, 128 * i:128 * i + 128, :], cst[:, i % 2, :]) \
                        .then_inc(s(f"cp_stored{i % 2}"), 16)

                prompt_state_out(0)
                prompt_state_out(1)
                prompt_state_out(2)
                prompt_state_out(3)
                act.wait_ge(s("np_mm"), h + 1)
                if h > 0:
                    act.wait_ge(s("np_stored"), 16 * h)
                act.activation(nst[:], B[0][0:1, :], ACT.Copy).then_inc(s("np_out"), 1)
                act.wait_ge(s("c_mm"), 32 * (h + 1))
                act.activation(snum, B[4][:, :], ACT.Copy).then_inc(s("snum"), 1)
                act.wait_ge(s("np_out"), h + 1)
                act.dma_start(O["n_p"][0, :, h, :], nst[:]).then_inc(s("np_stored"), 16)
                act.wait_ge(s("rden"), 2 * h + 1)
                for j in range(2):
                    act.activation(hhp[h][:, j, :], B[1 + j][:, :], ACT.Copy, scale=rden[:, j:j + 1]) \
                        .then_inc(s("hh"), 1)
                act.wait_ge(s("num_mm"), 2 * h + 2)
                act.wait_ge(s("rden"), 2 * h + 2)
                act.activation(hhs[h][0:NS], B[4][0:NS, :], ACT.Copy, scale=rden[0:NS, 2:3]).then_inc(s("hh"), 1)
            for m in range(KI):
                act.wait_ge(s("z_mm"), m + 1)
                act.activation(zs[:, m, :], B[m % 4][:, 0:NT], ACT.Silu).then_inc(s("zs"), 1)
                if m == 3:
                    act.wait_ge(s("mv"), 12)
                    act.activation(mvsd, mvsd, ACT.Sqrt, bias=eps5).then_inc(s("hsd"), 1)

            def moe(L, base):
                norm(1 + 2 * L, ("down_add", "out_add")[L])
                for n in range(6):
                    j, c = divmod(n, 2)
                    t = TOK[j][1]
                    act.wait_ge(s("htok_mm"), 6 * L + n + 1)
                    act.activation(htok[0:t, j, 512 * c:512 * c + 512], B[n][0:t, :], ACT.Copy) \
                        .then_inc(s("htok"), 1)
                act.wait_ge(s("router_dve"), 3 * L + 1)
                act.activation(rt[:, 320:332], rt[:, 300:312], ACT.Exp).then_inc(s("router_act"), 1)
                act.wait_ge(s("router_dve"), 3 * L + 2)
                act.activation(rt[:, 343:346], rt[:, 340:343], ACT.Exp).then_inc(s("router_act"), 1)

                def gathered(n):
                    c, m = divmod(n, 8)
                    act.wait_ge(s("gather_mm"), 16 * L + n + 1)
                    act.activation(xsT[:, m, NT * c:NT * c + NT], B[GATHER[n]][:, 0:NT], ACT.Copy) \
                        .then_inc(s("xs_a"), 1)

                def silu_gate(it, j):
                    act.wait_ge(s(f"gu_mm{j}"), it + 1)
                    act.activation(sg[CAP:P, j, :], B[j][0:CAP, :], ACT.Silu).then_inc(s(f"sg{j}"), 1)

                def outputs_out(it):
                    act.wait_ge(s("y_mm"), it + 1)
                    act.wait_ge(s("scatter_mm"), it * KD)
                    for c in range(2):
                        act.activation(ysb[:, F * c:F * c + F], B[2 + c][:, :], ACT.Copy).then_inc(s("y_out"), 1)

                for n in range(1, 8, 2):
                    gathered(n)
                silu_gate(base, 0)
                silu_gate(base, 1)
                for n in range(9, 16, 2):
                    gathered(n)
                outputs_out(base)
                act.wait_ge(s("table"), L + 1)
                last = act.value_load(table[0:1, ROUNDS * NE + 2:ROUNDS * NE + 3], min_val=1, max_val=ROUNDS * 16 - 1)
                with act.Fori(0, last) as i:
                    it = i + base
                    silu_gate(it + 1, 0)
                    silu_gate(it + 1, 1)
                    outputs_out(it + 1)
                return base + last + 1, base + last

            turns, last = moe(0, 0)
            norm(2, "moe_add", last * KD)
            for m in range(2 * KI):
                act.wait_ge(s("in_mm"), m + 1)
                dst = vT[:, m, :] if m < KI else uT[:, m - KI, :]
                act.activation(dst, B[m % 4][:, 0:NT], ACT.Gelu_apprx_tanh, bias=vec("cmlp_b_in", (m + KI) % (2 * KI))) \
                    .then_inc(s("gelu"), 1)
                if m == KI + 3:
                    for j, (_, n) in enumerate(TOK):
                        act.wait_ge(s("mv"), 12 + j + 1)
                        act.activation(mvc[0:n, j, 1:2], mvc[0:n, j, 1:2], ACT.Sqrt, bias=eps5[0:n]) \
                            .then_inc(s("hsd"), 1)
            _, last = moe(1, turns)
            norm(4, "moe_add", last * KD)
            for n in range(6):
                j, c = divmod(n, 2)
                t = TOK[j][1]
                act.wait_ge(s("x_tr"), KD + n + 1)
                act.activation(ytok[0:t, j, 512 * c:512 * c + 512], B[n][0:t, :], ACT.Copy).then_inc(s("y_ready"), 1)

        @block.tensor
        def _(pe):
            mm, tr = pe.matmul, pe.transpose

            def sum_squares(n, k):
                pe.wait_ge(s("sq"), KD * n + k + 1)
                ins = mm(B[7][:, 0:NT], ones[:], hT[:, k, :], start=(k == 0), stop=(k == KD - 1),
                         skip_group_check=True)
                if k == KD - 1:
                    ins.then_inc(s("ss"), 1)

            pe.wait_ge(s("consts"), 1)
            pe.wait_ge(s("x_landed"), 48)
            for k in range(KD):
                if k >= 2:
                    pe.wait_ge(s("xT"), k - 1)
                for j, (t0, n) in enumerate(TOK):
                    ins = tr(B[k % 2][:, t0:t0 + n], xtok[0:n, j, 128 * k:128 * k + 128], ident[0:n, 0:n])
                ins.then_inc(s("x_tr"), 1)
            pe.wait_ge(s("vec_landed"), 16 * len(vec_rows))
            tr(B[2][:, 0:128], raw_vec[:, 0, :], ident[:])
            tr(B[2][:, 128:192], raw_vec[0:64, 1, :], ident[0:64, 0:64]).then_inc(s("raw_tr"), 1)
            pe.wait_ge(s("consts"), 2)
            for k in range(KD):
                sum_squares(0, k)
            def small_weights():
                pe.wait_ge(s("raw_landed"), 16 * (3 + 2 + 4 + 3 + 4))
                pe.wait_ge(s("std"), 1)
                for i in range(4):
                    ins = tr(B[7][:, 48 * i:48 * i + 48], raw_qkv[0:48].rearrange("m (p d) -> m p d", d=4)[:, :, i],
                             ident[0:48, 0:48])
                ins.then_inc(s("raw_tr"), 1)
                for n in range(8):
                    ins = tr(B[4][:, 48 * n:48 * n + 48],
                             raw_if[0:48, n // 4, :].rearrange("t (p h) -> t p h", h=4)[:, :, n % 4], ident[0:48, 0:48])
                for i in range(MH):
                    ins = tr(B[4][:, 384 + 32 * i:416 + 32 * i], nraw[0:32, 128 * i:128 * i + 128], ident[0:32, 0:32])
                ins.then_inc(s("raw_tr"), 1)
                for e in range(8):
                    ins = tr(B[5][:, 64 * e:64 * e + 64], raw_re[0:64].rearrange("m (p e) -> m p e", e=8)[:, :, e],
                             ident[0:64, 0:64])
                ins.then_inc(s("raw_tr"), 1)
                for g in range(4):
                    ins = tr(B[6][:, 16 * g:16 * g + 16], raw_rg[0:16].rearrange("m (p g) -> m p g", g=4)[:, :, g],
                             ident[0:16, 0:16])
                for m in range(KI):
                    ins = tr(B[6][:, 64 + 24 * m:88 + 24 * m], raw_conv[0:24, 128 * m:128 * m + 128], ident[0:24, 0:24])
                ins.then_inc(s("raw_tr"), 1)

            def dense(key, groups, per, width, kt, rhs, done, freed, first=None, after=None):
                m = 0
                for j in range(groups):
                    landed(pe, key, j)
                    w = page(key, j).rearrange("p (k n) -> p k n", k=kt)
                    for i in range(per):
                        if m >= 4:
                            freed(m - 4)
                        for k in range(kt):
                            if m == 0 and first:
                                first(k)
                            ins = mm(B[m % 4][:, 0:NT], w[:, k, 128 * i:128 * i + 128], rhs(k),
                                     start=(k == 0), stop=(k == kt - 1))
                        ins.then_inc(s(done), 1)
                        if after:
                            after(m)
                        m += 1

            def normed(n):
                return lambda k: pe.wait_ge(s("h_norm"), KD * n + k + 1)

            def squares_behind(n):
                def after(m):
                    if m > 0:
                        sum_squares(n, m - 1)
                    if m == KD - 1:
                        sum_squares(n, m)
                return after

            dense("up", 4, 4, 512, KD, lambda k: hT[:, k, :], "xm_mm", lambda m: pe.wait_ge(s("xm_out"), 3 * m + 3),
                  first=normed(0), after=lambda m: small_weights() if m == 0 else None)
            pe.wait_ge(s("raw_out"), 5)

            def gate_part(m):
                pe.wait_ge(s("q_out"), m + 1)
                pe.wait_ge(s("k_out"), m + 1)
                pe.wait_ge(s("v_out"), m + 1)
                for n, src in enumerate((qT[:, m, :], kT[:, m, :], vtr[:, m % 2, :])):
                    ins = mm(B[6][32 * n:32 * n + 8, 0:NT], wif[:, 16 * n + m, :], src,
                             start=(m == 0), stop=(m == KI - 1), skip_group_check=True)
                ins.then_inc(s("gate_part"), 1)

            pe.wait_ge(s("bd"), 12)
            pe.wait_ge(s("xm_out"), 3 * KI)
            for m in range(KI):
                pe.wait_ge(s("xc"), 2 * m + 2)
                if m >= 2:
                    pe.wait_ge(s("q_out"), m - 1)
                    pe.wait_ge(s("k_out"), m - 1)
                    pe.wait_ge(s("v_out"), m - 1)
                mm(B[m % 2][:, 0:NT], bd[:, 0, m, :], xc[:, m, :], start=True, stop=True)
                mm(B[2 + m % 2][:, 0:NT], bd[:, 1, m, :], xc[:, m, :], start=True, stop=True)
                mm(B[4 + m % 2][:, 0:NPROMPT], bd[:, 2, m, :], xe[:, m, 3:XS], start=True, stop=True)
                mm(B[4 + m % 2][:, NPROMPT:NT], bd[:, 2, m, :], xms[:, m, :],
                   start=True, stop=True).then_inc(s("qkv_mm"), 1)
                if m >= 1:
                    gate_part(m - 1)
            gate_part(KI - 1)
            pe.wait_ge(s("gates_act"), 1)
            pe.wait_ge(s("masks"), 1)
            mm(B[0][0:4, 0:NT], gfold[0:96, 0:4], gt[0:96, 0, :], start=True, stop=True)
            mm(B[1][0:4, 0:NT], gfold[0:96, 4:8], gt[0:96, 0, :], start=True, stop=True).then_inc(s("gates_pe"), 1)
            pe.wait_ge(s("q_out"), KI)
            pe.wait_ge(s("k_out"), KI)
            pe.wait_ge(s("v_out"), KI)
            pe.wait_ge(s("cv27"), 2)
            for m in range(KI):
                if m in (8, 12):
                    pe.wait_ge(s("cv_out"), m // 4 - 1)
                ins = tr(B[4 + (m // 4) % 2][0:27, 128 * (m % 4):128 * (m % 4) + 128], cv27[:, m, :], ident[:])
                if m % 4 == 3:
                    ins.then_inc(s("cv_tr"), 1)
            def values_by_token(h):
                for j, (t0, t) in enumerate(TOK):
                    for i in range(MH):
                        m = MH * h + i
                        lhs = xe[:, m, 3 + t0:3 + t0 + t] if j < 2 else xms[:, m, :]
                        ins = mm(B[4 + j][0:t, 128 * i:128 * i + 128], lhs, bd[:, 2, m, :], start=True, stop=True)
                ins.then_inc(s("v_mm"), 1)

            def scores(h):
                for i in range(MH):
                    mm(B[7][:, 0:256], kT[:, MH * h + i, 0:128], qT[:, MH * h + i, 0:256],
                       start=(i == 0), stop=(i == MH - 1))
                for i in range(MH):
                    mm(B[7][:, 256:384], kT[:, MH * h + i, 128:256], qT[:, MH * h + i, 128:256],
                       start=(i == 0), stop=(i == MH - 1))
                for i in range(MH):
                    ins = mm(B[7][0:NS, 384:416], kT[:, MH * h + i, 256:288], qT[:, MH * h + i, 256:288],
                             start=(i == 0), stop=(i == MH - 1))
                ins.then_inc(s("st_mm"), 1)

            pe.wait_ge(s("cv_out"), 4)
            values_by_token(0)
            scores(0)
            pe.wait_ge(s("gates_dve"), 2)
            for j, (t0, n) in enumerate(TOK):
                tr(B[2][0:n, 128 * j:128 * j + 128], rows[:, t0:t0 + n], ident[:])
            tr(B[3][0:NB, 0:H], catA[0:4, NT:NT + 8], ident[0:4, 0:4]).then_inc(s("gates_pe"), 1)
            pe.wait_ge(s("tm"), 10)

            pe.wait_ge(s("masks"), 2)
            for h in range(H):
                if h > 0:
                    pe.wait_ge(s("np_out"), h)
                mm(B[0][:, 0:NT + 8 + NS], ident[0:4, h:h + 1].to_broadcast([4, P]), catA[:, :],
                   start=True, stop=True).then_inc(s("bc_mm"), 1)
                if h > 0:
                    pe.wait_ge(s("hh"), 3 * h - 1)
                    pe.wait_ge(s("rden"), 2 * h)
                for j, (t0, t) in enumerate(TOK):
                    for i in range(MH):
                        ins = tr(B[1 + j][0:t, 128 * i:128 * i + 128], kT[:, MH * h + i, t0:t0 + t], ident[:])
                ins.then_inc(s("k_mm"), 1)
                if h > 0:
                    pe.wait_ge(s("c_new"), 32 * h)
                    pe.wait_ge(s("hh"), 3 * h)
                    values_by_token(h)
                    pe.wait_ge(s("ns_out"), h)
                pe.wait_ge(s("wk"), 3 * h + 3)
                pe.wait_ge(s("vtok"), 3 * h + 3)
                pe.wait_ge(s("e_ready"), 3 * h + 3)
                for n in range(4):
                    mm(B[SPREAD[n]][:, :], spread[0:NS, n // 2, :], (wk, vtok)[n % 2][0:NS, 2, :],
                       start=True, stop=True).then_inc(s("spread_mm"), 1)

                def prompt_state(i, bank):
                    for j in range(2):
                        ins = mm(B[bank][:, :], wk[:, j, 128 * i:128 * i + 128], vtok[:, j, :],
                                 start=(j == 0), stop=(j == 1))
                    ins.then_inc(s("cp_mm"), 1)

                def between(b):
                    if b == 0 and h > 0:
                        scores(h)
                    elif b == 1:
                        pe.wait_ge(s("parts"), 8 * h + 7)
                        prompt_state(0, 0)
                    elif b == 2:
                        pe.wait_ge(s("stw"), 3 * h + 3)
                        prompt_state(1, 7)
                    elif b in (3, 4):
                        pe.wait_ge(s("cp_out"), MH * h + b - 2)
                        prompt_state(b - 1, (0, 7)[b - 3])
                    elif b == 5:
                        pe.wait_ge(s("cp_out"), MH * h + 3)
                        for j in range(2):
                            ins = mm(B[0][0:1, :], ones[:, 0:1], wk[:, j, :], start=(j == 0), stop=(j == 1))
                        ins.then_inc(s("np_mm"), 1)
                    elif b == 6:
                        pe.wait_ge(s("cp_out"), MH * h + 4)
                        mm(B[7][0:NB, :], bmask[0:NS, 0:NB], wk[0:NS, 2, :], start=True, stop=True) \
                            .then_inc(s("ns_mm"), 1)
                    elif b == 7:
                        pe.wait_ge(s("c_new"), 32 * h + 28)
                        mm(B[1][:, :], stw[:, 0:128], vtok[:, 0, :], start=True, stop=True)
                        mm(B[2][:, :], stw[:, 128:256], vtok[:, 0, :], start=True, stop=False)
                        mm(B[2][:, :], stw[:, 256:384], vtok[:, 1, :], start=False, stop=True)
                        mm(B[3][:, 0:1], stw[:, 0:128], ones[:, 0:1], start=True, stop=True)
                        mm(B[3][:, 1:2], stw[:, 128:256], ones[:, 0:1], start=True, stop=False)
                        mm(B[3][:, 1:2], stw[:, 256:384], ones[:, 0:1], start=False, stop=True) \
                            .then_inc(s("num_mm"), 1)

                pe.wait_ge(s("qz"), 2 * h + 1)
                for b in range(NB):
                    q = NB * h + b
                    pe.wait_ge(s(f"c_landed{q % 6}"), 16 * (q // 6 + 1))
                    for i in range(MH):
                        mm(B[4][NS * i:NS * i + NS, :], qz[:, i, NS * b:NS * b + NS], cview(q)[:, i, :],
                           start=(b == 0), stop=(b == NB - 1), skip_group_check=True)
                    if b % 4 == 0:
                        pe.wait_ge(s("parts"), 8 * h + 4 + b)
                    g = 32 * (b % 4)
                    for i in range(MH):
                        n = MH * b + i
                        if UPD_BEFORE[n] is not None:
                            pe.wait_ge(s("c_new"), 32 * h + UPD_BEFORE[n] + 1)
                        mm(B[UPD[n]][:, :], wk8[g:g + 32, b // 4, 128 * i:128 * i + 128], v8[g:g + 32, b // 4, :],
                           start=True, stop=True).then_inc(s("c_mm"), 1)
                    between(b)
                pe.wait_ge(s("rden"), 2 * h + 1)
                mm(B[3][0:NS, 2:3], stw[0:NS, 384:416], ones[0:NS, 0:1], start=True, stop=False)
                pe.wait_ge(s("qz"), 2 * h + 2)
                for i in range(MH):
                    mm(B[3][0:NS, 2:3], ew[:, 32 * i:32 * i + 32], ones[:, 0:1], start=False, stop=(i == MH - 1))
                pe.wait_ge(s("snum"), h + 1)
                mm(B[4][0:NS, :], fold, snum, start=True, stop=False)
                mm(B[4][0:NS, :], stw[0:NS, 384:416], vtok[0:NS, 2, :], start=False, stop=True) \
                    .then_inc(s("num_mm"), 1)
            pe.wait_ge(s("hh"), 3 * H)
            pe.wait_ge(s("c_new"), 32 * H)
            pe.wait_ge(s("np_out"), H)
            pe.wait_ge(s("ns_out"), H)
            def hidden(m):
                h, i = divmod(m, MH)
                pe.wait_ge(s("hn"), 3 * h + 3)
                if m >= 2:
                    pe.wait_ge(s("y_in"), m - 1)
                for j, (t0, n) in enumerate(TOK):
                    src = hhp[h][:, j, 128 * i:128 * i + 128] if j < 2 else hhs[h][0:NS, 128 * i:128 * i + 128]
                    ins = tr(B[4 + m % 2][:, t0:t0 + n], src, ident[0:n, 0:n])
                ins.then_inc(s("hn_tr"), 1)

            dense("z", 4, 4, 512, KD, lambda k: hT[:, k, :], "z_mm", lambda m: pe.wait_ge(s("zs"), m + 1),
                  after=lambda m: hidden(m - ZLAG) if m >= ZLAG else None)
            for m in range(KI - ZLAG, KI):
                hidden(m)
            dense("down", 4, 2, 256, KI, lambda k: xc[:, k, :], "down_mm", lambda m: pe.wait_ge(s("down_add"), m + 1),
                  first=lambda k: pe.wait_ge(s("y_mix"), k + 1), after=squares_behind(1))

            def moe(L, base):
                for j, (t0, t) in enumerate(TOK):
                    for k in range(KD):
                        if j == 0:
                            normed(1 + 2 * L)(k)
                        ins = mm(B[6][0:t, 36 * j:36 * j + 36], hT[:, k, t0:t0 + t], wr[:, L, k, :],
                                 start=(k == 0), stop=(k == KD - 1))
                ins.then_inc(s("router_pe"), 1)
                for n in range(6):
                    j, c = divmod(n, 2)
                    t0, t = TOK[j]
                    for k in range(4):
                        ins = tr(B[n][0:t, 128 * k:128 * k + 128], hT[:, 4 * c + k, t0:t0 + t], ident[:])
                    ins.then_inc(s("htok_mm"), 1)
                pe.wait_ge(s("router_dve"), 3 * L + 3)
                pe.wait_ge(s("consts"), 4)
                m2 = rt[:, 0:96].rearrange("p (j e) -> p j e", j=3)
                for j, (_, t) in enumerate(TOK):
                    for i in range(j):
                        mm(B[7][:, 32 * j:32 * j + 32], ones[:], m2[:, i, :], start=(i == 0), stop=False)
                    mm(B[7][:, 32 * j:32 * j + 32], before[0:t, :], m2[0:t, j, :], start=(j == 0), stop=True)
                for j, (_, t) in enumerate(TOK):
                    ins = mm(B[7][:, 96:128], ones[0:t, :], m2[0:t, j, :], start=(j == 0), stop=(j == 2))
                ins.then_inc(s("router_pe"), 1)
                pe.wait_ge(s("htok"), 6 * L + 6)

                def gather(n):
                    c, m = divmod(n, 8)
                    if 6 <= n < 8 or n >= 12:
                        o = n - 6 if n < 8 else n - 4
                        pe.wait_ge(s(f"xs_{'ba'[o % 2]}"), 8 * L + o // 2 + 1)
                    for i, (_, t) in enumerate(TOK):
                        if n == 0:
                            pe.wait_ge(s("sel"), 3 * L + i + 1)
                        ins = mm(B[GATHER[n]][:, 0:NT], htok[0:t, i, 128 * m:128 * m + 128],
                                 sel[0:t, i, NT * c:NT * c + NT], start=(i == 0), stop=(i == 2))
                    ins.then_inc(s("gather_mm"), 1)

                def gate_up(it, j):
                    gw, uw, _ = expert_pages(j)
                    x = xcx[:, j, :].rearrange("p (k c) -> p k c", k=KD)
                    pe.wait_ge(s(f"expert_landed{2 * j}"), (it + 1) * 16)
                    pe.wait_ge(s(f"expert_landed{2 * j + 1}"), (it + 1) * 16)
                    pe.wait_ge(s(f"xcx{j}"), it + (1 + L * (1 - j)))
                    for k in range(KD):
                        mm(B[j][0:CAP, :], x[:, k, :], gw[:, k, :], start=(k == 0), stop=(k == KD - 1))
                        ins = mm(B[j][CAP:P, :], x[:, k, :], uw[:, k, :], start=(k == 0), stop=(k == KD - 1))
                    ins.then_inc(s(f"gu_mm{j}"), 1)

                def outputs(it):
                    pe.wait_ge(s("moe_add"), it * KD)
                    for j in range(2):
                        pe.wait_ge(s(f"hx{j}"), it + 1)
                        for f in range(MF):
                            ins = mm(B[4 + 3 * j][:, CAP * f:CAP * f + CAP], hx[CAP:P, j, 128 * f:128 * f + 128],
                                     ident[CAP:P, CAP:P], start=True, stop=True)
                        ins.then_inc(s(f"ht_tr{j}"), 1)
                    for j in range(2):
                        pe.wait_ge(s(f"ht{j}"), it + 1)
                    pe.wait_ge(s("y_out"), it * 2)
                    for f in range(MF):
                        if f % 2 == 0:
                            for j in range(2):
                                pe.wait_ge(s(f"expert_landed{4 + 2 * (f // 2) + j}"), (it + 1) * 16)
                        for c in range(2):
                            for j in range(2):
                                dw = expert_pages(j)[2]
                                ins = mm(B[2 + c][CAP * j:CAP * j + CAP, :], hxT[:, j, CAP * f:CAP * f + CAP],
                                         dw[:, f, 512 * c:512 * c + 512], start=(f == 0), stop=(f == MF - 1),
                                         skip_group_check=True)
                    ins.then_inc(s("y_mm"), 1)

                def scatter(it):
                    pe.wait_ge(s("wpair"), it + 1)
                    for m in range(KD):
                        if m % 4 == 0:
                            pe.wait_ge(s("y_out"), it * 2 + (m // 4 + 1))
                        if m >= 3:
                            pe.wait_ge(s("moe_add"), it * KD + (m - 2))
                        mm(B[SCATTER[m % 3]][:, 0:NT], ysb[:, 128 * m:128 * m + 128], wpair, start=True, stop=True) \
                            .then_inc(s("scatter_mm"), 1)

                for n in range(8):
                    gather(n)
                gate_up(base, 0)
                gate_up(base, 1)
                outputs(base)
                for n in range(8, 16):
                    gather(n)
                pe.wait_ge(s("placew"), L + 1)
                pe.wait_ge(s("xs_a"), 8 * L + 8)
                pe.wait_ge(s("xs_b"), 8 * L + 8)
                for n in range(4):
                    if n >= 2:
                        pe.wait_ge(s("tokrow"), 4 * L + n - 1)
                    for j, (t0, t) in enumerate(TOK):
                        ins = mm(B[6 + n % 2][:, t0:t0 + t], placew[0:t, 3 * n + j:3 * n + j + 1].to_broadcast([t, P]),
                                 ident[0:t, 0:t], start=True, stop=True)
                    ins.then_inc(s("tokrow_mm"), 1)
                pe.wait_ge(s("tokrow"), 4 * L + 4)
                pe.wait_ge(s("table"), L + 1)
                last = pe.value_load(table[0:1, ROUNDS * NE + 2:ROUNDS * NE + 3], min_val=1, max_val=ROUNDS * 16 - 1)
                with pe.Fori(0, last) as i:
                    it = i + base
                    gate_up(it + 1, 0)
                    gate_up(it + 1, 1)
                    scatter(it)
                    outputs(it + 1)
                scatter(base + last)
                turns = base + last + 1
                for k in range(KD):
                    sum_squares(2 + 2 * L, k)
                return turns

            turns = moe(0, 0)
            def mix(m):
                if m >= 4:
                    pe.wait_ge(s("mixed"), m - 3)
                for j in range(2):
                    mm(B[4 + m % 4][:, 128 * j:128 * j + 128], vtk[:, j, 128 * m:128 * m + 128], wsT[:, m // 2, :],
                       start=True, stop=True)
                mm(B[4 + m % 4][:, 256:NT], vtk[0:NS, 2, 128 * m:128 * m + 128], wsS[0:NS, m // 2, :],
                   start=True, stop=True).then_inc(s("mix_mm"), 1)

            def behind(m):
                v_by_token(m)
                if m == 24:
                    pe.wait_ge(s("vtk"), 12)
                    pe.wait_ge(s("ws_masked"), 1)
                    pe.wait_ge(s("masks"), 3)
                    mm(B[4][0:NS, 0:CG * SB], rep[0:4, :], wsT[0:4, :, 0:SB], start=True, stop=True) \
                        .then_inc(s("ws_tr"), 1)
                if m == 27:
                    pe.wait_ge(s("masks"), 4)
                    pe.wait_ge(s("v_norm"), 3)
                if m >= 27:
                    for n in range(3 * (m - 27), 3 * (m - 27) + 3):
                        mix(n)

            def v_by_token(m):
                c = (m - 5) // 4
                if m == 5:
                    pe.wait_ge(s("ws_landed"), 16)
                    for g in range(CG):
                        ins = tr(B[4 + g // 4][:, 128 * (g % 4):128 * (g % 4) + 128], raw_ws[:, g, :], ident[:])
                        if g % 4 == 3:
                            ins.then_inc(s("ws_tr"), 1)
                    pe.wait_ge(s("ws_out"), 2)
                if m in (5, 9, 13, 17):
                    pe.wait_ge(s("gelu"), 4 * c + 4)
                    for j, (t0, t) in enumerate(TOK):
                        n = 3 * c + j
                        if n >= 4:
                            pe.wait_ge(s("vtk"), n - 3)
                        for i in range(4):
                            ins = tr(B[4 + n % 4][0:t, 128 * i:128 * i + 128], vT[:, 4 * c + i, t0:t0 + t], ident[:])
                        ins.then_inc(s("vtok_mm"), 1)

            dense("in", 8, 4, 512, KD, lambda k: hT[:, k, :], "in_mm", lambda m: pe.wait_ge(s("gelu"), m + 1),
                  first=normed(2), after=behind)
            mix(KI - 1)
            pe.wait_ge(s("gelu"), 2 * KI)
            dense("out", 4, 2, 256, KI, lambda k: uT[:, k, :], "out_mm", lambda m: pe.wait_ge(s("out_add"), m + 1),
                  first=lambda k: pe.wait_ge(s("mixed"), k + 1), after=squares_behind(3))
            moe(1, turns)
            for n in range(6):
                j, c = divmod(n, 2)
                t0, t = TOK[j]
                for k in range(4):
                    if j == 0:
                        normed(4)(4 * c + k)
                    ins = tr(B[n][0:t, 128 * k:128 * k + 128], hT[:, 4 * c + k, t0:t0 + t], ident[:])
                ins.then_inc(s("x_tr"), 1)

        @block.vector
        def _(dve):
            chain = [0]

            def link(ins):
                chain[0] += 1
                ins.then_inc(s("dve_chain"), 1)
                dve.wait_ge(s("dve_chain"), chain[0])

            tt, ts, stt, copy = dve.tensor_tensor, dve.tensor_scalar, dve.scalar_tensor_tensor, dve.tensor_copy

            def norm(n):
                dve.wait_ge(s("std"), n + 1)
                link(dve.reciprocal(rstd, stdv))
                for k in range(KD):
                    stt(hT[:, k, :], xT[:, k, :], vecs[:, NORM[n] + k:NORM[n] + k + 1], rstd, ALU.mult, ALU.mult) \
                        .then_inc(s("h_norm"), 1)

            def raw_copies(n, copies):
                dve.wait_ge(s("raw_tr"), n)
                for dst, src in copies:
                    ins = copy(dst, src)
                ins.then_inc(s("raw_out"), 1)

            for k in range(KD):
                dve.wait_ge(s("x_tr"), k + 1)
                copy(xT[:, k, :], B[k % 2][:, 0:NT]).then_inc(s("xT"), 1)
                dve.wait_ge(s("xT"), k + 1)
                tt(hT[:, k, :], xT[:, k, :], xT[:, k, :], ALU.mult).then_inc(s("sq"), 1)
            raw_copies(1, [(vecs[:], B[2][:, 0:192])])
            dve.wait_ge(s("raw_out"), 1)
            norm(0)
            raw_copies(2, [(wqkv, B[7][:, 0:192].rearrange("p (i m) -> p i m", i=4))])
            raw_copies(3, [(wif[:].rearrange("p t n -> p n t"), B[4][:, 0:384].rearrange("p (n t) -> p n t", n=8)),
                           (nT[:], B[4][:, 384:512].rearrange("p (i r) -> p i r", i=MH))])
            raw_copies(4, [(wr[:, i, :, G + EPG * g:G + EPG * g + EPG],
                            B[5][:, :].rearrange("p (e r k) -> p r k e", e=8, r=8)[:, 4 * i + g, :, :])
                           for i in range(2) for g in range(G)])
            dve.wait_ge(s("consts"), 5)
            raw_copies(5, [(wr[:, i, :, 0:G], B[6][:, 0:64].rearrange("p (g i k) -> p i k g", g=4, i=2)[:, i, :, :])
                           for i in range(2)] +
                       [(sample_view_all(xe), B[6][:, 64:448].rearrange("p (m b c) -> p m b c", m=KI, b=NB))])
            dve.wait_ge(s("raw_out"), 5)
            dve.wait_ge(s("consts"), 6)
            dve.tensor_reduce(gfold, ident[:, 0:96].rearrange("p (g c) -> p c g", g=3)[:, 0:8, :], AX.X, ALU.add) \
                .then_inc(s("masks"), 1)
            W = XE - 3
            for m in range(KI):
                dve.wait_ge(s("xm_out"), 3 * m + 3)
                if m >= 2:
                    dve.wait_ge(s("xc"), 2 * m - 2)
                y = ctmp[:, m % 2, 0:W]
                link(ts(y, xe[:, m, 0:W], vec("mlstm_conv_w", m), vec("mlstm_conv_b", m), ALU.mult, ALU.add))
                for i in range(1, 4):
                    ins = stt(y, xe[:, m, i:i + W], vec("mlstm_conv_w", KI * i + m), y, ALU.mult, ALU.add)
                    if i < 3:
                        link(ins)
                ins.then_inc(s("conv"), 1)
            for m in range(KI):
                dve.wait_ge(s("qkv_mm"), m + 1)
                copy(kT[:, m, :], B[2 + m % 2][:, 0:NT]).then_inc(s("k_out"), 1)
            dve.wait_ge(s("xc"), 2 * KI)
            copy(cv27[:, :, 0:3], xe[:, :, NPROMPT:NPROMPT + 3]).then_inc(s("cv27"), 1)
            copy(cv27[:, :, 3:27].rearrange("p m (b c) -> p m b c", c=3), sample_view_all(xe, 4)).then_inc(s("cv27"), 1)
            for n in range(4):
                dve.wait_ge(s("cv_tr"), n + 1)
                copy(cvout[0:27, 512 * n:512 * n + 512], B[4 + n % 2][0:27, :]).then_inc(s("cv_out"), 1)
            gi, gf, tmp, lf, ones4, fs, a, ap = (gt[0:4, n, :] for n in (1, 2, 3, 4, 5, 6, 7, 8))
            radd = gt[0:4, 9, :]
            dve.wait_ge(s("gates_act"), 1)
            link(dve.memset(ones4, 1.0))
            link(dve.memset(radd, 0.0))
            link(dve.memset(gt[0:4, 5, NPROMPT:NT:SB], 0.0))
            link(dve.memset(gt[0:4, 9, NPROMPT:NT:SB], -1.0e38))
            dve.wait_ge(s("gates_act"), 3)
            link(ts(tmp, gf, -1.0, None, ALU.mult))
            tt(tmp, tmp, gf, ALU.max).then_inc(s("gates_dve"), 1)
            dve.wait_ge(s("gates_act"), 5)
            link(stt(lf, gf, 0.0, tmp, ALU.min, ALU.subtract))
            link(dve.tensor_tensor_scan(fs, ones4, lf, 0.0, ALU.mult, ALU.add))
            link(tt(a, gi, fs, ALU.subtract))
            link(copy(ap, a))
            link(tt(gt[0:4, 8, NPROMPT:NT:SB], gt[0:4, 7, NPROMPT:NT:SB], m0[:], ALU.max))
            Am = catA[:, 0:NT]
            link(dve.tensor_tensor_scan(Am, radd, ap, NEG, ALU.add, ALU.max))
            bs = "p (b s) -> p b s"
            Amb = catA[:, NPROMPT:NT].rearrange(bs, s=SB)
            Alast = catA[:, NPROMPT + 3:NT:SB]
            dve.wait_ge(s("consts"), 7)
            link(tt(catA[:, NT:NT + 8], m0[:], Alast, ALU.subtract))
            link(tt(catA[:, NT + 8:NT + 8 + NS].rearrange(bs, s=SB), m0[:].unsqueeze(2).to_broadcast([4, NB, SB]), Amb,
                    ALU.subtract))
            link(copy(rows[0:4, :], a))
            link(tt(rows[32:36, :], fs, Am, ALU.add))
            link(ts(rows[96:100, 0:NPROMPT], gt[0:4, 7, 0:NPROMPT], catA[:, NPROMPT - 1:NPROMPT], None, ALU.subtract))
            tt(rows[96:100, NPROMPT:NT].rearrange(bs, s=SB), gt[0:4, 7, NPROMPT:NT].rearrange(bs, s=SB),
               Alast.unsqueeze(2).to_broadcast([4, NB, SB]), ALU.subtract).then_inc(s("gates_dve"), 1)
            for half in range(2):
                copy(spread[0:NS, half, :].rearrange("p (b c s) -> p b c s", b=4, c=8),
                     ident[0:NS, 16 * half:16 * half + 16].rearrange("p (b s) -> p b s", b=4).unsqueeze(2)
                     .to_broadcast([NS, 4, 8, 4]))
            dve.tensor_reduce(fold, ident[:].rearrange("p (i s) -> p s i", i=4), AX.X, ALU.add)
            link(dve.tensor_reduce(prod, ident[:].rearrange("p (b c s) -> p c b s", b=4, c=8), AX.XY, ALU.add))
            link(dve.tensor_reduce(notp[:, 0:1], prod[:, 3:8], AX.X, ALU.add))
            link(dve.tensor_reduce(notp[:, 1:2], prod[:, 6:8], AX.X, ALU.add))
            link(dve.tensor_reduce(notp[:, 3:4], prod[:, 2:6:3], AX.X, ALU.add))
            link(dve.tensor_reduce(notp[:, 2:3], prod[:, 1:8:3], AX.X, ALU.add))
            link(tt(notp[:, 2:3], notp[:, 2:3], notp[:, 3:4], ALU.add))
            ts(notp, notp, -1.0, None, ALU.mult).then_inc(s("masks"), 1)
            dve.wait_ge(s("masks"), 2)
            dve.wait_ge(s("tm"), 10)

            for h in range(H):
                dve.wait_ge(s("k_mm"), h + 1)
                if h > 0:
                    dve.wait_ge(s("num_mm"), 2 * h)
                for j, (_, n) in enumerate(TOK):
                    ts(wk[0:n, j, :], B[1 + j][0:n, :], tm[0:n, j, 8 + h:9 + h], KSCALE, ALU.mult, ALU.mult) \
                        .then_inc(s("wk"), 1)
                dve.wait_ge(s("bc_exp"), 2 * h + 2)
                dve.wait_ge(s("qz_zero"), 1)
                qi = qz[:, :, :].rearrange("p i (b x) -> p i b x", x=36)[:, :, :, 0:SB]
                q = qT[:, MH * h:MH * h + MH, NPROMPT:NT].rearrange("p i (b s) -> p i b s", s=SB)
                ib = ibc[:, h, :].rearrange(bs, s=SB)
                for i in range(MH):
                    ins = tt(qi[:, i], q[:, i], ib, ALU.mult)
                ins.then_inc(s("qz"), 1)
                if h == 0:
                    dve.wait_ge(s("cv_stored"), 32)

                def parts(n):
                    dst = (wk8, v8)[n % 2]
                    f = notp[:, 2 * (n % 2):2 * (n % 2) + 2]
                    y, z = y16[:, n % 2, :], z1[:, n % 2, :]
                    dve.wait_ge(s("y1"), 4 * h + n + 1)
                    stt(z, y, f[:, 0:1], B[SPREAD[n]][:, :], ALU.mult, ALU.add).then_inc(s("parts"), 1)
                    dve.wait_ge(s("parts"), 8 * h + 2 * n + 1)
                    link(copy(y, z))
                    stt(dst[:, n // 2, :], y, f[:, 1:2], z, ALU.mult, ALU.add).then_inc(s("parts"), 1)
                    dve.wait_ge(s("parts"), 8 * h + 2 * n + 2)

                def scores_and_normaliser():
                    dve.wait_ge(s("st_mm"), h + 1)
                    dve.wait_ge(s("e_masked"), 3 * h + 3)
                    for p, c0, c1 in ((P, 0, 256), (P, 256, 384), (NS, 384, 416)):
                        stt(stw[0:p, c0:c1], B[7][0:p, c0:c1], KSCALE, ew[0:p, c0:c1], ALU.mult, ALU.mult) \
                            .then_inc(s("stw"), 1)
                    dve.wait_ge(s("stw"), 3 * h + 3)
                    dve.wait_ge(s("qz"), 2 * h + 1)
                    npr = ew[:, 0:128].rearrange("p (i b s) -> p i b s", i=MH, s=SB)
                    for i in range(MH):
                        ins = tt(npr[:, i], qi[:, i],
                                 nT[:, i, h:32:H].unsqueeze(2).to_broadcast([P, NB, SB]), ALU.mult)
                    ins.then_inc(s("qz"), 1)

                def prompt_denominators():
                    dve.wait_ge(s("num_mm"), 2 * h + 1)
                    for j in range(2):
                        link(ts(dden[:, j:j + 1], B[3][:, j:j + 1], -1.0, None, ALU.mult))
                        link(stt(dden[:, j:j + 1], dden[:, j:j + 1], tm[:, j, 4 + h:5 + h], B[3][:, j:j + 1],
                                 ALU.max, ALU.max))
                    dve.reciprocal(rden[:, 0:2], dden[:, 0:2]).then_inc(s("rden"), 1)

                parts(0)
                parts(1)
                for b in range(NB):
                    for i in range(MH):
                        c = cview(NB * h + b)[:, i, :]
                        n = (NB * h + b) * MH + i
                        dve.wait_ge(s("c_mm"), n + 1)
                        stt(c, c, decb[:, h, b:b + 1], B[UPD[MH * b + i]][:, :], ALU.mult, ALU.add).then_inc(s("c_new"), 1)
                    if b == 0:
                        parts(2)
                        parts(3)
                        scores_and_normaliser()
                dve.wait_ge(s("ns_mm"), h + 1)
                dve.wait_ge(s(f"n_landed{h % 2}"), 16 * (h // 2 + 1))
                stt(nrow[:, h % 2, :], nrow[:, h % 2, :], decn[:, h:h + 1], B[7][0:NB, :], ALU.mult, ALU.add) \
                    .then_inc(s("ns_out"), 1)
                prompt_denominators()
                dve.wait_ge(s("num_mm"), 2 * h + 2)
                link(ts(dden[0:NS, 2:3], B[3][0:NS, 2:3], -1.0, None, ALU.mult))
                link(stt(dden[0:NS, 2:3], dden[0:NS, 2:3], tm[0:NS, 2, 4 + h:5 + h], B[3][0:NS, 2:3],
                         ALU.max, ALU.max))
                dve.reciprocal(rden[0:NS, 2:3], dden[0:NS, 2:3]).then_inc(s("rden"), 1)
            def hh(h, j):
                return hhp[h][:, j, :] if j < 2 else hhs[h][0:NS]

            dve.wait_ge(s("hh"), 3 * H)
            mean = rstd[:, 0:12]
            for h in range(H):
                for j, (_, n) in enumerate(TOK):
                    c = 3 * h + j
                    link(dve.bn_stats(lnst[0:n], hh(h, j)))
                    link(dve.bn_aggr(stdv[0:n, 2 * c:2 * c + 2], lnst[0:n]))
                    copy(mvsd[0:n, c:c + 1], stdv[0:n, 2 * c + 1:2 * c + 2]).then_inc(s("mv"), 1)
            dve.wait_ge(s("hsd"), 1)
            link(dve.reciprocal(mean, mvsd))
            for h in range(H):
                for j, (_, n) in enumerate(TOK):
                    c = 3 * h + j
                    ts(hh(h, j), hh(h, j), stdv[0:n, 2 * c:2 * c + 1], mean[0:n, c:c + 1], ALU.subtract, ALU.mult) \
                        .then_inc(s("hn"), 1)
            for m in range(KI):
                dve.wait_ge(s("hn_tr"), m + 1)
                dve.wait_ge(s("zs"), m + 1)
                t = (stdv, rstd)[m % 2]
                if m < 2:
                    dve.wait_ge(s("hn"), 3 * H)
                else:
                    dve.wait_ge(s("y_mix"), m - 1)
                ts(t, B[4 + m % 2][:, 0:NT], vec("mlstm_hn_w", m), None, ALU.mult).then_inc(s("y_in"), 1)
                dve.wait_ge(s("y_in"), m + 1)
                link(stt(t, xc[:, m, :], vec("mlstm_skip", m), t, ALU.mult, ALU.add))
                tt(xc[:, m, :], t, zs[:, m, :], ALU.mult).then_inc(s("y_mix"), 1)
            for m in range(KD):
                dve.wait_ge(s("down_mm"), m + 1)
                tt(xT[:, m, :], xT[:, m, :], B[m % 4][:, 0:NT], ALU.add).then_inc(s("down_add"), 1)

            def moe(L, base):
                norm(1 + 2 * L)

                def v3(o, n):
                    return rt[:, o:o + 3 * n].rearrange("p (j e) -> p j e", j=3)

                def bc(t, n):
                    return t.unsqueeze(2).to_broadcast([P, 3, n])

                def bj(t, n):
                    return t.unsqueeze(1).to_broadcast([P, 3, n])

                M, M0, M1 = v3(0, NE), v3(96, NE), v3(192, NE)
                lg, ge = v3(300, G), v3(320, G)
                gmax, gsum = rt[:, 312:315], rt[:, 332:335]
                diff, ediff = rt[:, 340:343], rt[:, 343:346]
                t1, t2 = rt[:, 346:349], rt[:, 349:352]
                lt = v3(400, 36)
                gm = v3(510, G)
                key = v3(530, NE)
                le = v3(630, NE)
                rank = v3(730, NE)
                nrep = rt[:, 860:1020].rearrange("p (r e) -> p r e", r=ROUNDS)
                off = rt[:, 1020:1180].rearrange("p (r e) -> p r e", r=ROUNDS)
                one160 = rt[:, 1180:1340]
                doff = rt[:, 1340:1500].rearrange("p (r e) -> p r e", r=ROUNDS)
                cnt = rt[:, 826:858]
                thr = rt[:, 1500:1505]
                pos = v3(1510, NE)
                tmp3 = v3(1610, NE)
                mx = rt[:, 1720:1721]
                rmax, rmin = rt[:, 1722:1725], rt[:, 1726:1729]

                dve.wait_ge(s("consts"), 6)
                link(dve.memset(rt, 0.0))
                link(dve.memset(one160, 1.0))
                dve.wait_ge(s("iota"), 3 * L + 3)
                dve.wait_ge(s("router_pe"), 2 * L + 1)
                for j, (_, n) in enumerate(TOK):
                    link(tt(lt[0:n, j, :], B[6][0:n, 36 * j:36 * j + 36], rbias[0:n, L, :], ALU.add))

                def first_max(out, val, vmax, idx, n):
                    link(dve.tensor_reduce(vmax, val, AX.X, ALU.max))
                    link(tt(out, val, bc(vmax, n), ALU.is_equal))
                    k = key[:, :, 0:n]
                    link(stt(k, out, -EARLIER, idx, ALU.mult, ALU.add))
                    link(dve.tensor_reduce(rmin, k, AX.X, ALU.min))
                    link(tt(out, k, bc(rmin, n), ALU.is_equal))

                first_max(gm, lt[:, :, 0:G], gmax, bj(iota32[:, 0:G], G), G)
                tt(lg, lt[:, :, 0:G], bc(gmax, G), ALU.subtract).then_inc(s("router_dve"), 1)
                link(ts(gm, gm, 1.0, 1.0e30, ALU.subtract, ALU.mult))
                for g in range(G):
                    link(tt(le[:, :, EPG * g:EPG * g + EPG], lt[:, :, G + EPG * g:G + EPG * g + EPG],
                            gm[:, :, g:g + 1].to_broadcast([P, 3, EPG]), ALU.add))
                idx32 = bj(iota32, NE)
                first_max(M0, le, rmax, idx32, NE)
                link(stt(le, M0, -2.0e30, le, ALU.mult, ALU.add))
                first_max(M1, le, t1, idx32, NE)
                tt(diff, t1, rmax, ALU.subtract).then_inc(s("router_dve"), 1)
                tt(M, M0, M1, ALU.add).then_inc(s("router_dve"), 1)
                dve.wait_ge(s("router_act"), 2 * L + 1)
                link(dve.tensor_reduce(gsum, ge, AX.X, ALU.add))
                dve.wait_ge(s("router_act"), 2 * L + 2)
                link(ts(t2, ediff, 1.0, None, ALU.add))
                link(tt(t2, t2, gsum, ALU.mult))
                link(dve.reciprocal(placew[:, 6:9], t2))
                link(tt(placew[:, 9:12], placew[:, 6:9], ediff, ALU.mult))
                dve.wait_ge(s("router_pe"), 2 * L + 2)
                link(copy(rt[:, 730:858], B[7][:, 0:128]))
                for r in range(ROUNDS):
                    link(ts(nrep[:, r, :], cnt, float(CAP * r), 0.0, ALU.subtract, ALU.max))
                link(ts(nrep, nrep, float(CAP), None, ALU.min))
                nflat, oflat = rt[:, 860:1020], rt[:, 1020:1180]
                link(dve.tensor_tensor_scan(oflat, one160, nflat, 0.0, ALU.mult, ALU.add))
                link(tt(oflat, oflat, nflat, ALU.subtract))
                link(tt(doff[:, 1:ROUNDS, :], off[:, 1:ROUNDS, :], off[:, 0:ROUNDS - 1, :], ALU.subtract))
                link(ts(doff[:, 1:ROUNDS, :], doff[:, 1:ROUNDS, :], float(CAP), None, ALU.subtract))
                link(tt(pos, rank, bj(off[:, 0, :], NE), ALU.add))
                for r in range(1, ROUNDS):
                    link(stt(tmp3, rank, float(CAP * r), bj(doff[:, r, :], NE), ALU.is_ge, ALU.mult))
                    link(tt(pos, pos, tmp3, ALU.add))
                for n, m in enumerate((M0, M1)):
                    link(tt(tmp3, pos, m, ALU.mult))
                    dve.tensor_reduce(slotw[:, 3 * n:3 * n + 3], tmp3, AX.X, ALU.add).then_inc(s("slots"), 1)
                    dve.wait_ge(s("slots"), 2 * L + n + 1)
                for j, (_, n) in enumerate(TOK):
                    link(ts(sel[0:n, j, :], iota[0:n], slotw[0:n, j:j + 1], None, ALU.is_equal))
                    stt(sel[0:n, j, :], iota[0:n], slotw[0:n, 3 + j:4 + j], sel[0:n, j, :], ALU.is_equal, ALU.add) \
                        .then_inc(s("sel"), 1)
                link(dve.tensor_reduce(mx, cnt, AX.X, ALU.max))
                for r in range(ROUNDS):
                    link(ts(thr[:, r:r + 1], mx, float(CAP * r), None, ALU.is_gt))
                link(dve.tensor_reduce(rt[:, 1721:1722], thr, AX.X, ALU.add))
                dve.wait_ge(s("moe_add"), base * KD)
                link(dve.memset(table[:, ROUNDS * NE:ROUNDS * NE + 1], 0))
                link(copy(table[:, 0:ROUNDS * NE], rt[0:1, 1020:1180]))
                link(ts(table[:, ROUNDS * NE + 2:ROUNDS * NE + 3], rt[0:1, 1721:1722], float(NE // 2), -1.0, ALU.mult,
                        ALU.add))
                copy(table[:, ROUNDS * NE + 1:ROUNDS * NE + 2], rt[0:1, 1721:1722]).then_inc(s("table"), 1)
                link(stt(pos, idx32, float(CAP), rank, ALU.mult, ALU.add))
                for r in range(1, ROUNDS):
                    link(ts(tmp3, rank, float(CAP * r), float(CAP * (NE - 1)), ALU.is_ge, ALU.mult))
                    link(tt(pos, pos, tmp3, ALU.add))
                link(tt(tmp3, pos, M0, ALU.mult))
                link(dve.tensor_reduce(placew[:, 0:3], tmp3, AX.X, ALU.add))
                link(tt(tmp3, pos, M1, ALU.mult))
                dve.tensor_reduce(placew[:, 3:6], tmp3, AX.X, ALU.add).then_inc(s("placew"), 1)

                def gathered(n):
                    c, m = divmod(n, 8)
                    dve.wait_ge(s("gather_mm"), 16 * L + n + 1)
                    copy(xsT[:, m, NT * c:NT * c + NT], B[GATHER[n]][:, 0:NT]).then_inc(s("xs_b"), 1)

                def fetch(n, j, freed=None):
                    o = dve.value_load(table[0:1, bass.ds(n, 1)], min_val=0, max_val=NSLOT)
                    if freed:
                        dve.wait_ge(*freed)
                    copy(xcx[:, j, :].rearrange("p (k c) -> p k c", k=KD), xsT[:, :, bass.ds(o, CAP)]) \
                        .then_inc(s(f"xcx{j}"), 1)

                def hidden_values(it, j):
                    dve.wait_ge(s(f"sg{j}"), it + 1)
                    tt(hx[CAP:P, j, :], sg[CAP:P, j, :], B[j][CAP:P, :], ALU.mult).then_inc(s(f"hx{j}"), 1)

                def hidden_features(it):
                    for j in range(2):
                        dve.wait_ge(s(f"ht_tr{j}"), it + 1)
                        copy(hxT[:, j, :], B[4 + 3 * j][:, 0:MF * CAP]).then_inc(s(f"ht{j}"), 1)

                def row_weights(i, it):
                    dve.wait_ge(s("scatter_mm"), it * KD)
                    place_n = rowplace[:, bass.ds(i, 1)]
                    stt(wpart, tokrow[:, 0, :], place_n, tokrow[:, 2, :], ALU.is_equal, ALU.mult) \
                        .then_inc(s("wparts"), 1)
                    stt(wpair, tokrow[:, 1, :], place_n, tokrow[:, 3, :], ALU.is_equal, ALU.mult) \
                        .then_inc(s("wparts"), 1)
                    dve.wait_ge(s("wparts"), it * 2 + 2)
                    tt(wpair, wpair, wpart, ALU.add).then_inc(s("wpair"), 1)

                def add_outputs(it):
                    for m in range(KD):
                        dve.wait_ge(s("scatter_mm"), it * KD + (m + 1))
                        tt(xT[:, m, :], xT[:, m, :], B[SCATTER[m % 3]][:, 0:NT], ALU.add).then_inc(s("moe_add"), 1)

                for n in range(0, 8, 2):
                    gathered(n)
                dve.wait_ge(s("xs_a"), 8 * L + 4)
                dve.wait_ge(s("xs_b"), 8 * L + 4)
                dve.wait_ge(s("table"), L + 1)
                fetch(0, 0)
                fetch(1, 1)
                hidden_values(base, 0)
                hidden_values(base, 1)
                hidden_features(base)
                for n in range(8, 16, 2):
                    gathered(n)
                for n in range(4):
                    dve.wait_ge(s("tokrow_mm"), 4 * L + n + 1)
                    copy(tokrow[:, n, :], B[6 + n % 2][:, 0:NT]).then_inc(s("tokrow"), 1)
                dve.wait_ge(s("tokrow"), 4 * L + 4)
                dve.wait_ge(s("xs_a"), 8 * L + 8)
                dve.wait_ge(s("xs_b"), 8 * L + 8)
                dve.wait_ge(s("xs_pad"), L + 1)
                fetch(2, 0, (s("gu_mm0"), base + 1))
                row_weights(0, base)
                last = dve.value_load(table[0:1, ROUNDS * NE + 2:ROUNDS * NE + 3], min_val=1, max_val=ROUNDS * 16 - 1)
                with dve.Fori(0, last) as i:
                    it = i + base
                    fetch(2 * i + 3, 1, (s("gu_mm1"), it + 1))
                    hidden_values(it + 1, 0)
                    fetch(2 * i + 4, 0, (s("gu_mm0"), it + 2))
                    hidden_values(it + 1, 1)
                    add_outputs(it)
                    hidden_features(it + 1)
                    row_weights(i + 1, it + 1)
                add_outputs(base + last)
                return base + last + 1

            turns = moe(0, 0)
            norm(2)
            for n in range(2):
                dve.wait_ge(s("ws_tr"), n + 1)
                copy(wsT[:, 4 * n:4 * n + 4, :], B[4 + n][:, :].rearrange("p (g t) -> p g t", g=4)) \
                    .then_inc(s("ws_out"), 1)
            dve.wait_ge(s("consts"), 1)
            copy(rep[0:4, :].rearrange("p (b s) -> p b s", s=SB), ident[0:4, 0:4].unsqueeze(1).to_broadcast([4, NB, SB])) \
                .then_inc(s("masks"), 1)
            for n in range(12):
                c, j = divmod(n, 3)
                t = TOK[j][1]
                dve.wait_ge(s("vtok_mm"), n + 1)
                copy(vtk[0:t, j, 512 * c:512 * c + 512], B[4 + n % 4][0:t, :]).then_inc(s("vtk"), 1)
                dve.wait_ge(s("vtk"), n + 1)
                link(dve.bn_stats(bnst[0:t, j, 6 * c:6 * c + 6], vtk[0:t, j, 512 * c:512 * c + 512]))
                if c == 3:
                    dve.bn_aggr(mvc[0:t, j, :], bnst[0:t, j, :]).then_inc(s("mv"), 1)
            dve.wait_ge(s("ln_landed"), 32)
            for j, (_, n) in enumerate(TOK):
                dve.wait_ge(s("hsd"), 1 + j + 1)
                link(dve.reciprocal(mvc[0:n, j, 1:2], mvc[0:n, j, 1:2]))
                link(ts(vtk[0:n, j, :], vtk[0:n, j, :], mvc[0:n, j, 0:1], mvc[0:n, j, 1:2], ALU.subtract, ALU.mult))
                link(tt(vtk[0:n, j, :], vtk[0:n, j, :], lnwb[0:n, 0, :], ALU.mult))
                tt(vtk[0:n, j, :], vtk[0:n, j, :], lnwb[0:n, 1, :], ALU.add).then_inc(s("v_norm"), 1)
            dve.wait_ge(s("ws_tr"), 3)
            tt(wsS[0:NS].rearrange("p g (b t) -> p g b t", t=SB),
               B[4][0:NS, 0:CG * SB].rearrange("p (g t) -> p g t", t=SB).unsqueeze(2).to_broadcast([NS, CG, NB, SB]),
               bmask[0:NS, 0:NB].unsqueeze(1).unsqueeze(3).to_broadcast([NS, CG, NB, SB]), ALU.mult) \
                .then_inc(s("masks"), 1)
            dve.wait_ge(s("bs_landed"), 16)
            for m in range(KI):
                g = m // 2
                dve.wait_ge(s("mix_mm"), m + 1)
                dve.wait_ge(s("gelu"), KI + m + 1)
                link(tt(mixt[:, 0:256].rearrange("p (j t) -> p j t", j=2), B[4 + m % 4][:, 0:256].rearrange("p (j t) -> p j t", j=2),
                        bsb[:, g, :].unsqueeze(1).to_broadcast([P, 2, P]), ALU.add))
                link(tt(mixt[:, 256:NT].rearrange(bs, s=SB), B[4 + m % 4][:, 256:NT].rearrange(bs, s=SB),
                        bsb[:, g, 0:SB].unsqueeze(1).to_broadcast([P, NB, SB]), ALU.add))
                ins = tt(uT[:, m, :], uT[:, m, :], mixt, ALU.mult)
                ins.then_inc(s("mixed"), 1)
                dve.wait_ge(s("mixed"), m + 1)
            for m in range(KD):
                dve.wait_ge(s("out_mm"), m + 1)
                stt(xT[:, m, :], B[m % 4][:, 0:NT], vec("cmlp_b_out", m), xT[:, m, :], ALU.add, ALU.add) \
                    .then_inc(s("out_add"), 1)
            moe(1, turns)
            norm(4)


def sample_view_all(xe, first=0):
    return xe[:, :, XS:XE].rearrange("p m (b x) -> p m b x", x=7)[:, :, :, first:first + 3]


_INS = ["x_prompt", "x_sample", "state_mlstm_C", "state_mlstm_n", "state_mlstm_m", "state_mlstm_conv",
        "norm_mix", "norm_ffn", "norm_final", "mlstm_w_up", "mlstm_conv_w", "mlstm_conv_b", "mlstm_w_q", "mlstm_w_k",
        "mlstm_w_v", "mlstm_w_ig", "mlstm_b_ig", "mlstm_w_fg", "mlstm_b_fg", "mlstm_skip", "mlstm_hn_w",
        "mlstm_w_down", "cmlp_w_in", "cmlp_b_in", "cmlp_ln_w", "cmlp_ln_b", "cmlp_w_s", "cmlp_b_s", "cmlp_w_out",
        "cmlp_b_out", "moe_w_rg", "moe_b_rg", "moe_w_re", "moe_b_re", "moe_w_gate", "moe_w_up", "moe_w_down"]
_OUTS = [("y_p", (1, NPROMPT, D)), ("y_s", (NB, SB, D)), ("C_p", (1, 1, H, DH, DH)), ("n_p", (1, 1, H, DH)),
         ("m_p", (1, 1, H)), ("conv_p", (1, 1, 3, INNER)), ("C_s", (1, NB, H, DH, DH)), ("n_s", (1, NB, H, DH)),
         ("m_s", (1, NB, H)), ("conv_s", (1, NB, 3, INNER)), ("v_s", (1, NB, SB, INNER))]


def kernel(**inputs):
    import numpy as _np
    import concourse.bacc as _bacc
    from concourse import mybir as _mybir
    from concourse.bass_utils import run_bass_kernel_spmd as _run

    nc = _bacc.Bacc("TRN2", target_bir_lowering=False, num_devices=1)
    arrays, ins, outs = {}, {}, {}
    for name in _INS:
        a = _np.ascontiguousarray(inputs[name])
        arrays[f"in_{name}"] = a
        ins[name] = nc.dram_tensor(f"in_{name}", a.shape, _mybir.dt.from_np(a.dtype), kind="ExternalInput").ap()
    for name, shape in _OUTS:
        outs[name] = nc.dram_tensor(f"out_{name}", shape, F32, kind="ExternalOutput").ap()
    build(nc, ins, outs)
    r = _run(nc, [arrays], core_ids=[0])
    return tuple(r.results[0][f"out_{name}"] for name, _ in _OUTS)
```
